# Optimizing a Trainium2 kernel written in Bass

```python
import math
import jax, jax.numpy as jnp
from jax import lax
import numpy as np

D_MODEL = 1024
BATCH = 1
SEQ = 512
DEPTH = 2

HEAD_DIM = 64
N_DIFF_HEADS = 4
DIFF_V_DIM = 2 * HEAD_DIM
DIFF_QK_WIDTH = N_DIFF_HEADS * 2 * HEAD_DIM
DIFF_WIDTH = N_DIFF_HEADS * DIFF_V_DIM
N_DIL_HEADS = 8
DIL_WIDTH = N_DIL_HEADS * HEAD_DIM
MIX_WIDTH = DIFF_WIDTH + DIL_WIDTH
IN_SPLITS = (DIFF_QK_WIDTH, 2 * DIFF_QK_WIDTH, 2 * DIFF_QK_WIDTH + DIFF_WIDTH,
             2 * DIFF_QK_WIDTH + DIFF_WIDTH + DIL_WIDTH,
             2 * DIFF_QK_WIDTH + DIFF_WIDTH + 2 * DIL_WIDTH)
IN_PROJ_WIDTH = 2 * DIFF_QK_WIDTH + DIFF_WIDTH + 3 * DIL_WIDTH
DILATED_PAIRS = ((128, 1), (512, 4), (2048, 16))
ROPE_THETA = 500000.0
ROPE_DIM = HEAD_DIM // 4
D_FF = 2816
CONV_WIDTH = 3
Q_BLOCK = 128
EPS = 1e-6
NEG_INF = -1e30
MAX_POS_OFFSET = 4096

kernel_name = "hymba_diff_dilated_convffn_adaln"

def rms_norm(x, g):
    xf = x.astype(jnp.float32)
    y = xf * lax.rsqrt(jnp.mean(xf * xf, axis=-1, keepdims=True) + EPS)
    return (y * g.astype(jnp.float32)).astype(x.dtype)

def rope_angles(positions):
    inv_freq = ROPE_THETA ** (-jnp.arange(0, ROPE_DIM, 2, dtype=jnp.float32) / ROPE_DIM)
    ang = positions.astype(jnp.float32)[..., None] * inv_freq
    return jnp.cos(ang), jnp.sin(ang)

def apply_partial_rope(x, cos, sin):
    bshape = cos.shape[:2] + (1,) * (x.ndim - 3) + cos.shape[-1:]
    cos = cos.reshape(bshape).astype(x.dtype)
    sin = sin.reshape(bshape).astype(x.dtype)
    half = ROPE_DIM // 2
    x1, x2 = x[..., :half], x[..., half:ROPE_DIM]
    return jnp.concatenate([x1 * cos - x2 * sin, x2 * cos + x1 * sin, x[..., ROPE_DIM:]], axis=-1)

def differential_attention(q, k, v, lam, lam_init, subln_g):
    B, S = q.shape[:2]
    qh = q.transpose(0, 2, 3, 1, 4)
    kh = k.transpose(0, 2, 3, 1, 4)
    vh = v.transpose(0, 2, 1, 3)
    scale = HEAD_DIM ** -0.5
    outs = []
    for n in range(S // Q_BLOCK):
        q0 = n * Q_BLOCK
        kv_len = q0 + Q_BLOCK
        s = jnp.einsum('bhiqe,bhike->bhiqk', qh[:, :, :, q0:kv_len],
                       kh[:, :, :, :kv_len]).astype(jnp.float32) * scale
        causal = (q0 + jnp.arange(Q_BLOCK))[:, None] >= jnp.arange(kv_len)[None, :]
        p = jax.nn.softmax(jnp.where(causal, s, NEG_INF), axis=-1)
        a = p[:, :, 0] - lam * p[:, :, 1]
        outs.append(jnp.einsum('bhqk,bhkv->bqhv', a.astype(v.dtype), vh[:, :, :kv_len]))
    o = jnp.concatenate(outs, axis=1)
    o = rms_norm(o, subln_g) * (1.0 - lam_init)
    return o.reshape(B, S, DIFF_WIDTH)

def dilated_branch(q, k, v, window, dilation):
    B, S, H, E = q.shape
    r = window // dilation
    L = S // dilation
    nb = -(-L // r)
    Lp = nb * r
    def sub(t):
        return t.reshape(B, L, dilation, H, E)
    qs = jnp.pad(sub(q), ((0, 0), (0, Lp - L), (0, 0), (0, 0), (0, 0))).reshape(B, nb, r, dilation, H, E)
    def ctx(t):
        tp = jnp.pad(sub(t), ((0, 0), (r, Lp - L), (0, 0), (0, 0), (0, 0))).reshape(B, nb + 1, r, dilation, H, E)
        return jnp.concatenate([tp[:, :-1], tp[:, 1:]], axis=2)
    kc, vc = ctx(k), ctx(v)
    s = jnp.einsum('bnqrhe,bnkrhe->bnrhqk', qs, kc).astype(jnp.float32) * (HEAD_DIM ** -0.5)
    qq = jnp.arange(r)[:, None]
    kk = jnp.arange(2 * r)[None, :]
    blk = jnp.arange(nb)[:, None, None]
    valid = (kk >= qq) & (kk <= qq + r) & ((blk - 1) * r + kk >= 0)
    s = jnp.where(valid[None, :, None, None], s, NEG_INF)
    lse = jax.nn.logsumexp(s, axis=-1)
    p = jnp.exp(s - lse[..., None])
    o = jnp.einsum('bnrhqk,bnkrhe->bnqrhe', p.astype(v.dtype), vc)
    o = o.reshape(B, Lp, dilation, H, E)[:, :L].reshape(B, S, H, E)
    lse = lse.transpose(0, 1, 4, 2, 3).reshape(B, Lp, dilation, H)[:, :L].reshape(B, S, H)
    return o, lse

def dilated_attention(q, k, v):
    outs, lses = [], []
    for window, dilation in DILATED_PAIRS:
        o, lse = dilated_branch(q, k, v, window, dilation)
        outs.append(o)
        lses.append(lse)
    w = jax.nn.softmax(jnp.stack(lses, axis=0), axis=0)
    o = jnp.sum(w[..., None] * jnp.stack(outs, axis=0).astype(jnp.float32), axis=0)
    return o.astype(q.dtype)

def hybrid_mixer(h, cos, sin, lam_init, w_in, w_out, diff_q_g, diff_k_g, lam_q1, lam_k1, lam_q2, lam_k2,
                 diff_subln_g, dil_q_g, dil_k_g, dil_out_g):
    B, S, _ = h.shape
    proj = h @ w_in
    dq, dk, dv, lq, lk, lv = jnp.split(proj, IN_SPLITS, axis=-1)
    dq = apply_partial_rope(rms_norm(dq.reshape(B, S, N_DIFF_HEADS, 2, HEAD_DIM), diff_q_g), cos, sin)
    dk = apply_partial_rope(rms_norm(dk.reshape(B, S, N_DIFF_HEADS, 2, HEAD_DIM), diff_k_g), cos, sin)
    dv = dv.reshape(B, S, N_DIFF_HEADS, DIFF_V_DIM)
    lam = (jnp.exp(jnp.sum(lam_q1.astype(jnp.float32) * lam_k1.astype(jnp.float32)))
           - jnp.exp(jnp.sum(lam_q2.astype(jnp.float32) * lam_k2.astype(jnp.float32))) + lam_init)
    out_a = differential_attention(dq, dk, dv, lam, lam_init, diff_subln_g)
    lq = apply_partial_rope(rms_norm(lq.reshape(B, S, N_DIL_HEADS, HEAD_DIM), dil_q_g), cos, sin)
    lk = apply_partial_rope(rms_norm(lk.reshape(B, S, N_DIL_HEADS, HEAD_DIM), dil_k_g), cos, sin)
    lv = lv.reshape(B, S, N_DIL_HEADS, HEAD_DIM)
    out_b = rms_norm(dilated_attention(lq, lk, lv), dil_out_g).reshape(B, S, DIL_WIDTH)
    return jnp.concatenate([out_a, out_b], axis=-1) @ w_out

def conv_ffn(h, w_up, conv_w, conv_b, w_down):
    u = h @ w_up
    u = lax.conv_general_dilated(u, conv_w[:, None, :], window_strides=(1,),
                                 padding=[(CONV_WIDTH - 1, 0)],
                                 dimension_numbers=('NWC', 'WIO', 'NWC'),
                                 feature_group_count=2 * D_FF) + conv_b
    g, val = jnp.split(u, 2, axis=-1)
    return (jax.nn.silu(g) * val) @ w_down

def setup_inputs(seed: int = 0) -> dict:
    key = jax.random.key(seed)
    ks = jax.random.split(key, 24)
    f32 = jnp.float32
    def nrm(k, shape, scale):
        return jax.random.normal(k, shape, f32) * scale
    def gain(k, shape):
        return 1.0 + 0.02 * jax.random.normal(k, shape, f32)
    start = jax.random.randint(ks[2], (BATCH, 1), 0, MAX_POS_OFFSET, dtype=jnp.int32)
    positions = start + jnp.arange(SEQ, dtype=jnp.int32)[None, :]
    return {
        "x": nrm(ks[0], (BATCH, SEQ, D_MODEL), 1.0),
        "c": nrm(ks[1], (BATCH, D_MODEL), 1.0),
        "positions": positions,
        "g_mix": gain(ks[3], (DEPTH, D_MODEL)),
        "g_ffn": gain(ks[4], (DEPTH, D_MODEL)),
        "w_ada": nrm(ks[5], (DEPTH, D_MODEL, 6 * D_MODEL), 0.5 * D_MODEL ** -0.5),
        "b_ada": nrm(ks[6], (DEPTH, 6 * D_MODEL), 0.01),
        "w_in": nrm(ks[7], (DEPTH, D_MODEL, IN_PROJ_WIDTH), D_MODEL ** -0.5),
        "w_out": nrm(ks[8], (DEPTH, MIX_WIDTH, D_MODEL), MIX_WIDTH ** -0.5),
        "diff_q_g": gain(ks[9], (DEPTH, HEAD_DIM)),
        "diff_k_g": gain(ks[10], (DEPTH, HEAD_DIM)),
        "lam_q1": nrm(ks[11], (DEPTH, HEAD_DIM), 0.1),
        "lam_k1": nrm(ks[12], (DEPTH, HEAD_DIM), 0.1),
        "lam_q2": nrm(ks[13], (DEPTH, HEAD_DIM), 0.1),
        "lam_k2": nrm(ks[14], (DEPTH, HEAD_DIM), 0.1),
        "diff_subln_g": gain(ks[15], (DEPTH, DIFF_V_DIM)),
        "dil_q_g": gain(ks[16], (DEPTH, HEAD_DIM)),
        "dil_k_g": gain(ks[17], (DEPTH, HEAD_DIM)),
        "dil_out_g": gain(ks[18], (DEPTH, HEAD_DIM)),
        "w_up": nrm(ks[19], (DEPTH, D_MODEL, 2 * D_FF), D_MODEL ** -0.5),
        "conv_w": nrm(ks[20], (DEPTH, CONV_WIDTH, 2 * D_FF), CONV_WIDTH ** -0.5),
        "conv_b": nrm(ks[21], (DEPTH, 2 * D_FF), 0.01),
        "w_down": nrm(ks[22], (DEPTH, D_FF, D_MODEL), D_FF ** -0.5),
    }

def reference(x, c, positions, g_mix, g_ffn, w_ada, b_ada, w_in, w_out, diff_q_g, diff_k_g,
              lam_q1, lam_k1, lam_q2, lam_k2, diff_subln_g, dil_q_g, dil_k_g, dil_out_g,
              w_up, conv_w, conv_b, w_down):
    cos, sin = rope_angles(positions)
    cond = jax.nn.silu(c)
    for l in range(DEPTH):
        lam_init = 0.8 - 0.6 * math.exp(-0.3 * l)
        mod = (cond @ w_ada[l] + b_ada[l])[:, None, :]
        sh_a, sc_a, gt_a, sh_f, sc_f, gt_f = jnp.split(mod, 6, axis=-1)
        h = rms_norm(x, g_mix[l]) * (1.0 + sc_a) + sh_a
        x = x + gt_a * hybrid_mixer(h, cos, sin, lam_init, w_in[l], w_out[l], diff_q_g[l], diff_k_g[l],
                                    lam_q1[l], lam_k1[l], lam_q2[l], lam_k2[l], diff_subln_g[l],
                                    dil_q_g[l], dil_k_g[l], dil_out_g[l])
        h = rms_norm(x, g_ffn[l]) * (1.0 + sc_f) + sh_f
        x = x + gt_f * conv_ffn(h, w_up[l], conv_w[l], conv_b[l], w_down[l])
    return x


_drawn_inputs = setup_inputs


def setup_inputs(seed=0):
    import zlib

    import numpy as np

    out = dict(_drawn_inputs(seed))
    spreads = {}
    factors = {'g_mix': 8.0,
     'g_ffn': 7.172,
     'b_ada': 2.892,
     'diff_q_g': 8.0,
     'diff_k_g': 8.0,
     'lam_q1': 8.0,
     'lam_k1': 7.78,
     'lam_q2': 8.0,
     'lam_k2': 8.0,
     'diff_subln_g': 8.0,
     'dil_q_g': 8.0,
     'dil_k_g': 8.0,
     'dil_out_g': 8.0,
     'conv_b': 8.0}
    for name, (base, spread) in spreads.items():
        noise = np.random.default_rng([zlib.crc32(name.encode()), seed]).standard_normal(out[name].shape)
        drawn = base * np.exp(spread * noise) if base else spread * noise
        out[name] = __import__('jax').numpy.asarray(drawn.astype(out[name].dtype))
    for name, factor in factors.items():
        out[name] = (out[name] * factor).astype(out[name].dtype)
    return out
```

```python
import math
from contextlib import ExitStack

import numpy as np

import concourse.bass as bass
from concourse import mybir

F32 = mybir.dt.float32
F32R = mybir.dt.float32r
I32 = mybir.dt.int32
ALU = mybir.AluOpType
ACT = mybir.ActivationFunctionType
AX = mybir.AxisListType

P = 128
LAYERS = 2
D = 1024
S = 512
HEAD = 64
D_FF = 2816
ROPE = HEAD // 4
ROPE_HALF = ROPE // 2
THETA = 500000.0
EPS = 1e-6
BIG = 1e30

KD = D // P
TT = S // P
GROUPS = 6
GW = 512
GH = GW // HEAD
FT = D_FF // P
FFN_SETS = (12, 10)
ACT_SLOTS = max(FFN_SETS)
TASKS = 8
DIFF_TASKS = 4
STEPS = TASKS * TT
ROWS = 2 * STEPS
T_DIFF = DIFF_TASKS * TT
T_ALL = T_DIFF + 2 * (TASKS - DIFF_TASKS) * TT
SLOT = 2048

P_IN = 0
P_OUT = P_IN + GROUPS
OUT_PAIRS = 2
P_UP, P_DOWN = [], []
_p = P_OUT + OUT_PAIRS
for _n in FFN_SETS:
    P_UP.append(_p)
    P_DOWN.append(_p + _n // 2)
    _p += _n
PAIRS = _p

USED0_LAYER = GROUPS + OUT_PAIRS + FT // 2
USED1_LAYER = (OUT_PAIRS - 1) + sum(n // 2 - 1 for n in FFN_SETS)
USED0_OUT = GROUPS
USED1_OUT = 0
USED0_DOWN = [GROUPS + OUT_PAIRS, GROUPS + OUT_PAIRS + FFN_SETS[0] // 2]
USED1_DOWN = [OUT_PAIRS - 1, OUT_PAIRS - 1 + FFN_SETS[0] // 2 - 1]

UP_LAYER = 2 * FT
UP_BASE = [0, 2 * FFN_SETS[0]]
FF_BASE = [0, FFN_SETS[0]]
X_LAYER = 3 * KD
X_INIT = KD

ADA_ADDS = 2 * (KD - 1)

C_W0, C_W1, C_W2, C_B = (i * 2 * FT for i in range(4))
C_ADA = 8 * FT
C_GMIX = C_ADA + 6 * KD
C_GFFN = C_GMIX + KD
C_COND = C_GFFN + KD
PARAMS = C_COND + KD
SH_A, SC_A, GT_A, SH_F, SC_F, GT_F = range(6)
G_DQ, G_DK, G_LQ, G_LK, G_SUB, G_OUT = range(6)


def lam_init(layer):
    return 0.8 - 0.6 * math.exp(-0.3 * layer)


def split_two_pi(scale):
    rest, parts = 2 * math.pi * scale, []
    for _ in range(3):
        ulp = 2.0 ** (math.floor(math.log2(rest)) - 7)
        part = math.floor(rest / ulp) * ulp
        parts.append(part)
        rest -= part
    return parts + [float(np.float32(rest))]


def trunk_kernel(nc, x, c, positions, g_mix, g_ffn, w_ada, b_ada, w_in, w_out, diff_q_g, diff_k_g,
                 lam_q1, lam_k1, lam_q2, lam_k2, diff_subln_g, dil_q_g, dil_k_g, dil_out_g,
                 w_up, conv_w, conv_b, w_down, out):
    ctx = ExitStack()
    with ctx:
        def sb(name, shape, dt=F32):
            return ctx.enter_context(nc.sbuf_tensor(name, shape, dt))

        def sem(name):
            return ctx.enter_context(nc.semaphore(name))

        xT = sb("xT", [P, KD, S])
        h_hi = sb("h_hi", [P, KD, S], F32R)
        h_lo = sb("h_lo", [P, KD, S], F32R)
        w_raw = [sb(f"w_raw{s}", [P, SLOT]) for s in range(2)]
        w_hi = [sb(f"w_hi{s}", [P, SLOT], F32R) for s in range(2)]
        w_lo = [sb(f"w_lo{s}", [P, SLOT], F32R) for s in range(2)]
        ada_raw = [sb(f"ada_raw{i}", [P, D]) for i in range(4)]
        ada_acc = [sb(f"ada_acc{i}", [P, D]) for i in range(2)]
        work = [sb(f"work{i}", [P, S]) for i in range(8)]
        maskA = sb("maskA", [P, S])
        maskB = sb("maskB", [P, S])
        ident = sb("ident", [P, P])
        mean_w = sb("mean_w", [P, P])
        ones = sb("ones", [P, 1])
        par = sb("par", [P, LAYERS, PARAMS])
        gcol = sb("gcol", [P, 6 * LAYERS])
        mod = sb("mod", [P, 6 * KD])
        cond = sb("cond", [P, KD])
        afac = sb("afac", [P, KD])
        neglam = sb("neglam", [P, LAYERS])
        ropeC = sb("ropeC", [P, 4 * LAYERS, TT, ROPE])
        ropeS = sb("ropeS", [P, 4 * LAYERS, TT, ROPE])
        small = sb("small", [P, 6, GH])
        mneg = sb("mneg", [P, ROWS])
        lsum = sb("lsum", [P, ROWS])
        comb = sb("comb", [P, 2, 2])
        with ExitStack() as inner:
            qkT = inner.enter_context(nc.sbuf_tensor("qkT", [P, 16, S], F32))
            vnat = inner.enter_context(nc.sbuf_tensor("vnat", [P, TT, 2 * GW], F32))
        with ExitStack() as inner:
            act_hi = inner.enter_context(nc.sbuf_tensor("act_hi", [P, ACT_SLOTS, S], F32R))
            act_lo = inner.enter_context(nc.sbuf_tensor("act_lo", [P, ACT_SLOTS, S], F32R))
        with ExitStack() as inner:
            xnat = inner.enter_context(nc.sbuf_tensor("xnat", [P, TT, D], F32))
            prow = inner.enter_context(nc.sbuf_tensor("prow", [P, 3 * LAYERS + 1, P], F32))
            lamv = inner.enter_context(nc.sbuf_tensor("lamv", [P, 4, LAYERS, HEAD], F32))
            gnat = inner.enter_context(nc.sbuf_tensor("gnat", [P, 4 * LAYERS, ROPE], F32))
            gswap = inner.enter_context(nc.sbuf_tensor("gswap", [P, 4 * LAYERS, ROPE], F32))
            pos_i = inner.enter_context(nc.sbuf_tensor("pos_i", [P, TT], I32))
            pos_f = inner.enter_context(nc.sbuf_tensor("pos_f", [P, TT], F32))
            ang = inner.enter_context(nc.sbuf_tensor("ang", [P, TT, ROPE_HALF], F32))
            turns = inner.enter_context(nc.sbuf_tensor("turns", [P, TT, ROPE_HALF], F32))
            trig_in = inner.enter_context(nc.sbuf_tensor("trig_in", [P, 2, TT, ROPE_HALF], F32))
            trig = inner.enter_context(nc.sbuf_tensor("trig", [P, 2, TT, ROPE_HALF], F32))
            cos16 = inner.enter_context(nc.sbuf_tensor("cos16", [P, TT, ROPE], F32))
            sin16 = inner.enter_context(nc.sbuf_tensor("sin16", [P, TT, ROPE], F32))
            delta = inner.enter_context(nc.sbuf_tensor("delta", [P, S], I32))
            rem = inner.enter_context(nc.sbuf_tensor("rem", [P, 2, S], I32))
            cnt = inner.enter_context(nc.sbuf_tensor("cnt", [P, 5, S], F32))
            lam_s = inner.enter_context(nc.sbuf_tensor("lam_s", [P, 3, 4], F32))

        bank = [ctx.enter_context(nc.psum_tensor(f"bank{i}", [P, 512], F32)) for i in range(8)]

        params_loaded = sem("params_loaded")
        x_loaded = sem("x_loaded")
        rows_set = sem("rows_set")
        ident_ready = sem("ident_ready")
        pool_mask = sem("pool_mask")
        setup_dve = sem("setup_dve")
        setup_act = sem("setup_act")
        setup_pe = sem("setup_pe")
        cond_ready = sem("cond_ready")
        raw_loaded = [sem(f"raw_loaded{s}") for s in range(2)]
        hi_ready = [sem(f"hi_ready{s}") for s in range(2)]
        lo_ready = [sem(f"lo_ready{s}") for s in range(2)]
        weights_used = [sem(f"weights_used{s}") for s in range(2)]
        ada_loaded = [sem(f"ada_loaded{i}") for i in range(4)]
        ada_scaled = sem("ada_scaled")
        ada_step = sem("ada_step")
        ada_summed = sem("ada_summed")
        mod_ready = sem("mod_ready")
        x_done = sem("x_done")
        sq_done = sem("sq_done")
        mean_done = sem("mean_done")
        norm_dve = sem("norm_dve")
        norm_act = sem("norm_act")
        afac_done = sem("afac_done")
        h_pre = sem("h_pre")
        h_hi_done = sem("h_hi_done")
        h_lo_done = sem("h_lo_done")
        proj_done = sem("proj_done")
        nat_act = sem("nat_act")
        nat_dve = sem("nat_dve")
        rope_dve = sem("rope_dve")
        nat_mul = sem("nat_mul")
        nat_ready = sem("nat_ready")
        nat_turned = sem("nat_turned")
        qk_ready = sem("qk_ready")
        v_ready = sem("v_ready")
        scores_mm = sem("scores_mm")
        score_done = sem("score_done")
        exp_done = sem("exp_done")
        comb_done = sem("comb_done")
        p_turned = sem("p_turned")
        pT_ready = sem("pT_ready")
        pv_done = sem("pv_done")
        fin_dve = sem("fin_dve")
        fin_act = sem("fin_act")
        o_turned = sem("o_turned")
        o_hi_done = sem("o_hi_done")
        o_lo_done = sem("o_lo_done")
        acc_done = sem("acc_done")
        up_done = sem("up_done")
        tap2_done = sem("tap2_done")
        tap1_done = sem("tap1_done")
        conv_done = sem("conv_done")
        silu_done = sem("silu_done")
        prod_done = sem("prod_done")
        act_hi_done = sem("act_hi_done")
        act_lo_done = sem("act_lo_done")
        out_turned = sem("out_turned")
        out_copied_dve = sem("out_copied_dve")
        out_copied_act = sem("out_copied_act")
        out_stored = sem("out_stored")

        def is_diff(task):
            return task < DIFF_TASKS

        def turn_units(task, n):
            if is_diff(task):
                return [(task * TT + n, 0)]
            base = T_DIFF + (task - DIFF_TASKS) * 2 * TT + 2 * n
            return [(base, 0), (base + 1, 1)]

        def row_of(task, n, e):
            return task * 8 + 2 * n + e

        QK_GROUPS = [0, 1, 3, 4]

        def qk_index(g):
            return QK_GROUPS.index(g)

        def slot_free(eng, L, p, s):
            if p == 0:
                eng.wait_ge(weights_used[0], L * USED0_LAYER)
                if s == 1:
                    eng.wait_ge(acc_done, L * X_LAYER)
                return
            q = p - 1
            if q < P_OUT:
                if s == 0:
                    eng.wait_ge(weights_used[0], L * USED0_LAYER + q + 1)
                else:
                    eng.wait_ge(proj_done, (L * GROUPS + q + 1) * TT)
                return
            if q < P_OUT + OUT_PAIRS:
                if s == 0:
                    eng.wait_ge(weights_used[0], L * USED0_LAYER + USED0_OUT + q - P_OUT + 1)
                elif q == P_OUT + OUT_PAIRS - 1:
                    eng.wait_ge(acc_done, L * X_LAYER + KD)
                else:
                    eng.wait_ge(weights_used[1], L * USED1_LAYER + USED1_OUT + q - P_OUT + 1)
                return
            raise AssertionError("pairs of the feed-forward loops have waits of their own")

        def split_hi(L, p, s, width=SLOT):
            nc.scalar.wait_ge(raw_loaded[s], (L * PAIRS + p + 1) * 16)
            nc.scalar.activation(w_hi[s][:, 0:width], w_raw[s][:, 0:width], ACT.Copy)\
                .then_inc(hi_ready[s], 1)

        def split_lo(L, p, s, width=SLOT):
            nc.vector.wait_ge(hi_ready[s], L * PAIRS + p + 1)
            nc.vector.tensor_tensor(w_lo[s][:, 0:width], w_raw[s][:, 0:width],
                                    w_hi[s][:, 0:width], ALU.subtract).then_inc(lo_ready[s], 1)

        block = ctx.enter_context(nc.Block())

        @block.sync
        def _(sp):
            for t in range(TT):
                sp.dma_start(xnat[:, t, :], x[0, t * P:(t + 1) * P, :]).then_inc(x_loaded, 16)
            n = 0
            for l in range(LAYERS):
                rows = [(0, 0, conv_w[l, 0], 2 * FT), (0, 2 * FT, conv_w[l, 1], 2 * FT),
                        (1, 0, conv_w[l, 2], 2 * FT), (1, 2 * FT, conv_b[l], 2 * FT),
                        (2, 0, b_ada[l], 6 * KD), (2, 6 * KD, g_mix[l], KD),
                        (2, 7 * KD, g_ffn[l], KD), (2, 8 * KD, c[0], KD)]
                for blk, r0, src, k in rows:
                    sp.dma_start(prow[r0:r0 + k, 3 * l + blk, :],
                                 src.rearrange("(r q) -> r q", q=P)).then_inc(params_loaded, 16)
                    n += 1
            sp.wait_ge(rows_set, 1)
            G = 3 * LAYERS
            for k, g in enumerate((diff_q_g, diff_k_g, dil_q_g, dil_k_g)):
                for half in range(2):
                    sp.dma_start(prow[2 * k:2 * k + 2, G, half * HEAD + ROPE:(half + 1) * HEAD],
                                 g[:, ROPE:HEAD]).then_inc(params_loaded, 16)
                    n += 1
                sp.dma_start(gnat[:, 2 * k:2 * k + 2, :],
                             g[:, 0:ROPE].partition_broadcast(P)).then_inc(params_loaded, 16)
                n += 1
            sp.dma_start(prow[2 * G_SUB:2 * G_SUB + 2, G, :], diff_subln_g).then_inc(params_loaded, 16)
            for half in range(2):
                sp.dma_start(prow[2 * G_OUT:2 * G_OUT + 2, G, half * HEAD:(half + 1) * HEAD],
                             dil_out_g).then_inc(params_loaded, 16)
            for i, v in enumerate((lam_q1, lam_k1, lam_q2, lam_k2)):
                sp.dma_start(lamv[:, i, :, :], v.partition_broadcast(P)).then_inc(params_loaded, 16)
            with nc.allow_non_contiguous_dma(reason="512 positions, one a partition and tile"):
                sp.dma_start(pos_i[:, :], positions[0].rearrange("(t p) -> p t", p=P))\
                    .then_inc(params_loaded, 16)
            assert n + 8 == N_PARAM_LOADS

            def load(L, p, s, dst, src):
                sp.wait_ge(lo_ready[s], L * PAIRS + p)
                sp.dma_start(dst, src).then_inc(raw_loaded[s], 16)

            with sp.Fori(0, LAYERS) as L:
                for g in range(GROUPS):
                    for s in range(2):
                        load(L, P_IN + g, s, w_raw[s][:, :].rearrange("p (k n) -> p k n", n=GW),
                             w_in[L, s * 512:(s + 1) * 512, g * GW:(g + 1) * GW]
                             .rearrange("(k p) n -> p k n", p=P))
                for q in range(OUT_PAIRS):
                    for s in range(2):
                        r0 = (2 * q + s) * 2 * P
                        load(L, P_OUT + q, s, w_raw[s][:, :].rearrange("p (k n) -> p k n", n=D),
                             w_out[L, r0:r0 + 2 * P, :].rearrange("(k p) n -> p k n", p=P))
                for half, tiles in enumerate(FFN_SETS):
                    with sp.Fori(0, tiles // 2) as i:
                        for s in range(2):
                            col = i * (2 * P) + (s * D_FF + FF_BASE[half] * P)
                            load(L, P_UP[half] + i, s,
                                 w_raw[s][:, :].rearrange("p (k n) -> p k n", n=2 * P),
                                 w_up[L, :, bass.ds(col, 2 * P)].rearrange("(k p) n -> p k n", p=P))
                    with sp.Fori(0, tiles // 2) as i:
                        for s in range(2):
                            row = i * (2 * P) + (s * P + FF_BASE[half] * P)
                            load(L, P_DOWN[half] + i, s, w_raw[s][:, 0:D],
                                 w_down[L, bass.ds(row, P), :])
            for t in range(TT):
                sp.wait_ge(out_copied_dve, t + 1)
                sp.wait_ge(out_copied_act, t + 1)
                sp.dma_start(out[0, t * P:(t + 1) * P, :], xnat[:, t, :]).then_inc(out_stored, 16)
            sp.wait_ge(out_stored, 16 * TT)

        @block.gpsimd
        def _(pool):
            pool.memset(ident[:, :], 0.0).then_inc(pool_mask, 1)
            pool.memset(maskA[:, :], 0.0).then_inc(pool_mask, 1)
            pool.memset(cnt[:, 0, :], 1.0).then_inc(pool_mask, 1)
            pool.iota(delta[:, :], pattern=[[-1, S]], base=S - P, channel_multiplier=1)\
                .then_inc(pool_mask, 1)
            pool.wait_ge(pool_mask, 4)
            pool.affine_select(out=ident[:, :], in_=ident[:, :], compare_op=ALU.not_equal, fill=1.0,
                               base=0, pattern=[[-1, P]], channel_multiplier=1).then_inc(ident_ready, 1)
            diag = maskA[:, S - P:S]
            pool.affine_select(out=diag, in_=diag, compare_op=ALU.is_ge, fill=BIG,
                               base=0, pattern=[[-1, P]], channel_multiplier=1).then_inc(pool_mask, 1)
            pool.affine_select(out=cnt[:, 0, :], in_=cnt[:, 0, :], compare_op=ALU.is_ge, fill=0.0,
                               base=S - P, pattern=[[-1, S]], channel_multiplier=1)\
                .then_inc(pool_mask, 1)
            pool.wait_ge(pool_mask, 6)
            pool.affine_select(out=cnt[:, 0, :], in_=cnt[:, 0, :], compare_op=ALU.is_ge, fill=0.0,
                               base=P - (S - P), pattern=[[1, S]], channel_multiplier=-1)\
                .then_inc(pool_mask, 1)
            pool.wait_ge(setup_dve, SD_STRIDED)
            pool.affine_select(out=cnt[:, 1, :], in_=cnt[:, 1, :], compare_op=ALU.is_ge, fill=0.0,
                               base=S - P, pattern=[[-1, S]], channel_multiplier=1)\
                .then_inc(pool_mask, 1)

            pool.wait_ge(cond_ready, 1)
            with pool.Fori(0, LAYERS) as L:
                with pool.Fori(0, 3) as i:
                    for b in range(2):
                        def load(k):
                            row = k * P
                            pool.dma_start(ada_raw[k % 4][:, :],
                                           w_ada[L, row:row + P, bass.ds(i * (2 * D) + b * D, D)])\
                                .then_inc(ada_loaded[k % 4], 16)
                        first = (L * 3 + i) * (2 * KD) + b * KD
                        slot_turns = (L * 3 + i) * 4 + 2 * b
                        adds = (L * 3 + i) * ADA_ADDS + b * (KD - 1)
                        pool.wait_ge(ada_step, adds)
                        for k in range(4):
                            load(k)
                        pool.wait_ge(ada_summed, L * 3 + i)
                        for k in range(KD):
                            pool.wait_ge(ada_loaded[k % 4], (slot_turns + k // 4 + 1) * 16)
                            pool.nop(nofuse=True)
                            pool.tensor_scalar(ada_acc[b][:, :] if k == 0 else ada_raw[k % 4][:, :],
                                               ada_raw[k % 4][:, :], cond[:, k:k + 1], None,
                                               ALU.mult).then_inc(ada_scaled, 1)
                            pool.wait_ge(ada_scaled, first + k + 1)
                            if k:
                                pool.tensor_tensor(ada_acc[b][:, :], ada_acc[b][:, :],
                                                   ada_raw[k % 4][:, :], ALU.add)\
                                    .then_inc(ada_step, 1)
                            if k + 4 < KD:
                                pool.wait_ge(ada_step, adds + k)
                                load(k + 4)

        @block.scalar
        def _(act):
            A = nc.scalar

            A.preload_act_table(ACT.Silu)
            act.wait_ge(setup_dve, SD_PAR0)
            A.activation(cond[:, :], par[:, 0, C_COND:C_COND + KD], ACT.Silu).then_inc(cond_ready, 1)
            act.wait_ge(setup_dve, SD_TRIG)
            A.activation(trig[:, :, :, :], trig_in[:, :, :, :], ACT.Sin).then_inc(setup_act, 1)
            A.preload_act_table_set("natural_log_exp_and_others")
            act.wait_ge(setup_dve, SD_LAM)
            A.activation(lam_s[:, 1, :], lam_s[:, 0, :], ACT.Exp).then_inc(setup_act, 1)

            def norm(L, which):
                N = L * 2 + which
                base = X_INIT + L * X_LAYER + which * KD - KD
                for m in range(KD):
                    act.wait_ge(x_done, base + m + 1)
                    if m >= 2:
                        act.wait_ge(mean_done, N * KD + m - 1)
                    A.activation(work[m % 2][:, :], xT[:, m, :], ACT.Square).then_inc(sq_done, 1)
                act.wait_ge(norm_dve, N * 3 + 1)
                A.activation(work[3][:, :], work[2][:, :], ACT.Ln).then_inc(norm_act, 1)
                act.wait_ge(norm_act, N * 3 + 1)
                A.activation(work[4][:, :], work[3][:, :], ACT.Exp, scale=-0.5).then_inc(norm_act, 1)
                act.wait_ge(norm_act, N * 3 + 2)
                A.activation(work[5][:, :], work[4][:, :], ACT.Square).then_inc(norm_act, 1)
                shift = (SH_A, SH_F)[which] * KD
                for m in range(KD):
                    act.wait_ge(h_pre, N * KD + m + 1)
                    A.activation(h_hi[:, m, :], work[6 + m % 2][:, :], ACT.Identity,
                                 bias=mod[:, shift + m:shift + m + 1]).then_inc(h_hi_done, 1)

            def nat_stats(L, g, t):
                Q = (L * 4 + qk_index(g)) * TT + t
                act.wait_ge(proj_done, (L * GROUPS + g) * TT + t + 1)
                act.wait_ge(nat_dve, Q * 5)
                A.activation(work[7][:, :], bank[t][:, :], ACT.Square).then_inc(nat_act, 1)
                act.wait_ge(nat_dve, Q * 5 + 2)
                A.activation(small[:, 1, :], small[:, 0, :], ACT.Ln).then_inc(nat_act, 1)
                act.wait_ge(nat_act, Q * 3 + 2)
                A.activation(small[:, 2, :], small[:, 1, :], ACT.Exp, scale=-0.5).then_inc(nat_act, 1)

            def qk_evacuate(L, g, t):
                k = qk_index(g)
                act.wait_ge(nat_turned, (L * 4 + k) * TT + t + 1)
                act.nop(nofuse=True)
                A.activation(qkT[:, 4 * k:4 * k + 4, t * P:(t + 1) * P],
                             bank[4 + t % 2][:, :].rearrange("p (b n) -> p b n", n=P), ACT.Copy,
                             scale=gcol[:, bass.ds(L + LAYERS * k, 1)]).then_inc(qk_ready, 1)

            def v_copy(L, g, t):
                act.wait_ge(proj_done, (L * GROUPS + g) * TT + t + 1)
                A.activation(vnat[:, t, (g // 3) * GW:(g // 3 + 1) * GW], bank[t][:, :], ACT.Copy)\
                    .then_inc(v_ready, 1)

            def exps(L, task, n):
                W = (n + 1) * P
                for e in range(2):
                    r = row_of(task, n, e)
                    buf = work[(n % 2) * 2 + e][:, 0:W]
                    act.wait_ge(score_done, L * ROWS + r + 1)
                    A.activation(buf, buf, ACT.Exp, bias=mneg[:, r:r + 1], scale=-1.0,
                                 accum_out=lsum[:, r:r + 1]).then_inc(exp_done, 1)

            def pT_copy(L, task, n):
                W = (n + 1) * P
                for i, _ in turn_units(task, n):
                    act.wait_ge(p_turned, L * T_ALL + i + 1)
                    if i >= 2:
                        act.wait_ge(pv_done, L * T_ALL + i - 1)
                    A.activation(work[4 + i % 2][:, 0:W], bank[4 + i % 2][:, 0:W], ACT.Copy)\
                        .then_inc(pT_ready, 1)

            def finish(L, task, stage):
                F = L * TASKS + task
                if stage == 1:
                    act.wait_ge(fin_dve, F * 8 + 2)
                    A.activation(work[7][:, :], work[6][:, :], ACT.Square).then_inc(fin_act, 1)
                if stage == 2:
                    act.wait_ge(fin_dve, F * 8 + 4)
                    A.activation(small[:, 1, :], small[:, 0, :], ACT.Ln).then_inc(fin_act, 1)
                    act.wait_ge(fin_act, F * 3 + 2)
                    A.activation(small[:, 2, :], small[:, 1, :], ACT.Exp, scale=-0.5)\
                        .then_inc(fin_act, 1)
                if stage == 3:
                    act.wait_ge(o_turned, F + 1)
                    kind = G_SUB if is_diff(task) else G_OUT
                    act.nop(nofuse=True)
                    A.activation(h_hi[:, task, :], bank[6 + task % 2][:, :], ACT.Copy,
                                 scale=gcol[:, bass.ds(L + LAYERS * kind, 1)]).then_inc(o_hi_done, 1)

            with act.Fori(0, LAYERS) as L:
                A.preload_act_table_set("natural_log_exp_and_others")
                slot_free(act, L, 0, 0)
                split_hi(L, 0, 0)
                norm(L, 0)
                for g in range(GROUPS):
                    slot_free(act, L, g, 1)
                    split_hi(L, g, 1)
                    for t in range(TT):
                        if g - 1 in QK_GROUPS:
                            qk_evacuate(L, g - 1, t)
                    slot_free(act, L, g + 1, 0)
                    split_hi(L, g + 1, 0)
                    for t in range(TT):
                        if g in QK_GROUPS:
                            nat_stats(L, g, t)
                        else:
                            v_copy(L, g, t)
                slot_free(act, L, P_OUT, 1)
                split_hi(L, P_OUT, 1)

                steps = [(task, n) for task in range(TASKS) for n in range(TT)]
                exps(L, 0, 0)
                for k, (task, n) in enumerate(steps):
                    if k + 1 < STEPS:
                        exps(L, *steps[k + 1])
                    pT_copy(L, task, n)
                    if task >= 1 and n >= 1:
                        finish(L, task - 1, n)
                for stage in (1, 2, 3):
                    finish(L, TASKS - 1, stage)

                for q in range(OUT_PAIRS):
                    if q:
                        slot_free(act, L, P_OUT + q, 1)
                        split_hi(L, P_OUT + q, 1)
                    slot_free(act, L, P_OUT + q + 1, 0)
                    split_hi(L, P_OUT + q + 1, 0)
                norm(L, 1)
                A.preload_act_table(ACT.Silu)

                for half, tiles in enumerate(FFN_SETS):
                    pairs = tiles // 2
                    with act.Fori(0, pairs) as i:
                        X = L * UP_LAYER + (i * 4 + UP_BASE[half])
                        Y = L * FT + (i * 2 + FF_BASE[half])
                        act.wait_ge(up_done, X)
                        act.wait_ge(acc_done, L * X_LAYER + (half + 1) * KD)
                        split_hi(L, i + P_UP[half], 1)
                        for part in range(2):
                            for q in range(2):
                                b = 2 * part + q
                                col = i * 2 + (part * FT + FF_BASE[half] + q)
                                act.wait_ge(up_done, X + b + 1)
                                act.wait_ge(prod_done, Y)
                                act.wait_ge(act_lo_done, Y)
                                act.nop(nofuse=True)
                                A.activation(work[b][:, :], bank[b][:, :], ACT.Identity,
                                             scale=par[:, L, bass.ds(col + C_W2, 1)],
                                             bias=par[:, L, bass.ds(col + C_B, 1)])\
                                    .then_inc(tap2_done, 1)
                            if part == 0:
                                for q in range(2):
                                    act.wait_ge(conv_done, X + 4 + q + 1)
                                    A.activation(work[4 + q][:, :], work[q][:, :], ACT.Silu)\
                                        .then_inc(silu_done, 1)
                                act.wait_ge(up_done, X + 2)
                                split_hi(L, i + (P_UP[half] + 1), 0)
                        for q in range(2):
                            act.wait_ge(prod_done, Y + q + 1)
                            act.nop(nofuse=True)
                            A.activation(act_hi[:, bass.ds(i * 2 + q, 1), :],
                                         work[2 + q][:, :].unsqueeze(1), ACT.Copy)\
                                .then_inc(act_hi_done, 1)
                    act.wait_ge(up_done, L * UP_LAYER + UP_BASE[half] + 2 * tiles)
                    split_hi(L, P_DOWN[half], 1, D)

                    def split_down(i):
                        act.wait_ge(weights_used[0], L * USED0_LAYER + (i + USED0_DOWN[half]))
                        split_hi(L, i + P_DOWN[half], 0, D)
                        act.wait_ge(weights_used[1], L * USED1_LAYER + (i + USED1_DOWN[half]))
                        split_hi(L, i + P_DOWN[half], 1, D)
                    with act.Fori(1, pairs) as i:
                        split_down(i)
                    if half == 0:
                        act.wait_ge(weights_used[0], L * USED0_LAYER + USED0_DOWN[half] + pairs)
                        split_hi(L, P_UP[1], 0)

            for t in range(TT):
                act.wait_ge(out_turned, 2 * t + 2)
                A.activation(xnat[:, t, 512:D], bank[2 * t + 1][:, :], ACT.Copy)\
                    .then_inc(out_copied_act, 1)

        @block.tensor
        def _(pe):
            M = nc.tensor.matmul

            def three(dst, w, wsl, h, hsl, first, last):
                M(dst, w[0][wsl], h[0][hsl], start=first, stop=False)
                M(dst, w[1][wsl], h[0][hsl], start=False, stop=False)
                return M(dst, w[0][wsl], h[1][hsl], start=False, stop=last)

            pe.wait_ge(ident_ready, 1)
            pe.wait_ge(params_loaded, 16 * N_PARAM_LOADS)
            for l in range(LAYERS):
                at = 0
                for blk, k in ((0, 4 * FT), (1, 4 * FT), (2, 6 * KD + 3 * KD)):
                    last = nc.tensor.transpose(bank[l][:, at:at + k], prow[0:k, 3 * l + blk, :],
                                               ident[0:k, 0:k])
                    at += k
                last.then_inc(setup_pe, 1)
            nc.tensor.transpose(bank[2][:, 0:12], prow[0:12, 3 * LAYERS, :], ident[0:12, 0:12])\
                .then_inc(setup_pe, 1)
            for m in range(KD):
                b = bank[4 + m % 4]
                if m >= 4:
                    pe.wait_ge(x_done, m - 3)
                for t in range(TT):
                    if m == 0:
                        pe.wait_ge(x_loaded, 16 * TT)
                    last = nc.tensor.transpose(b[:, t * P:(t + 1) * P], xnat[:, t, m * P:(m + 1) * P],
                                               ident[:, :])
                last.then_inc(setup_pe, 1)

            def norm_means(L, which):
                N = L * 2 + which
                for m in range(KD):
                    pe.wait_ge(sq_done, N * KD + m + 1)
                    M(bank[0][:, :], mean_w[:, :], work[m % 2][:, :], start=(m == 0),
                      stop=(m == KD - 1)).then_inc(mean_done, 1)

            def reduce_ada(L, i, b):
                pe.wait_ge(ada_step, (L * 3 + (i + 1)) * ADA_ADDS)
                for a in range(2):
                    for m in range(KD):
                        last = M(b[:, a * KD + m:a * KD + m + 1], ada_acc[a][:, m * P:(m + 1) * P],
                                 ones[:, :], start=True, stop=True)
                last.then_inc(ada_summed, 1)

            def turn_nat(L, g, t):
                k = qk_index(g)
                Q = (L * 4 + k) * TT + t
                pe.wait_ge(nat_ready, Q + 1)
                if k * TT + t >= 2:
                    pe.wait_ge(qk_ready, Q - 1)
                for b in range(4):
                    last = nc.tensor.transpose(bank[4 + t % 2][:, b * P:(b + 1) * P],
                                               work[5 + t % 2][:, b * P:(b + 1) * P], ident[:, :])
                last.then_inc(nat_turned, 1)

            def scores(L, task, n):
                W = (n + 1) * P
                for e in range(2):
                    r = row_of(task, n, e)
                    if r >= 4:
                        pe.wait_ge(score_done, L * ROWS + r - 3)
                    base = 0 if is_diff(task) else 8
                    f = task if is_diff(task) else task - DIFF_TASKS
                    M(bank[(n % 2) * 2 + e][:, 0:W],
                      qkT[e * HEAD:(e + 1) * HEAD, base + f, n * P:(n + 1) * P],
                      qkT[e * HEAD:(e + 1) * HEAD, base + 4 + f, 0:W],
                      start=True, stop=True).then_inc(scores_mm, 1)

            def turn_p(L, task, n):
                for i, e in turn_units(task, n):
                    if is_diff(task):
                        pe.wait_ge(comb_done, (L * T_DIFF + i + 1) * 3)
                    else:
                        pe.wait_ge(exp_done, L * ROWS + row_of(task, n, e) + 1)
                    if i >= 2:
                        pe.wait_ge(pT_ready, L * T_ALL + i - 1)
                    for b in range(n + 1):
                        last = nc.tensor.transpose(bank[4 + i % 2][:, b * P:(b + 1) * P],
                                                   work[(n % 2) * 2 + e][:, b * P:(b + 1) * P],
                                                   ident[:, :])
                    last.then_inc(p_turned, 1)

            def weigh_values(L, task, n):
                for i, e in turn_units(task, n):
                    pe.wait_ge(pT_ready, L * T_ALL + i + 1)
                    if n == 0 and e == 0 and task >= 2:
                        pe.wait_ge(o_lo_done, L * TASKS + task - 1)
                    if is_diff(task):
                        dst, v0, w = n * P, task * P, P
                    else:
                        dst, v0, w = n * P + e * HEAD, GW + (task - DIFF_TASKS) * P + e * HEAD, HEAD
                    for b in range(n + 1):
                        last = M(bank[6 + task % 2][:, dst:dst + w],
                                 work[4 + i % 2][:, b * P:(b + 1) * P], vnat[:, b, v0:v0 + w],
                                 start=(b == 0), stop=(b == n))
                    last.then_inc(pv_done, 1)

            def turn_o(L, task):
                pe.wait_ge(fin_dve, (L * TASKS + task + 1) * 8)
                for n in range(TT):
                    last = nc.tensor.transpose(bank[6 + task % 2][:, n * P:(n + 1) * P],
                                               work[6][:, n * P:(n + 1) * P], ident[:, :])
                last.then_inc(o_turned, 1)

            with pe.Fori(0, LAYERS) as L:
                norm_means(L, 0)
                reduce_ada(L, 0, bank[7])
                for g in range(GROUPS):
                    for s in range(2):
                        pe.wait_ge(lo_ready[s], L * PAIRS + P_IN + g + 1)
                        for t in range(TT):
                            if s == 0 and g:
                                if g - 1 in QK_GROUPS:
                                    pe.wait_ge(nat_mul, (L * 4 + qk_index(g - 1)) * TT + t + 1)
                                else:
                                    pe.wait_ge(v_ready, (L * 2 + (g - 1) // 3) * TT + t + 1)
                            for k in range(4):
                                kt = 4 * s + k
                                if g == 0 and t == 0:
                                    pe.wait_ge(h_lo_done, L * 2 * KD + kt + 1)
                                last = three(bank[t][:, :], (h_hi, h_lo),
                                             (slice(None), kt, slice(t * P, (t + 1) * P)),
                                             (w_hi[s], w_lo[s]),
                                             (slice(None), slice(k * GW, (k + 1) * GW)),
                                             kt == 0, kt == KD - 1)
                            if s == 1:
                                last.then_inc(proj_done, 1)
                            elif t == TT - 1:
                                last.then_inc(weights_used[0], 1)
                            if s == 0 and g - 1 in QK_GROUPS:
                                turn_nat(L, g - 1, t)
                    if g == 2:
                        pe.wait_ge(mod_ready, L * 3 + 1)
                        reduce_ada(L, 1, bank[7])

                pe.wait_ge(qk_ready, (L + 1) * 4 * TT)
                pe.wait_ge(v_ready, (L + 1) * 2 * TT)
                pe.wait_ge(mod_ready, L * 3 + 2)
                steps = [(task, n) for task in range(TASKS) for n in range(TT)]
                scores(L, 0, 0)
                for k, (task, n) in enumerate(steps):
                    if k + 1 < STEPS:
                        scores(L, *steps[k + 1])
                    turn_p(L, task, n)
                    if k:
                        weigh_values(L, *steps[k - 1])
                    if task >= 1 and n == 3:
                        turn_o(L, task - 1)
                weigh_values(L, *steps[-1])
                pe.wait_ge(pT_ready, (L + 1) * T_ALL)
                reduce_ada(L, 2, bank[4])
                turn_o(L, TASKS - 1)

                pe.wait_ge(mod_ready, L * 3 + 3)
                for q in range(OUT_PAIRS):
                    for s in range(2):
                        pe.wait_ge(lo_ready[s], L * PAIRS + P_OUT + q + 1)
                        unit = 2 * q + s
                        for m in range(KD):
                            if unit == 0 and m == 0:
                                pe.wait_ge(o_lo_done, L * TASKS + 2)
                            if unit == 0 and m == 6:
                                pe.wait_ge(o_lo_done, L * TASKS + TASKS)
                            for k in range(2):
                                kt = 2 * unit + k
                                last = three(bank[m][:, :], (w_hi[s], w_lo[s]),
                                             (slice(None), slice(k * D + m * P, k * D + (m + 1) * P)),
                                             (h_hi, h_lo), (slice(None), kt, slice(None)),
                                             kt == 0, kt == KD - 1)
                            if kt == KD - 1:
                                last.then_inc(acc_done, 1)
                        if unit < 2 * OUT_PAIRS - 1:
                            last.then_inc(weights_used[s], 1)
                norm_means(L, 1)

                for half, tiles in enumerate(FFN_SETS):
                    pairs = tiles // 2
                    if half == 0:
                        pe.wait_ge(h_lo_done, (L + 1) * 2 * KD)
                    pe.wait_ge(x_done, L * X_LAYER + (X_INIT + half * KD + 4))
                    pe.nop(nofuse=True)
                    with pe.Fori(0, pairs) as i:
                        X = L * UP_LAYER + (i * 4 + UP_BASE[half])
                        for s in range(2):
                            pe.wait_ge(lo_ready[s], L * PAIRS + (i + (P_UP[half] + 1)))
                            for q in range(2):
                                b = 2 * s + q
                                pe.wait_ge(conv_done, X + b + 1)
                                for kt in range(KD):
                                    last = three(bank[b][:, :], (w_hi[s], w_lo[s]),
                                                 (slice(None), slice(kt * 2 * P + q * P, kt * 2 * P + (q + 1) * P)),
                                                 (h_hi, h_lo), (slice(None), kt, slice(None)),
                                                 kt == 0, kt == KD - 1)
                                last.then_inc(up_done, 1)

                    def down_pair(i, first, final):
                        for s in range(2):
                            pe.wait_ge(lo_ready[s], L * PAIRS + (i + (P_DOWN[half] + 1)))
                            pe.wait_ge(act_lo_done, L * FT + (i * 2 + (FF_BASE[half] + s + 1)))
                            rhs = (slice(None), bass.ds(i * 2 + s, 1), slice(None))
                            start = first and s == 0
                            stop = final and s == 1
                            for m in ((4, 5, 6, 7, 0, 1, 2, 3) if start else range(KD)):
                                if start and m == 4 and half:
                                    pe.wait_ge(x_done, L * X_LAYER + (X_INIT + 2 * KD))
                                if start and m == 0:
                                    pe.wait_ge(conv_done, L * UP_LAYER + UP_BASE[half] + 2 * tiles + 4)
                                last = three(bank[m][:, :].unsqueeze(1), (w_hi[s], w_lo[s]),
                                             (slice(None), slice(m * P, (m + 1) * P)),
                                             (act_hi, act_lo), rhs, start, stop)
                                if stop:
                                    last.then_inc(acc_done, 1)
                            if not stop:
                                last.then_inc(weights_used[s], 1)

                    down_pair(0, True, False)
                    with pe.Fori(1, pairs - 1) as i:
                        down_pair(i, False, False)
                    down_pair(pairs - 1, False, True)

            pe.wait_ge(x_done, X_INIT + LAYERS * X_LAYER)
            for t in range(TT):
                for f in range(2):
                    for m in range(4):
                        last = nc.tensor.transpose(bank[2 * t + f][:, m * P:(m + 1) * P],
                                                   xT[:, 4 * f + m, t * P:(t + 1) * P], ident[:, :])
                    last.then_inc(out_turned, 1)

        @block.vector
        def _(dve):
            V = nc.vector
            count = [0]

            def setup(ins):
                ins.then_inc(setup_dve, 1)
                count[0] += 1
                dve.wait_ge(setup_dve, count[0])
                return count[0]

            V.memset(prow[0:12, 3 * LAYERS, :], 1.0).then_inc(rows_set, 1)
            setup(V.memset(mean_w[:, :], 1.0 / D))
            setup(V.memset(ones[:, :], 1.0))
            V.memset(small[:, 0, :], 1.0).then_inc(conv_done, 4)
            dve.wait_ge(pool_mask, 4)
            setup(V.tensor_scalar(rem[:, 0, :], delta[:, :], 3, None, ALU.bitwise_and))
            setup(V.tensor_scalar(rem[:, 1, :], delta[:, :], 15, None, ALU.bitwise_and))
            setup(V.tensor_scalar(cnt[:, 1, :], rem[:, 0, :], 0.0, None, ALU.is_equal))
            setup(V.tensor_scalar(cnt[:, 2, :], rem[:, 1, :], 0.0, None, ALU.is_equal))
            assert setup(V.tensor_tensor(cnt[:, 1, :], cnt[:, 1, :], cnt[:, 2, :], ALU.add)) == SD_STRIDED
            for l in range(LAYERS):
                dve.wait_ge(setup_pe, l + 1)
                last = setup(V.tensor_copy(par[:, l, :], bank[l][:, 0:PARAMS]))
                assert l or last == SD_PAR0
            dve.wait_ge(setup_pe, LAYERS + 1)
            setup(V.tensor_copy(gcol[:, :], bank[2][:, 0:12]))
            for l in range(LAYERS):
                k = G_SUB * LAYERS + l
                setup(V.tensor_scalar(gcol[:, k:k + 1], gcol[:, k:k + 1], 1.0 - lam_init(l), None,
                                      ALU.mult))
            for m in range(KD):
                dve.wait_ge(setup_pe, LAYERS + 2 + m)
                V.tensor_copy(xT[:, m, :], bank[4 + m % 4][:, :]).then_inc(x_done, 1)
            setup(V.tensor_copy(pos_f[:, :], pos_i[:, :]))
            inv_freq = np.float32(THETA) ** (-np.arange(0, ROPE, 2, dtype=np.float32) / np.float32(ROPE))
            for j in range(ROPE_HALF):
                setup(V.tensor_scalar(ang[:, :, j], pos_f[:, :], float(inv_freq[j]), None, ALU.mult))
            magic = 1.5 * 2 ** 23
            for scale in (2 ** 13, 1):
                setup(V.tensor_scalar(turns[:, :, :], ang[:, :, :], 1 / (2 * math.pi * scale), magic,
                                      ALU.mult, ALU.add))
                setup(V.tensor_scalar(turns[:, :, :], turns[:, :, :], -magic, None, ALU.add))
                for part in split_two_pi(scale):
                    setup(V.scalar_tensor_tensor(out=ang[:, :, :], in0=turns[:, :, :], scalar=-part,
                                                 in1=ang[:, :, :], op0=ALU.mult, op1=ALU.add))
            pi = 3.1415925
            setup(V.tensor_scalar(trig_in[:, 1, :, :], ang[:, :, :], pi, -pi, ALU.min, ALU.max))
            setup(V.scalar_tensor_tensor(out=turns[:, :, :], in0=trig_in[:, 1, :, :], scalar=-1.0,
                                         in1=trig_in[:, 1, :, :], op0=ALU.mult, op1=ALU.max))
            assert setup(V.tensor_scalar(trig_in[:, 0, :, :], turns[:, :, :], -1.0, math.pi / 2,
                                         ALU.mult, ALU.add)) == SD_TRIG
            dve.wait_ge(setup_act, 1)
            for half in range(2):
                sl = slice(half * ROPE_HALF, (half + 1) * ROPE_HALF)
                setup(V.tensor_copy(cos16[:, :, sl], trig[:, 0, :, :]))
                setup(V.tensor_scalar(sin16[:, :, sl], trig[:, 1, :, :], 1.0 if half else -1.0, None,
                                      ALU.mult))
                setup(V.tensor_copy(gswap[:, :, sl],
                                    gnat[:, :, (1 - half) * ROPE_HALF:(2 - half) * ROPE_HALF]))
            tall = [P, 4 * LAYERS, TT, ROPE]
            setup(V.tensor_tensor(ropeC[:, :, :, :], cos16[:, :, :].unsqueeze(1).to_broadcast(tall),
                                  gnat[:, :, :].unsqueeze(2).to_broadcast(tall), ALU.mult))
            setup(V.tensor_tensor(ropeS[:, :, :, :], sin16[:, :, :].unsqueeze(1).to_broadcast(tall),
                                  gswap[:, :, :].unsqueeze(2).to_broadcast(tall), ALU.mult))
            for i in range(2):
                setup(V.tensor_tensor(lamv[:, 2 * i, :, :], lamv[:, 2 * i, :, :],
                                      lamv[:, 2 * i + 1, :, :], ALU.mult))
                last = setup(V.tensor_reduce(lam_s[:, 0, 2 * i:2 * i + 2], lamv[:, 2 * i, :, :],
                                             AX.X, ALU.add))
            assert last == SD_LAM
            dve.wait_ge(setup_act, 2)
            for l in range(LAYERS):
                setup(V.tensor_tensor(neglam[:, l:l + 1], lam_s[:, 1, 2 + l:3 + l],
                                      lam_s[:, 1, l:l + 1], ALU.subtract))
                setup(V.tensor_scalar(neglam[:, l:l + 1], neglam[:, l:l + 1], -lam_init(l), None,
                                      ALU.add))
            dve.wait_ge(pool_mask, 8)
            setup(V.tensor_tensor(cnt[:, 0, :], cnt[:, 0, :], cnt[:, 1, :], ALU.add))
            setup(V.tensor_scalar(maskB[:, :], cnt[:, 0, :], 0.0, BIG, ALU.is_equal, ALU.mult))
            for m in (2, 3):
                setup(V.tensor_scalar(cnt[:, 1 + m, :], cnt[:, 0, :], float(m), -math.log(m),
                                      ALU.is_equal, ALU.mult))
                setup(V.tensor_tensor(maskB[:, :], maskB[:, :], cnt[:, 1 + m, :], ALU.add))

            def take_mod(L, i, b):
                dve.wait_ge(ada_summed, L * 3 + i + 1)
                V.tensor_tensor(mod[:, 2 * i * KD:2 * (i + 1) * KD], b[:, 0:2 * KD],
                                par[:, L, C_ADA + 2 * i * KD:C_ADA + 2 * (i + 1) * KD], ALU.add)\
                    .then_inc(mod_ready, 1)

            def norm(L, which):
                N = L * 2 + which
                scale, gain = ((SC_A, C_GMIX), (SC_F, C_GFFN))[which]
                dve.wait_ge(mod_ready, L * 3 + 1 + 2 * which)
                V.scalar_tensor_tensor(out=afac[:, :], in0=mod[:, scale * KD:(scale + 1) * KD],
                                       scalar=1.0, in1=par[:, L, gain:gain + KD],
                                       op0=ALU.add, op1=ALU.mult).then_inc(afac_done, 1)
                dve.wait_ge(afac_done, N * 2 + 1)
                V.tensor_scalar(afac[:, :], afac[:, :], -0.5, None, ALU.mult).then_inc(afac_done, 1)
                dve.wait_ge(mean_done, (N + 1) * KD)
                V.tensor_scalar(work[2][:, :], bank[0][:, :], EPS, None, ALU.add).then_inc(norm_dve, 1)
                dve.wait_ge(norm_act, N * 3 + 3)
                V.tensor_tensor(work[5][:, :], work[5][:, :], work[2][:, :], ALU.mult)\
                    .then_inc(norm_dve, 1)
                dve.wait_ge(norm_dve, N * 3 + 2)
                V.scalar_tensor_tensor(out=work[4][:, :], in0=work[5][:, :], scalar=-3.0,
                                       in1=work[4][:, :], op0=ALU.add, op1=ALU.mult)\
                    .then_inc(norm_dve, 1)
                dve.wait_ge(norm_dve, N * 3 + 3)
                dve.wait_ge(afac_done, N * 2 + 2)
                shift = (SH_A, SH_F)[which] * KD

                def lo(m):
                    dve.wait_ge(h_hi_done, N * KD + m + 1)
                    V.scalar_tensor_tensor(out=h_lo[:, m, :], in0=work[6 + m % 2][:, :],
                                           scalar=mod[:, shift + m:shift + m + 1],
                                           in1=h_hi[:, m, :], op0=ALU.add, op1=ALU.subtract)\
                        .then_inc(h_lo_done, 1)
                for m in range(KD):
                    if m >= 2:
                        dve.wait_ge(h_lo_done, N * KD + m - 1)
                    V.scalar_tensor_tensor(out=work[6 + m % 2][:, :], in0=xT[:, m, :],
                                           scalar=afac[:, m:m + 1], in1=work[4][:, :],
                                           op0=ALU.mult, op1=ALU.mult).then_inc(h_pre, 1)
                    if m:
                        lo(m - 1)
                lo(KD - 1)

            def newton(dst, y, v, tmp, done, base):
                V.tensor_tensor(tmp, y, y, ALU.mult).then_inc(done, 1)
                dve.wait_ge(done, base + 1)
                V.tensor_tensor(tmp, tmp, v, ALU.mult).then_inc(done, 1)
                dve.wait_ge(done, base + 2)
                V.scalar_tensor_tensor(out=dst, in0=tmp, scalar=-3.0, in1=y, op0=ALU.add,
                                       op1=ALU.mult).then_inc(done, 1)
                dve.wait_ge(done, base + 3)

            def nat(L, g, t):
                k = qk_index(g)
                Q = (L * 4 + k) * TT + t
                heads = [P, GH, HEAD]
                dve.wait_ge(nat_act, Q * 3 + 1)
                V.tensor_reduce(small[:, 3, :], work[7][:, :].rearrange("p (h d) -> p h d", d=HEAD),
                                AX.X, ALU.add).then_inc(nat_dve, 1)
                dve.wait_ge(nat_dve, Q * 5 + 1)
                V.tensor_scalar(small[:, 0, :], small[:, 3, :], 1.0 / HEAD, EPS, ALU.mult, ALU.add)\
                    .then_inc(nat_dve, 1)
                dve.wait_ge(nat_act, Q * 3 + 3)
                newton(small[:, 4, :], small[:, 2, :], small[:, 0, :], small[:, 5, :], nat_dve,
                       Q * 5 + 2)
                buf = work[5 + t % 2]
                if k * TT + t >= 2:
                    dve.wait_ge(nat_turned, Q - 1)
                fac = -0.5 * (-HEAD ** -0.5 if g in (0, 3) else 1.0)
                V.scalar_tensor_tensor(out=buf[:, :].rearrange("p (h d) -> p h d", d=HEAD),
                                       in0=bank[t][:, :].rearrange("p (h d) -> p h d", d=HEAD),
                                       scalar=fac, in1=small[:, 4, :].unsqueeze(2).to_broadcast(heads),
                                       op0=ALU.mult, op1=ALU.mult).then_inc(nat_mul, 1)
                dve.wait_ge(nat_mul, Q + 1)
                head = buf[:, :].rearrange("p (h d) -> p h d", d=HEAD)[:, :, 0:ROPE]
                pair = head.rearrange("p h (a d) -> p h a d", a=2)
                own = work[4][:, 0:GH * ROPE].rearrange("p (h d) -> p h d", d=ROPE)
                other = work[4][:, GH * ROPE:2 * GH * ROPE].rearrange("p (h a d) -> p h a d", a=2,
                                                                      d=ROPE_HALF)
                table = bass.ds(L + LAYERS * k, 1)
                V.tensor_tensor(own, head, ropeC[:, table, t, :].to_broadcast([P, GH, ROPE]),
                                ALU.mult).then_inc(rope_dve, 1)
                V.tensor_tensor(other, pair[:, :, ::-1, :],
                                ropeS[:, table, t, :].rearrange("p o (a d) -> p o a d", a=2)
                                .to_broadcast([P, GH, 2, ROPE_HALF]), ALU.mult).then_inc(rope_dve, 1)
                dve.wait_ge(rope_dve, Q * 2 + 2)
                V.tensor_tensor(head, own, other.rearrange("p h a d -> p h (a d)"), ALU.add)\
                    .then_inc(nat_ready, 1)
                dve.wait_ge(nat_ready, Q + 1)

            def score_rows(L, task, n):
                W = (n + 1) * P
                mask = maskA if is_diff(task) else maskB
                for e in range(2):
                    r = row_of(task, n, e)
                    dve.wait_ge(scores_mm, L * ROWS + r + 1)
                    if task * TT + n >= 2:
                        last_unit = turn_units(*divmod(task * TT + n - 2, TT))[-1][0]
                        dve.wait_ge(p_turned, L * T_ALL + last_unit + 1)
                    dve.nop(nofuse=True)
                    V.tensor_tensor_reduce(work[(n % 2) * 2 + e][:, 0:W],
                                           bank[(n % 2) * 2 + e][:, 0:W], mask[:, S - W:S],
                                           1.0, 3e38, ALU.add, ALU.min, mneg[:, r:r + 1])\
                        .then_inc(score_done, 1)

            def combine(L, task, n):
                W = (n + 1) * P
                i = task * TT + n
                B = (L * T_DIFF + i) * 3
                r = row_of(task, n, 0)
                c2 = comb[:, n % 2, :]
                dve.wait_ge(exp_done, L * ROWS + r + 2)
                V.reciprocal(c2[:, 0:1], lsum[:, r + 1:r + 2]).then_inc(comb_done, 1)
                dve.wait_ge(comb_done, B + 1)
                V.scalar_tensor_tensor(out=c2[:, 1:2], in0=lsum[:, r:r + 1], scalar=c2[:, 0:1],
                                       in1=neglam[:, bass.ds(L, 1)], op0=ALU.mult, op1=ALU.mult)\
                    .then_inc(comb_done, 1)
                dve.wait_ge(comb_done, B + 2)
                p1, p2 = (work[(n % 2) * 2 + e][:, 0:W] for e in range(2))
                V.scalar_tensor_tensor(out=p1, in0=p2, scalar=c2[:, 1:2], in1=p1,
                                       op0=ALU.mult, op1=ALU.add).then_inc(comb_done, 1)

            def finish(L, task, stage):
                F = L * TASKS + task
                per = 1 if is_diff(task) else 2
                k = TT * per
                shape = [P, k, P // per]
                o = work[6][:, :].rearrange("p (k d) -> p k d", k=k)
                if stage == 1:
                    dve.wait_ge(pv_done, L * T_ALL + turn_units(task, TT - 1)[-1][0] + 1)
                    r0 = row_of(task, 0, 0)
                    V.reciprocal(small[:, 3, 0:k], lsum[:, r0:r0 + 8:2 // per]).then_inc(fin_dve, 1)
                    dve.wait_ge(fin_dve, F * 8 + 1)
                    if task:
                        dve.wait_ge(o_turned, F)
                    V.tensor_tensor(o, bank[6 + task % 2][:, :].rearrange("p (k d) -> p k d", k=k),
                                    small[:, 3, 0:k].unsqueeze(2).to_broadcast(shape), ALU.mult)\
                        .then_inc(fin_dve, 1)
                if stage == 2:
                    dve.wait_ge(fin_act, F * 3 + 1)
                    V.tensor_reduce(small[:, 5, 0:k], work[7][:, :].rearrange("p (k d) -> p k d", k=k),
                                    AX.X, ALU.add).then_inc(fin_dve, 1)
                    dve.wait_ge(fin_dve, F * 8 + 3)
                    V.tensor_scalar(small[:, 0, :], small[:, 5, :], per / P, EPS, ALU.mult,
                                    ALU.add).then_inc(fin_dve, 1)
                if stage == 3:
                    dve.wait_ge(fin_act, F * 3 + 3)
                    newton(small[:, 4, 0:k], small[:, 2, 0:k], small[:, 0, 0:k], small[:, 5, 0:k],
                           fin_dve, F * 8 + 4)
                    V.scalar_tensor_tensor(out=o, in0=o, scalar=-0.5,
                                           in1=small[:, 4, 0:k].unsqueeze(2).to_broadcast(shape),
                                           op0=ALU.mult, op1=ALU.mult).then_inc(fin_dve, 1)
                if stage == 4:
                    dve.wait_ge(o_hi_done, F + 1)
                    kind = G_SUB if is_diff(task) else G_OUT
                    V.scalar_tensor_tensor(out=h_lo[:, task, :], in0=bank[6 + task % 2][:, :],
                                           scalar=gcol[:, bass.ds(L + LAYERS * kind, 1)],
                                           in1=h_hi[:, task, :], op0=ALU.mult, op1=ALU.subtract)\
                        .then_inc(o_lo_done, 1)

            def update_x(L, which, gate):
                for m in range(KD):
                    dve.wait_ge(acc_done, L * X_LAYER + which * KD + m + 1)
                    V.scalar_tensor_tensor(out=xT[:, m, :], in0=bank[m][:, :],
                                           scalar=mod[:, gate * KD + m:gate * KD + m + 1],
                                           in1=xT[:, m, :], op0=ALU.mult, op1=ALU.add)\
                        .then_inc(x_done, 1)

            with dve.Fori(0, LAYERS) as L:
                split_lo(L, 0, 0)
                take_mod(L, 0, bank[7])
                norm(L, 0)
                for g in range(GROUPS):
                    split_lo(L, g, 1)
                    split_lo(L, g + 1, 0)
                    for t in range(TT):
                        if g in QK_GROUPS:
                            nat(L, g, t)
                    if g == 3:
                        take_mod(L, 1, bank[7])
                split_lo(L, P_OUT, 1)

                steps = [(task, n) for task in range(TASKS) for n in range(TT)]
                score_rows(L, 0, 0)
                for k, (task, n) in enumerate(steps):
                    if is_diff(task):
                        combine(L, task, n)
                    if task >= 1 and n >= 1:
                        finish(L, task - 1, n)
                    if k + 1 < STEPS:
                        score_rows(L, *steps[k + 1])
                    if n == 0 and task >= 2:
                        finish(L, task - 2, 4)
                finish(L, TASKS - 2, 4)
                take_mod(L, 2, bank[4])
                for stage in (1, 2, 3, 4):
                    finish(L, TASKS - 1, stage)

                for q in range(OUT_PAIRS):
                    if q:
                        split_lo(L, P_OUT + q, 1)
                    split_lo(L, P_OUT + q + 1, 0)
                update_x(L, 0, GT_A)
                norm(L, 1)

                for half, tiles in enumerate(FFN_SETS):
                    pairs = tiles // 2
                    with dve.Fori(0, pairs) as i:
                        X = L * UP_LAYER + (i * 4 + UP_BASE[half])
                        Y = L * FT + (i * 2 + FF_BASE[half])
                        split_lo(L, i + P_UP[half], 1)
                        for part in range(2):
                            for q in range(2):
                                b = 2 * part + q
                                col = i * 2 + (part * FT + FF_BASE[half] + q)
                                dve.wait_ge(tap2_done, X + b + 1)
                                for tap, lag, done in ((C_W1, 1, tap1_done), (C_W0, 2, conv_done)):
                                    V.scalar_tensor_tensor(
                                        out=work[b][:, lag:S], in0=bank[b][:, 0:S - lag],
                                        scalar=par[:, L, bass.ds(col + tap, 1)],
                                        in1=work[b][:, lag:S], op0=ALU.mult, op1=ALU.add)\
                                        .then_inc(done, 1)
                                    if tap == C_W1:
                                        dve.wait_ge(tap1_done, X + b + 1)
                            if part == 0:
                                split_lo(L, i + (P_UP[half] + 1), 0)
                        for q in range(2):
                            dve.wait_ge(silu_done, Y + q + 1)
                            dve.wait_ge(conv_done, X + 6 + q + 1)
                            V.tensor_tensor(work[2 + q][:, :], work[2 + q][:, :], work[4 + q][:, :],
                                            ALU.mult).then_inc(prod_done, 1)
                        for q in range(2):
                            dve.wait_ge(act_hi_done, Y + q + 1)
                            V.tensor_tensor(act_lo[:, bass.ds(i * 2 + q, 1), :],
                                            work[2 + q][:, :].unsqueeze(1),
                                            act_hi[:, bass.ds(i * 2 + q, 1), :], ALU.subtract)\
                                .then_inc(act_lo_done, 1)
                    split_lo(L, P_DOWN[half], 1, D)
                    with dve.Fori(1, pairs) as i:
                        for s in range(2):
                            split_lo(L, i + P_DOWN[half], s, D)
                    if half == 0:
                        split_lo(L, P_UP[1], 0)
                    update_x(L, 1 + half, GT_F)

            for t in range(TT):
                dve.wait_ge(out_turned, 2 * t + 1)
                V.tensor_copy(xnat[:, t, 0:512], bank[2 * t][:, :]).then_inc(out_copied_dve, 1)


SD_STRIDED = 7
SD_PAR0 = SD_STRIDED + 1
SD_TRIG = SD_PAR0 + LAYERS - 1 + 1 + LAYERS + 1 + ROPE_HALF + 2 * 6 + 3
SD_LAM = SD_TRIG + 6 + 2 + 4
N_PARAM_LOADS = LAYERS * 8 + 4 * 3 + 8

_INS = ["x", "c", "positions", "g_mix", "g_ffn", "w_ada", "b_ada", "w_in", "w_out", "diff_q_g",
        "diff_k_g", "lam_q1", "lam_k1", "lam_q2", "lam_k2", "diff_subln_g", "dil_q_g", "dil_k_g",
        "dil_out_g", "w_up", "conv_w", "conv_b", "w_down"]


def kernel(**inputs):
    import concourse.bacc as bacc
    from concourse.bass_utils import run_bass_kernel_spmd

    nc = bacc.Bacc("TRN2", target_bir_lowering=False, num_devices=1)
    arrays, args = {}, []
    for name in _INS:
        a = np.ascontiguousarray(inputs[name])
        arrays[f"in_{name}"] = a
        args.append(nc.dram_tensor(f"in_{name}", a.shape, mybir.dt.from_np(a.dtype),
                                   kind="ExternalInput").ap())
    args.append(nc.dram_tensor("out_x", (1, S, D), F32, kind="ExternalOutput").ap())
    trunk_kernel(nc, *args)
    r = run_bass_kernel_spmd(nc, [arrays], core_ids=[0])
    return r.results[0]["out_x"]
```

```python
import math
from contextlib import ExitStack

import numpy as np

import concourse.bass as bass
from concourse import mybir

F32 = mybir.dt.float32
F32R = mybir.dt.float32r
I32 = mybir.dt.int32
ALU = mybir.AluOpType
ACT = mybir.ActivationFunctionType
AX = mybir.AxisListType

P = 128
LAYERS = 2
D = 1024
S = 512
HEAD = 64
D_FF = 2816
ROPE = HEAD // 4
ROPE_HALF = ROPE // 2
THETA = 500000.0
EPS = 1e-6
BIG = 1e30

KD = D // P
TT = S // P
GROUPS = 6
GW = 512
GH = GW // HEAD
FT = D_FF // P
FFN_SETS = (12, 10)
ACT_SLOTS = max(FFN_SETS)
TASKS = 8
DIFF_TASKS = 4
STEPS = TASKS * TT
ROWS = 2 * STEPS
T_DIFF = DIFF_TASKS * TT
T_ALL = T_DIFF + 2 * (TASKS - DIFF_TASKS) * TT
SLOT = 2048

P_IN = 0
P_OUT = P_IN + GROUPS
OUT_PAIRS = 2
P_UP, P_DOWN = [], []
_p = P_OUT + OUT_PAIRS
for _n in FFN_SETS:
    P_UP.append(_p)
    P_DOWN.append(_p + _n // 2)
    _p += _n
PAIRS = _p

USED0_LAYER = GROUPS + OUT_PAIRS + FT // 2
USED1_LAYER = (OUT_PAIRS - 1) + sum(n // 2 - 1 for n in FFN_SETS)
USED0_OUT = GROUPS
USED1_OUT = 0
USED0_DOWN = [GROUPS + OUT_PAIRS, GROUPS + OUT_PAIRS + FFN_SETS[0] // 2]
USED1_DOWN = [OUT_PAIRS - 1, OUT_PAIRS - 1 + FFN_SETS[0] // 2 - 1]

UP_LAYER = 2 * FT
UP_BASE = [0, 2 * FFN_SETS[0]]
FF_BASE = [0, FFN_SETS[0]]
X_LAYER = 3 * KD
X_INIT = KD

ADA_ADDS = 2 * (KD - 1)

W_SQ, W_NAT, W_ROPE, W_PROB, W_TURNED, W_OSQ, W_OUT = 0, 1, 3, 4, 8, 9, 10
W_TILE, W_V, W_Y, W_YY = 8, 10, 11, 12
ADA_SLOT = 2 * TT - 1

C_W0, C_W1, C_W2, C_B = (i * 2 * FT for i in range(4))
C_ADA = 8 * FT
C_GMIX = C_ADA + 6 * KD
C_GFFN = C_GMIX + KD
C_COND = C_GFFN + KD
PARAMS = C_COND + KD
SH_A, SC_A, GT_A, SH_F, SC_F, GT_F = range(6)
G_DQ, G_DK, G_LQ, G_LK, G_SUB, G_OUT = range(6)


def lam_init(layer):
    return 0.8 - 0.6 * math.exp(-0.3 * layer)


def split_two_pi(scale):
    rest, parts = 2 * math.pi * scale, []
    for _ in range(3):
        ulp = 2.0 ** (math.floor(math.log2(rest)) - 7)
        part = math.floor(rest / ulp) * ulp
        parts.append(part)
        rest -= part
    return parts + [float(np.float32(rest))]


def trunk_kernel(nc, x, c, positions, g_mix, g_ffn, w_ada, b_ada, w_in, w_out, diff_q_g, diff_k_g,
                 lam_q1, lam_k1, lam_q2, lam_k2, diff_subln_g, dil_q_g, dil_k_g, dil_out_g,
                 w_up, conv_w, conv_b, w_down, out):
    ctx = ExitStack()
    with ctx:
        def sb(name, shape, dt=F32):
            return ctx.enter_context(nc.sbuf_tensor(name, shape, dt))

        def sem(name):
            return ctx.enter_context(nc.semaphore(name))

        xT = sb("xT", [P, KD, S])
        h_hi = sb("h_hi", [P, KD, S], F32R)
        h_lo = sb("h_lo", [P, KD, S], F32R)
        w_raw = [sb(f"w_raw{s}", [P, SLOT]) for s in range(2)]
        w_hi = [sb(f"w_hi{s}", [P, SLOT], F32R) for s in range(2)]
        w_lo = [sb(f"w_lo{s}", [P, SLOT], F32R) for s in range(2)]
        ada_raw = [sb(f"ada_raw{i}", [P, D]) for i in range(2)]
        ada_acc = sb("ada_acc", [P, 2 * D])
        scratch = sb("scratch", [P, 14, S])
        work = [scratch[:, i, :] for i in range(14)]
        ada_first = [scratch[:, 4 * i:4 * i + 4, :].rearrange("p a n -> p (a n)") for i in range(2)]
        maskA = sb("maskA", [P, S])
        maskB = sb("maskB", [P, S])
        ident = sb("ident", [P, P])
        mean_w = sb("mean_w", [P, P])
        ones = sb("ones", [P, 1])
        par = sb("par", [P, LAYERS, PARAMS])
        gcol = sb("gcol", [P, 6 * LAYERS])
        mod = sb("mod", [P, 6 * KD])
        cond = sb("cond", [P, KD])
        afac = sb("afac", [P, KD])
        neglam = sb("neglam", [P, LAYERS])
        ropeC = sb("ropeC", [P, 4 * LAYERS, TT, ROPE])
        ropeS = sb("ropeS", [P, 4 * LAYERS, TT, ROPE])
        small = sb("small", [P, 6, GH])
        fsmall = sb("fsmall", [P, 6, GH])
        mneg = sb("mneg", [P, ROWS])
        lsum = sb("lsum", [P, ROWS])
        comb = sb("comb", [P, 2, 2])
        with ExitStack() as inner:
            qkT = inner.enter_context(nc.sbuf_tensor("qkT", [P, 16, S], F32))
            vnat = inner.enter_context(nc.sbuf_tensor("vnat", [P, TT, 2 * GW], F32))
        with ExitStack() as inner:
            act_hi = inner.enter_context(nc.sbuf_tensor("act_hi", [P, ACT_SLOTS, S], F32R))
            act_lo = inner.enter_context(nc.sbuf_tensor("act_lo", [P, ACT_SLOTS, S], F32R))
        with ExitStack() as inner:
            xnat = inner.enter_context(nc.sbuf_tensor("xnat", [P, TT, D], F32))
            prow = inner.enter_context(nc.sbuf_tensor("prow", [P, 3 * LAYERS + 1, P], F32))
            lamv = inner.enter_context(nc.sbuf_tensor("lamv", [P, 4, LAYERS, HEAD], F32))
            gnat = inner.enter_context(nc.sbuf_tensor("gnat", [P, 4 * LAYERS, ROPE], F32))
            gswap = inner.enter_context(nc.sbuf_tensor("gswap", [P, 4 * LAYERS, ROPE], F32))
            pos_i = inner.enter_context(nc.sbuf_tensor("pos_i", [P, TT], I32))
            pos_f = inner.enter_context(nc.sbuf_tensor("pos_f", [P, TT], F32))
            ang = inner.enter_context(nc.sbuf_tensor("ang", [P, TT, ROPE_HALF], F32))
            turns = inner.enter_context(nc.sbuf_tensor("turns", [P, TT, ROPE_HALF], F32))
            trig_in = inner.enter_context(nc.sbuf_tensor("trig_in", [P, 2, TT, ROPE_HALF], F32))
            trig = inner.enter_context(nc.sbuf_tensor("trig", [P, 2, TT, ROPE_HALF], F32))
            cos16 = inner.enter_context(nc.sbuf_tensor("cos16", [P, TT, ROPE], F32))
            sin16 = inner.enter_context(nc.sbuf_tensor("sin16", [P, TT, ROPE], F32))
            delta = inner.enter_context(nc.sbuf_tensor("delta", [P, S], I32))
            rem = inner.enter_context(nc.sbuf_tensor("rem", [P, 2, S], I32))
            cnt = inner.enter_context(nc.sbuf_tensor("cnt", [P, 5, S], F32))
            lam_s = inner.enter_context(nc.sbuf_tensor("lam_s", [P, 3, 4], F32))

        bank = [ctx.enter_context(nc.psum_tensor(f"bank{i}", [P, 512], F32)) for i in range(8)]

        params_loaded = sem("params_loaded")
        x_loaded = sem("x_loaded")
        rows_set = sem("rows_set")
        ident_ready = sem("ident_ready")
        pool_mask = sem("pool_mask")
        setup_dve = sem("setup_dve")
        setup_act = sem("setup_act")
        setup_pe = sem("setup_pe")
        cond_ready = sem("cond_ready")
        raw_loaded = [sem(f"raw_loaded{s}") for s in range(2)]
        hi_ready = [sem(f"hi_ready{s}") for s in range(2)]
        lo_ready = [sem(f"lo_ready{s}") for s in range(2)]
        weights_used = [sem(f"weights_used{s}") for s in range(2)]
        ada_loaded = [sem(f"ada_loaded{i}") for i in range(2)]
        first_loaded = [sem(f"first_loaded{i}") for i in range(2)]
        first_summed = sem("first_summed")
        ada_scaled = sem("ada_scaled")
        ada_step = sem("ada_step")
        ada_summed = sem("ada_summed")
        mod_ready = sem("mod_ready")
        x_done = sem("x_done")
        sq_done = sem("sq_done")
        mean_done = sem("mean_done")
        norm_dve = sem("norm_dve")
        norm_act = sem("norm_act")
        afac_done = sem("afac_done")
        h_pre = sem("h_pre")
        h_hi_done = sem("h_hi_done")
        h_lo_done = sem("h_lo_done")
        proj_done = sem("proj_done")
        nat_act = sem("nat_act")
        nat_dve = sem("nat_dve")
        rope_dve = sem("rope_dve")
        nat_mul = sem("nat_mul")
        nat_ready = sem("nat_ready")
        nat_turned = sem("nat_turned")
        qk_ready = sem("qk_ready")
        v_ready = sem("v_ready")
        scores_mm = sem("scores_mm")
        score_done = sem("score_done")
        exp_done = sem("exp_done")
        comb_done = sem("comb_done")
        p_turned = sem("p_turned")
        pT_ready = sem("pT_ready")
        pv_done = sem("pv_done")
        fin_dve = sem("fin_dve")
        fin_act = sem("fin_act")
        o_turned = sem("o_turned")
        o_hi_done = sem("o_hi_done")
        o_lo_done = sem("o_lo_done")
        acc_done = sem("acc_done")
        up_done = sem("up_done")
        tap2_done = sem("tap2_done")
        tap1_done = sem("tap1_done")
        conv_done = sem("conv_done")
        silu_done = sem("silu_done")
        prod_done = sem("prod_done")
        act_hi_done = sem("act_hi_done")
        act_lo_done = sem("act_lo_done")
        out_turned = sem("out_turned")
        out_copied_dve = sem("out_copied_dve")
        out_copied_act = sem("out_copied_act")
        out_stored = sem("out_stored")

        def is_diff(task):
            return task < DIFF_TASKS

        def turn_units(task, n):
            if is_diff(task):
                return [(task * TT + n, 0)]
            base = T_DIFF + (task - DIFF_TASKS) * 2 * TT + 2 * n
            return [(base, 0), (base + 1, 1)]

        def score_bank(task, n, e):
            return bank[4 + e] if is_diff(task) or n % 2 else bank[e]

        def turn_bank(i):
            return bank[6] if i < T_DIFF or i % 2 else bank[2]

        def out_bank(task):
            return bank[7] if is_diff(task) or task % 2 else bank[3]

        def prob(n, e):
            return work[W_PROB + (n % 2) * 2 + e]

        def turned(i):
            return work[W_TURNED if i < T_DIFF or i % 2 == 0 else W_NAT]

        def normed(task):
            return work[W_OUT + task] if is_diff(task) else work[W_NAT + 1 + task % 2]

        def f_bank(task):
            return bank[7] if is_diff(task) else out_bank(task)

        def row_of(task, n, e):
            return task * 8 + 2 * n + e

        QK_GROUPS = [0, 1, 3, 4]

        def qk_index(g):
            return QK_GROUPS.index(g)

        def slot_of(g, s, t):
            return (g - 3) * 2 * TT + s * TT + t

        def turned_tile(g, s, t):
            g, t = (g, t - 2) if s == 1 and t >= 2 else (g - 1, t + 2) if s == 0 and t < 2 else (-1, 0)
            return (g, t) if g in QK_GROUPS else None

        def has(a):
            return 0 <= a < T_DIFF

        def has_end(a):
            return has(a) and a % TT == 0

        def step(a):
            return divmod(a, TT)

        def slot_free(eng, L, p, s):
            if p == 0:
                eng.wait_ge(weights_used[0], L * USED0_LAYER + 1)
                if s == 1:
                    eng.wait_ge(acc_done, L * X_LAYER + 1)
                return
            q = p - 1
            if q < P_OUT:
                if s == 0:
                    eng.wait_ge(weights_used[0], L * USED0_LAYER + q + 2)
                else:
                    eng.wait_ge(proj_done, (L * GROUPS + q + 1) * TT)
                return
            if q < P_OUT + OUT_PAIRS:
                if s == 0:
                    eng.wait_ge(weights_used[0], L * USED0_LAYER + USED0_OUT + q - P_OUT + 2)
                elif q == P_OUT + OUT_PAIRS - 1:
                    eng.wait_ge(acc_done, L * X_LAYER + KD + 1)
                else:
                    eng.wait_ge(weights_used[1], L * USED1_LAYER + USED1_OUT + q - P_OUT + 1)
                return
            raise AssertionError("pairs of the feed-forward loops have waits of their own")

        def split_hi(L, p, s, width=SLOT):
            nc.scalar.wait_ge(raw_loaded[s], (L * PAIRS + p + 1) * 16)
            nc.scalar.activation(w_hi[s][:, 0:width], w_raw[s][:, 0:width], ACT.Copy)\
                .then_inc(hi_ready[s], 1)

        def split_lo(L, p, s, width=SLOT):
            nc.vector.wait_ge(hi_ready[s], L * PAIRS + p + 1)
            nc.vector.tensor_tensor(w_lo[s][:, 0:width], w_raw[s][:, 0:width],
                                    w_hi[s][:, 0:width], ALU.subtract).then_inc(lo_ready[s], 1)

        block = ctx.enter_context(nc.Block())

        @block.sync
        def _(sp):
            for t in range(TT):
                sp.dma_start(xnat[:, t, :], x[0, t * P:(t + 1) * P, :]).then_inc(x_loaded, 16)
            n = 0
            for l in range(LAYERS):
                rows = [(0, 0, conv_w[l, 0], 2 * FT), (0, 2 * FT, conv_w[l, 1], 2 * FT),
                        (1, 0, conv_w[l, 2], 2 * FT), (1, 2 * FT, conv_b[l], 2 * FT),
                        (2, 0, b_ada[l], 6 * KD), (2, 6 * KD, g_mix[l], KD),
                        (2, 7 * KD, g_ffn[l], KD), (2, 8 * KD, c[0], KD)]
                for blk, r0, src, k in rows:
                    sp.dma_start(prow[r0:r0 + k, 3 * l + blk, :],
                                 src.rearrange("(r q) -> r q", q=P)).then_inc(params_loaded, 16)
                    n += 1
            def load_first(k):
                sp.dma_start(ada_first[k % 2], w_ada[0, k * P:(k + 1) * P, 0:2 * D])\
                    .then_inc(first_loaded[k % 2], 16)
            load_first(0)
            load_first(1)
            sp.wait_ge(rows_set, 1)
            G = 3 * LAYERS
            for k, g in enumerate((diff_q_g, diff_k_g, dil_q_g, dil_k_g)):
                for half in range(2):
                    sp.dma_start(prow[2 * k:2 * k + 2, G, half * HEAD + ROPE:(half + 1) * HEAD],
                                 g[:, ROPE:HEAD]).then_inc(params_loaded, 16)
                    n += 1
                sp.dma_start(gnat[:, 2 * k:2 * k + 2, :],
                             g[:, 0:ROPE].partition_broadcast(P)).then_inc(params_loaded, 16)
                n += 1
            sp.dma_start(prow[2 * G_SUB:2 * G_SUB + 2, G, :], diff_subln_g).then_inc(params_loaded, 16)
            for half in range(2):
                sp.dma_start(prow[2 * G_OUT:2 * G_OUT + 2, G, half * HEAD:(half + 1) * HEAD],
                             dil_out_g).then_inc(params_loaded, 16)
            for i, v in enumerate((lam_q1, lam_k1, lam_q2, lam_k2)):
                sp.dma_start(lamv[:, i, :, :], v.partition_broadcast(P)).then_inc(params_loaded, 16)
            with nc.allow_non_contiguous_dma(reason="512 positions, one a partition and tile"):
                sp.dma_start(pos_i[:, :], positions[0].rearrange("(t p) -> p t", p=P))\
                    .then_inc(params_loaded, 16)
            assert n + 8 == N_PARAM_LOADS
            for k in range(2, KD):
                sp.wait_ge(first_summed, k - 1)
                load_first(k)

            def load(L, p, s, dst, src):
                sp.wait_ge(lo_ready[s], L * PAIRS + p + 1)
                sp.dma_start(dst, src).then_inc(raw_loaded[s], 16)

            with sp.Fori(0, LAYERS) as L:
                for g in range(GROUPS):
                    for s in range(2):
                        load(L, P_IN + g, s, w_raw[s][:, :].rearrange("p (k n) -> p k n", n=GW),
                             w_in[L, s * 512:(s + 1) * 512, g * GW:(g + 1) * GW]
                             .rearrange("(k p) n -> p k n", p=P))
                for q in range(OUT_PAIRS):
                    for s in range(2):
                        r0 = (2 * q + s) * 2 * P
                        load(L, P_OUT + q, s, w_raw[s][:, :].rearrange("p (k n) -> p k n", n=D),
                             w_out[L, r0:r0 + 2 * P, :].rearrange("(k p) n -> p k n", p=P))
                for half, tiles in enumerate(FFN_SETS):
                    with sp.Fori(0, tiles // 2) as i:
                        for s in range(2):
                            col = i * (2 * P) + (s * D_FF + FF_BASE[half] * P)
                            load(L, P_UP[half] + i, s,
                                 w_raw[s][:, :].rearrange("p (k n) -> p k n", n=2 * P),
                                 w_up[L, :, bass.ds(col, 2 * P)].rearrange("(k p) n -> p k n", p=P))
                    with sp.Fori(0, tiles // 2) as i:
                        for s in range(2):
                            row = i * (2 * P) + (s * P + FF_BASE[half] * P)
                            load(L, P_DOWN[half] + i, s, w_raw[s][:, 0:D],
                                 w_down[L, bass.ds(row, P), :])
            for t in range(TT):
                sp.wait_ge(out_copied_dve, t + 1)
                sp.wait_ge(out_copied_act, t + 1)
                sp.dma_start(out[0, t * P:(t + 1) * P, :], xnat[:, t, :]).then_inc(out_stored, 16)
            sp.wait_ge(out_stored, 16 * TT)

        @block.gpsimd
        def _(pool):
            pool.memset(ident[:, :], 0.0).then_inc(pool_mask, 1)
            pool.memset(maskA[:, :], 0.0).then_inc(pool_mask, 1)
            pool.memset(cnt[:, 0, :], 1.0).then_inc(pool_mask, 1)
            pool.iota(delta[:, :], pattern=[[-1, S]], base=S - P, channel_multiplier=1)\
                .then_inc(pool_mask, 1)
            pool.wait_ge(pool_mask, 4)
            pool.affine_select(out=ident[:, :], in_=ident[:, :], compare_op=ALU.not_equal, fill=1.0,
                               base=0, pattern=[[-1, P]], channel_multiplier=1).then_inc(ident_ready, 1)
            diag = maskA[:, S - P:S]
            pool.affine_select(out=diag, in_=diag, compare_op=ALU.is_ge, fill=BIG,
                               base=0, pattern=[[-1, P]], channel_multiplier=1).then_inc(pool_mask, 1)
            pool.affine_select(out=cnt[:, 0, :], in_=cnt[:, 0, :], compare_op=ALU.is_ge, fill=0.0,
                               base=S - P, pattern=[[-1, S]], channel_multiplier=1)\
                .then_inc(pool_mask, 1)
            pool.wait_ge(pool_mask, 6)
            pool.affine_select(out=cnt[:, 0, :], in_=cnt[:, 0, :], compare_op=ALU.is_ge, fill=0.0,
                               base=P - (S - P), pattern=[[1, S]], channel_multiplier=-1)\
                .then_inc(pool_mask, 1)
            pool.wait_ge(setup_dve, SD_STRIDED)
            pool.affine_select(out=cnt[:, 1, :], in_=cnt[:, 1, :], compare_op=ALU.is_ge, fill=0.0,
                               base=S - P, pattern=[[-1, S]], channel_multiplier=1)\
                .then_inc(pool_mask, 1)
            pool.wait_ge(pool_mask, 8)
            pool.tensor_tensor(cnt[:, 0, :], cnt[:, 0, :], cnt[:, 1, :], ALU.add).then_inc(ada_step, 1)
            pool.wait_ge(ada_step, 1)
            pool.tensor_scalar(maskB[:, :], cnt[:, 0, :], 0.0, BIG, ALU.is_equal, ALU.mult)\
                .then_inc(pool_mask, 1)
            for m in (2, 3):
                pool.tensor_scalar(cnt[:, 1 + m, :], cnt[:, 0, :], float(m), -math.log(m),
                                   ALU.is_equal, ALU.mult).then_inc(pool_mask, 1)
            for m in (2, 3):
                pool.wait_ge(pool_mask, 9 + m)
                pool.tensor_tensor(maskB[:, :], maskB[:, :], cnt[:, 1 + m, :], ALU.add)\
                    .then_inc(pool_mask, 1)

            def ada_pair(l, i):
                f = i + (3 * l - 1)
                for b in range(2):
                    def load(k):
                        pool.dma_start(ada_raw[k % 2][:, :],
                                       w_ada[l, k * P:(k + 1) * P, bass.ds(i * (2 * D) + b * D, D)])\
                            .then_inc(ada_loaded[k % 2], 16)
                    scaled = f * (2 * KD) + b * KD
                    adds = f * ADA_ADDS + (b * (KD - 1) + 1)
                    pool.wait_ge(ada_step, adds)
                    for k in range(2):
                        load(k)
                    if b == 0:
                        pool.wait_ge(ada_summed, f + 1)
                    acc = ada_acc[:, b * D:(b + 1) * D]
                    for k in range(KD):
                        raw = ada_raw[k % 2][:, :]
                        pool.wait_ge(ada_loaded[k % 2], (f * KD + (b * (KD // 2) + k // 2 + 1)) * 16)
                        pool.nop(nofuse=True)
                        pool.tensor_tensor(raw if k else acc, raw,
                                           cond[:, k:k + 1].to_broadcast([P, D]), ALU.mult)\
                            .then_inc(ada_scaled, 1)
                        pool.wait_ge(ada_scaled, scaled + (k + 1))
                        if k:
                            pool.tensor_tensor(acc, acc, raw, ALU.add).then_inc(ada_step, 1)
                        if k + 2 < KD:
                            if k:
                                pool.wait_ge(ada_step, adds + k)
                            load(k + 2)

            pool.wait_ge(cond_ready, 1)
            with pool.Fori(1, 3) as i:
                ada_pair(0, i)
            with pool.Fori(0, 3) as i:
                ada_pair(1, i)

        @block.scalar
        def _(act):
            A = nc.scalar

            A.preload_act_table(ACT.Silu)
            act.wait_ge(setup_dve, SD_PAR0)
            A.activation(cond[:, :], par[:, 0, C_COND:C_COND + KD], ACT.Silu).then_inc(cond_ready, 1)
            act.wait_ge(setup_dve, SD_TRIG)
            A.activation(trig[:, :, :, :], trig_in[:, :, :, :], ACT.Sin).then_inc(setup_act, 1)
            A.preload_act_table_set("natural_log_exp_and_others")
            act.wait_ge(setup_dve, SD_LAM)
            A.activation(lam_s[:, 1, :], lam_s[:, 0, :], ACT.Exp).then_inc(setup_act, 1)

            def norm(L, which):
                N = L * 2 + which
                base = X_INIT + L * X_LAYER + which * KD - KD
                for m in range(KD):
                    act.wait_ge(x_done, base + m + 1)
                    if m >= 2:
                        act.wait_ge(mean_done, N * KD + m - 1)
                    A.activation(work[W_TILE + m % 2], xT[:, m, :], ACT.Square).then_inc(sq_done, 1)
                act.wait_ge(norm_dve, N * 3 + 1)
                A.activation(work[W_Y], work[W_V], ACT.Ln).then_inc(norm_act, 1)
                act.wait_ge(norm_act, N * 3 + 1)
                A.activation(work[W_Y], work[W_Y], ACT.Exp, scale=-0.5).then_inc(norm_act, 1)
                act.wait_ge(norm_act, N * 3 + 2)
                A.activation(work[W_YY], work[W_Y], ACT.Square).then_inc(norm_act, 1)
                shift = (SH_A, SH_F)[which] * KD
                for m in range(KD):
                    act.wait_ge(h_pre, N * KD + m + 1)
                    A.activation(h_hi[:, m, :], work[W_TILE + m % 2], ACT.Identity,
                                 bias=mod[:, shift + m:shift + m + 1]).then_inc(h_hi_done, 1)

            def nat_stats(L, g, t):
                Q = (L * 4 + qk_index(g)) * TT + t
                act.wait_ge(proj_done, (L * GROUPS + g) * TT + t + 1)
                if qk_index(g) * TT + t:
                    act.wait_ge(nat_dve, Q * 5)
                A.activation(work[W_SQ], bank[t][:, :], ACT.Square).then_inc(nat_act, 1)
                act.wait_ge(nat_dve, Q * 5 + 2)
                A.activation(small[:, 1, :], small[:, 0, :], ACT.Ln).then_inc(nat_act, 1)
                act.wait_ge(nat_act, Q * 3 + 2)
                A.activation(small[:, 2, :], small[:, 1, :], ACT.Exp, scale=-0.5).then_inc(nat_act, 1)

            def qk_evacuate(L, g, t):
                k = qk_index(g)
                act.wait_ge(nat_turned, (L * 4 + k) * TT + t + 1)
                act.nop(nofuse=True)
                A.activation(qkT[:, 4 * k:4 * k + 4, t * P:(t + 1) * P],
                             bank[6][:, :].rearrange("p (b n) -> p b n", n=P), ACT.Copy,
                             scale=gcol[:, bass.ds(L + LAYERS * k, 1)]).then_inc(qk_ready, 1)

            def v_copy(L, g, t):
                act.wait_ge(proj_done, (L * GROUPS + g) * TT + t + 1)
                A.activation(vnat[:, t, (g // 3) * GW:(g // 3 + 1) * GW], bank[t][:, :], ACT.Copy)\
                    .then_inc(v_ready, 1)

            def exps(L, task, n):
                W = (n + 1) * P
                for e in range(2):
                    r = row_of(task, n, e)
                    buf = prob(n, e)[:, 0:W]
                    act.wait_ge(score_done, L * ROWS + r + 1)
                    A.activation(buf, buf, ACT.Exp, bias=mneg[:, r:r + 1], scale=-1.0,
                                 accum_out=lsum[:, r:r + 1]).then_inc(exp_done, 1)

            def pT_copy(L, task, n):
                W = (n + 1) * P
                for i, _ in turn_units(task, n):
                    act.wait_ge(p_turned, L * T_ALL + i + 1)
                    if 1 <= i <= T_DIFF:
                        act.wait_ge(pv_done, L * T_ALL + i)
                    elif i:
                        act.wait_ge(pv_done, L * T_ALL + i - 1)
                    A.activation(turned(i)[:, 0:W], turn_bank(i)[:, 0:W], ACT.Copy)\
                        .then_inc(pT_ready, 1)

            def finish(L, task, stage):
                F = L * TASKS + task
                k = TT if is_diff(task) else 2 * TT
                if stage == 1:
                    act.wait_ge(fin_dve, F * 8 + 2)
                    A.activation(work[W_OSQ], normed(task), ACT.Square).then_inc(fin_act, 1)
                if stage == 2:
                    act.wait_ge(fin_dve, F * 8 + 4)
                    A.activation(fsmall[:, 1, 0:k], fsmall[:, 0, 0:k], ACT.Ln).then_inc(fin_act, 1)
                    act.wait_ge(fin_act, F * 3 + 2)
                    A.activation(fsmall[:, 2, 0:k], fsmall[:, 1, 0:k], ACT.Exp, scale=-0.5)\
                        .then_inc(fin_act, 1)
                if stage == 4:
                    act.wait_ge(o_turned, F + 1)
                    kind = G_SUB if is_diff(task) else G_OUT
                    act.nop(nofuse=True)
                    A.activation(h_hi[:, task, :], f_bank(task)[:, :], ACT.Copy,
                                 scale=gcol[:, bass.ds(L + LAYERS * kind, 1)]).then_inc(o_hi_done, 1)

            with act.Fori(0, LAYERS) as L:
                A.preload_act_table_set("natural_log_exp_and_others")
                slot_free(act, L, 0, 0)
                split_hi(L, 0, 0)
                norm(L, 0)
                for g in range(GROUPS):
                    for s in range(2):
                        if s == 0:
                            slot_free(act, L, g, 1)
                            split_hi(L, g, 1)
                        else:
                            slot_free(act, L, g + 1, 0)
                            split_hi(L, g + 1, 0)
                        for t in range(TT):
                            j = slot_of(g, s, t)
                            if has(j - 3):
                                pT_copy(L, *step(j - 3))
                            if has(j - 1):
                                exps(L, *step(j - 1))
                            for stage, lag in ((1, 7), (2, 8)):
                                if has_end(j - lag):
                                    finish(L, (j - lag) // TT, stage)
                            if turned_tile(g, s, t):
                                qk_evacuate(L, *turned_tile(g, s, t))
                            if s == 1 and g in QK_GROUPS:
                                nat_stats(L, g, t)
                            if s == 1 and g not in QK_GROUPS:
                                v_copy(L, g, t)
                slot_free(act, L, P_OUT, 1)
                split_hi(L, P_OUT, 1)

                exps(L, *step(T_DIFF))
                for k in range(T_DIFF, STEPS):
                    task, n = step(k)
                    if k + 1 < STEPS:
                        exps(L, *step(k + 1))
                    pT_copy(L, task, n)
                    if task == DIFF_TASKS:
                        finish(L, n, 4)
                    elif n >= 1:
                        finish(L, task - 1, n)
                    elif task > DIFF_TASKS + 1:
                        finish(L, task - 2, 4)
                finish(L, TASKS - 1, 1)
                finish(L, TASKS - 2, 4)
                finish(L, TASKS - 1, 2)
                finish(L, TASKS - 1, 4)

                for q in range(OUT_PAIRS):
                    if q:
                        slot_free(act, L, P_OUT + q, 1)
                        split_hi(L, P_OUT + q, 1)
                    slot_free(act, L, P_OUT + q + 1, 0)
                    split_hi(L, P_OUT + q + 1, 0)
                norm(L, 1)
                A.preload_act_table(ACT.Silu)

                for half, tiles in enumerate(FFN_SETS):
                    pairs = tiles // 2
                    with act.Fori(0, pairs) as i:
                        X = L * UP_LAYER + (i * 4 + UP_BASE[half])
                        Y = L * FT + (i * 2 + FF_BASE[half])
                        act.wait_ge(up_done, X + 1)
                        act.wait_ge(acc_done, L * X_LAYER + (half + 1) * KD + 1)
                        split_hi(L, i + P_UP[half], 1)
                        for part in range(2):
                            for q in range(2):
                                b = 2 * part + q
                                col = i * 2 + (part * FT + FF_BASE[half] + q)
                                act.wait_ge(act_lo_done, Y + 1)
                                act.wait_ge(up_done, X + b + 2)
                                act.nop(nofuse=True)
                                A.activation(work[b], bank[b][:, :], ACT.Identity,
                                             scale=par[:, L, bass.ds(col + C_W2, 1)],
                                             bias=par[:, L, bass.ds(col + C_B, 1)])\
                                    .then_inc(tap2_done, 1)
                            if part == 0:
                                for q in range(2):
                                    act.wait_ge(conv_done, X + 4 + q + 1)
                                    A.activation(work[4 + q], work[q], ACT.Silu)\
                                        .then_inc(silu_done, 1)
                                act.wait_ge(up_done, X + 3)
                                split_hi(L, i + (P_UP[half] + 1), 0)
                        for q in range(2):
                            act.wait_ge(prod_done, Y + q + 1)
                            act.nop(nofuse=True)
                            A.activation(act_hi[:, bass.ds(i * 2 + q, 1), :],
                                         work[2 + q].unsqueeze(1), ACT.Copy)\
                                .then_inc(act_hi_done, 1)
                    act.wait_ge(up_done, L * UP_LAYER + UP_BASE[half] + 2 * tiles + 1)
                    split_hi(L, P_DOWN[half], 1, D)

                    def split_down(i):
                        act.wait_ge(weights_used[0], L * USED0_LAYER + (i + (USED0_DOWN[half] + 1)))
                        split_hi(L, i + P_DOWN[half], 0, D)
                        act.wait_ge(weights_used[1], L * USED1_LAYER + (i + USED1_DOWN[half]))
                        split_hi(L, i + P_DOWN[half], 1, D)
                    with act.Fori(1, pairs) as i:
                        split_down(i)
                    if half == 0:
                        act.wait_ge(weights_used[0], L * USED0_LAYER + USED0_DOWN[half] + pairs + 1)
                        split_hi(L, P_UP[1], 0)

            for t in range(TT):
                act.wait_ge(out_turned, 2 * t + 2)
                A.activation(xnat[:, t, 512:D], bank[2 * t + 1][:, :], ACT.Copy)\
                    .then_inc(out_copied_act, 1)

        @block.tensor
        def _(pe):
            M = nc.tensor.matmul

            def three(dst, w, wsl, h, hsl, first, last):
                M(dst, w[0][wsl], h[0][hsl], start=first, stop=False)
                M(dst, w[1][wsl], h[0][hsl], start=False, stop=False)
                return M(dst, w[0][wsl], h[1][hsl], start=False, stop=last)

            pe.wait_ge(ident_ready, 1)
            pe.wait_ge(params_loaded, 16 * N_PARAM_LOADS)
            for l in range(LAYERS):
                at = 0
                for blk, k in ((0, 4 * FT), (1, 4 * FT), (2, 6 * KD + 3 * KD)):
                    last = nc.tensor.transpose(bank[l][:, at:at + k], prow[0:k, 3 * l + blk, :],
                                               ident[0:k, 0:k])
                    at += k
                last.then_inc(setup_pe, 1)
            nc.tensor.transpose(bank[2][:, 0:12], prow[0:12, 3 * LAYERS, :], ident[0:12, 0:12])\
                .then_inc(setup_pe, 1)
            for m in range(KD):
                b = bank[4 + m % 4]
                if m >= 4:
                    pe.wait_ge(x_done, m - 3)
                for t in range(TT):
                    if m == 0:
                        pe.wait_ge(x_loaded, 16 * TT)
                    last = nc.tensor.transpose(b[:, t * P:(t + 1) * P], xnat[:, t, m * P:(m + 1) * P],
                                               ident[:, :])
                last.then_inc(setup_pe, 1)
            pe.wait_ge(setup_dve, 2)
            for done in (weights_used[0], acc_done, up_done):
                M(bank[3][0:1, 0:1], ones[:, :], ones[:, :], start=True, stop=True).then_inc(done, 1)

            def norm_means(L, which):
                N = L * 2 + which
                for m in range(KD):
                    pe.wait_ge(sq_done, N * KD + m + 1)
                    M(bank[0][:, :], mean_w[:, :], work[W_TILE + m % 2], start=(m == 0),
                      stop=(m == KD - 1)).then_inc(mean_done, 1)

            def reduce_ada(L, i, b):
                if i == 0:
                    pe.wait_ge(first_summed, KD)
                pe.wait_ge(ada_step, (L * 3 + i) * ADA_ADDS + 1)
                for a in range(2):
                    for m in range(KD):
                        last = M(b[:, a * KD + m:a * KD + m + 1], ada_acc[:, a * D + m * P:a * D + (m + 1) * P],
                                 ones[:, :], start=True, stop=True)
                last.then_inc(ada_summed, 1)

            def turn_nat(L, g, t, j):
                k = qk_index(g)
                Q = (L * 4 + k) * TT + t
                pe.wait_ge(nat_ready, Q + 1)
                if k * TT + t:
                    pe.wait_ge(qk_ready, Q)
                if j >= 3:
                    pe.wait_ge(pT_ready, L * T_ALL + j - 2)
                for b in range(4):
                    last = nc.tensor.transpose(bank[6][:, b * P:(b + 1) * P],
                                               work[W_NAT + t % 2][:, b * P:(b + 1) * P], ident[:, :])
                last.then_inc(nat_turned, 1)

            def scores(L, task, n):
                W = (n + 1) * P
                for e in range(2):
                    r = row_of(task, n, e)
                    if is_diff(task):
                        if r >= 2:
                            pe.wait_ge(score_done, L * ROWS + r - 1)
                    elif r >= 2 * T_DIFF + 2:
                        pe.wait_ge(score_done, L * ROWS + r - 3)
                    base = 0 if is_diff(task) else 8
                    f = task if is_diff(task) else task - DIFF_TASKS
                    M(score_bank(task, n, e)[:, 0:W],
                      qkT[e * HEAD:(e + 1) * HEAD, base + f, n * P:(n + 1) * P],
                      qkT[e * HEAD:(e + 1) * HEAD, base + 4 + f, 0:W],
                      start=True, stop=True).then_inc(scores_mm, 1)

            def turn_p(L, task, n):
                for i, e in turn_units(task, n):
                    if is_diff(task):
                        pe.wait_ge(comb_done, (L * T_DIFF + i + 1) * 3)
                    else:
                        pe.wait_ge(exp_done, L * ROWS + row_of(task, n, e) + 1)
                    if 1 <= i < T_DIFF:
                        pe.wait_ge(pT_ready, L * T_ALL + i)
                    elif i:
                        pe.wait_ge(pT_ready, L * T_ALL + i - 1)
                    for b in range(n + 1):
                        last = nc.tensor.transpose(turn_bank(i)[:, b * P:(b + 1) * P],
                                                   prob(n, e)[:, b * P:(b + 1) * P], ident[:, :])
                    last.then_inc(p_turned, 1)

            def weigh_values(L, task, n):
                for i, e in turn_units(task, n):
                    pe.wait_ge(pT_ready, L * T_ALL + i + 1)
                    if n == 0 and e == 0 and task:
                        if is_diff(task):
                            pe.wait_ge(fin_dve, (L * TASKS + task - 1) * 8 + 2)
                        elif task > DIFF_TASKS:
                            pe.wait_ge(o_lo_done, L * TASKS + task - 1)
                    if is_diff(task):
                        dst, v0, w = n * P, task * P, P
                    else:
                        dst, v0, w = n * P + e * HEAD, GW + (task - DIFF_TASKS) * P + e * HEAD, HEAD
                    for b in range(n + 1):
                        last = M(out_bank(task)[:, dst:dst + w],
                                 turned(i)[:, b * P:(b + 1) * P], vnat[:, b, v0:v0 + w],
                                 start=(b == 0), stop=(b == n))
                    last.then_inc(pv_done, 1)

            def turn_o(L, task):
                pe.wait_ge(fin_dve, (L * TASKS + task + 1) * 8)
                if is_diff(task):
                    if task == 0:
                        pe.wait_ge(fin_dve, (L * TASKS + DIFF_TASKS) * 8)
                    else:
                        pe.wait_ge(o_lo_done, L * TASKS + task)
                for n in range(TT):
                    last = nc.tensor.transpose(f_bank(task)[:, n * P:(n + 1) * P],
                                               normed(task)[:, n * P:(n + 1) * P], ident[:, :])
                last.then_inc(o_turned, 1)

            with pe.Fori(0, LAYERS) as L:
                norm_means(L, 0)
                reduce_ada(L, 0, bank[7])
                def project(t, s, k):
                    kt = 4 * s + k
                    return three(bank[t][:, :], (h_hi, h_lo),
                                 (slice(None), kt, slice(t * P, (t + 1) * P)),
                                 (w_hi[s], w_lo[s]), (slice(None), slice(k * GW, (k + 1) * GW)),
                                 kt == 0, kt == KD - 1)

                for g in range(GROUPS):
                    for s in range(2):
                        pe.wait_ge(lo_ready[s], L * PAIRS + P_IN + g + 2)
                        if g == 0 and s == 0:
                            for k in range(4):
                                pe.wait_ge(h_lo_done, L * 2 * KD + k + 1)
                                for t in range(TT):
                                    last = project(t, s, k)
                            last.then_inc(weights_used[0], 1)
                            continue
                        for t in range(TT):
                            if s == 0:
                                if g - 1 in QK_GROUPS:
                                    pe.wait_ge(nat_mul, (L * 4 + qk_index(g - 1)) * TT + t + 1)
                                else:
                                    pe.wait_ge(v_ready, (L * 2 + (g - 1) // 3) * TT + t + 1)
                            for k in range(4):
                                if g == 0 and t == 0:
                                    pe.wait_ge(h_lo_done, L * 2 * KD + 4 + k + 1)
                                last = project(t, s, k)
                            if s == 1:
                                last.then_inc(proj_done, 1)
                            elif t == TT - 1:
                                last.then_inc(weights_used[0], 1)
                            j = slot_of(g, s, t)
                            tile = turned_tile(g, s, t)
                            if j == ADA_SLOT + 1:
                                pe.wait_ge(mod_ready, L * 3 + 2)
                            if tile:
                                turn_nat(L, *tile, j)
                            if j == 0:
                                pe.wait_ge(qk_ready, (L * 4 + 2) * TT)
                                pe.wait_ge(v_ready, (L * 2 + 1) * TT)
                            if has(j):
                                scores(L, *step(j))
                            if has(j - 3):
                                weigh_values(L, *step(j - 3))
                            if has(j - 2):
                                if tile:
                                    pe.wait_ge(qk_ready, (L * 4 + qk_index(tile[0])) * TT + tile[1] + 1)
                                turn_p(L, *step(j - 2))
                            if j == ADA_SLOT:
                                pe.wait_ge(pT_ready, L * T_ALL + j - 1)
                                reduce_ada(L, 1, bank[6])

                pe.wait_ge(qk_ready, (L + 1) * 4 * TT)
                pe.wait_ge(v_ready, (L * 2 + 1) * TT + 2)
                scores(L, *step(T_DIFF))
                for k in range(T_DIFF, STEPS):
                    task, n = step(k)
                    if k + 1 < STEPS:
                        scores(L, *step(k + 1))
                    if k == T_DIFF:
                        pe.wait_ge(v_ready, (L + 1) * 2 * TT)
                    turn_p(L, task, n)
                    if k > T_DIFF:
                        weigh_values(L, *step(k - 1))
                    if task == DIFF_TASKS:
                        turn_o(L, n)
                    elif n == 3:
                        turn_o(L, task - 1)
                weigh_values(L, TASKS - 1, TT - 1)

                for q in range(OUT_PAIRS):
                    for s in range(2):
                        pe.wait_ge(lo_ready[s], L * PAIRS + P_OUT + q + 2)
                        unit = 2 * q + s
                        for m in ((0, 1, 2, 4, 5, 6, 3, 7) if unit == 0 else range(KD)):
                            if unit == 0 and m == 0:
                                pe.wait_ge(o_lo_done, L * TASKS + 2)
                                pe.wait_ge(pT_ready, (L + 1) * T_ALL)
                            if unit == 0 and m == 3:
                                turn_o(L, TASKS - 1)
                                pe.wait_ge(o_lo_done, L * TASKS + TASKS - 1)
                            if unit == 0 and m == 7:
                                pe.wait_ge(o_lo_done, L * TASKS + TASKS)
                            for k in range(2):
                                kt = 2 * unit + k
                                last = three(bank[m][:, :], (w_hi[s], w_lo[s]),
                                             (slice(None), slice(k * D + m * P, k * D + (m + 1) * P)),
                                             (h_hi, h_lo), (slice(None), kt, slice(None)),
                                             kt == 0, kt == KD - 1)
                            if kt == KD - 1:
                                last.then_inc(acc_done, 1)
                        if unit < 2 * OUT_PAIRS - 1:
                            last.then_inc(weights_used[s], 1)
                norm_means(L, 1)
                pe.wait_ge(x_done, L * X_LAYER + (X_INIT + KD))
                reduce_ada(L, 2, bank[7])

                for half, tiles in enumerate(FFN_SETS):
                    pairs = tiles // 2
                    pe.wait_ge(x_done, L * X_LAYER + (X_INIT + half * KD + 4))
                    pe.nop(nofuse=True)
                    with pe.Fori(0, pairs) as i:
                        X = L * UP_LAYER + (i * 4 + UP_BASE[half])

                        def up(s, q, kt):
                            at = kt * 2 * P + q * P
                            return three(bank[2 * s + q][:, :], (w_hi[s], w_lo[s]),
                                         (slice(None), slice(at, at + P)),
                                         (h_hi, h_lo), (slice(None), kt, slice(None)),
                                         kt == 0, kt == KD - 1)

                        pe.wait_ge(lo_ready[0], L * PAIRS + (i + (P_UP[half] + 2)))
                        pe.wait_ge(conv_done, X + 2)
                        for kt in range(KD):
                            if half == 0:
                                pe.wait_ge(h_lo_done, (L * 2 + 1) * KD + kt + 1)
                            for q in range(2):
                                last = up(0, q, kt)
                                if kt == KD - 1:
                                    last.then_inc(up_done, 1)
                        pe.wait_ge(lo_ready[1], L * PAIRS + (i + (P_UP[half] + 2)))
                        for q in range(2):
                            pe.wait_ge(conv_done, X + q + 3)
                            for kt in range(KD):
                                last = up(1, q, kt)
                            last.then_inc(up_done, 1)

                    def down_pair(i, first, final):
                        for s in range(2):
                            pe.wait_ge(lo_ready[s], L * PAIRS + (i + (P_DOWN[half] + 2)))
                            pe.wait_ge(act_lo_done, L * FT + (i * 2 + (FF_BASE[half] + s + 2)))
                            rhs = (slice(None), bass.ds(i * 2 + s, 1), slice(None))
                            start = first and s == 0
                            stop = final and s == 1
                            for m in ((4, 5, 6, 7, 0, 1, 2, 3) if start else range(KD)):
                                if start and m == 4 and half:
                                    pe.wait_ge(x_done, L * X_LAYER + (X_INIT + 2 * KD))
                                if start and m == 0:
                                    pe.wait_ge(conv_done, L * UP_LAYER + UP_BASE[half] + 2 * tiles + 4)
                                last = three(bank[m][:, :].unsqueeze(1), (w_hi[s], w_lo[s]),
                                             (slice(None), slice(m * P, (m + 1) * P)),
                                             (act_hi, act_lo), rhs, start, stop)
                                if stop:
                                    last.then_inc(acc_done, 1)
                            if not stop:
                                last.then_inc(weights_used[s], 1)

                    down_pair(0, True, False)
                    with pe.Fori(1, pairs - 1) as i:
                        down_pair(i, False, False)
                    down_pair(pairs - 1, False, True)

            pe.wait_ge(x_done, X_INIT + LAYERS * X_LAYER)
            for t in range(TT):
                for f in range(2):
                    for m in range(4):
                        last = nc.tensor.transpose(bank[2 * t + f][:, m * P:(m + 1) * P],
                                                   xT[:, 4 * f + m, t * P:(t + 1) * P], ident[:, :])
                    last.then_inc(out_turned, 1)

        @block.vector
        def _(dve):
            V = nc.vector
            count = [0]

            def setup(ins):
                ins.then_inc(setup_dve, 1)
                count[0] += 1
                dve.wait_ge(setup_dve, count[0])
                return count[0]

            V.memset(prow[0:12, 3 * LAYERS, :], 1.0).then_inc(rows_set, 1)
            setup(V.memset(mean_w[:, :], 1.0 / D))
            setup(V.memset(ones[:, :], 1.0))
            for i, done in enumerate((*lo_ready, act_lo_done)):
                V.memset(small[:, i, :], 1.0).then_inc(done, 1)
            V.memset(small[:, 3, :], 1.0).then_inc(conv_done, 4)
            dve.wait_ge(pool_mask, 4)
            setup(V.tensor_scalar(rem[:, 0, :], delta[:, :], 3, None, ALU.bitwise_and))
            setup(V.tensor_scalar(rem[:, 1, :], delta[:, :], 15, None, ALU.bitwise_and))
            setup(V.tensor_scalar(cnt[:, 1, :], rem[:, 0, :], 0.0, None, ALU.is_equal))
            setup(V.tensor_scalar(cnt[:, 2, :], rem[:, 1, :], 0.0, None, ALU.is_equal))
            assert setup(V.tensor_tensor(cnt[:, 1, :], cnt[:, 1, :], cnt[:, 2, :], ALU.add)) == SD_STRIDED
            for l in range(LAYERS):
                dve.wait_ge(setup_pe, l + 1)
                last = setup(V.tensor_copy(par[:, l, :], bank[l][:, 0:PARAMS]))
                assert l or last == SD_PAR0
            dve.wait_ge(setup_pe, LAYERS + 1)
            setup(V.tensor_copy(gcol[:, :], bank[2][:, 0:12]))
            for l in range(LAYERS):
                k = G_SUB * LAYERS + l
                setup(V.tensor_scalar(gcol[:, k:k + 1], gcol[:, k:k + 1], 1.0 - lam_init(l), None,
                                      ALU.mult))
            for m in range(KD):
                dve.wait_ge(setup_pe, LAYERS + 2 + m)
                V.tensor_copy(xT[:, m, :], bank[4 + m % 4][:, :]).then_inc(x_done, 1)
            setup(V.tensor_copy(pos_f[:, :], pos_i[:, :]))
            inv_freq = np.float32(THETA) ** (-np.arange(0, ROPE, 2, dtype=np.float32) / np.float32(ROPE))
            for j in range(ROPE_HALF):
                setup(V.tensor_scalar(ang[:, :, j], pos_f[:, :], float(inv_freq[j]), None, ALU.mult))
            magic = 1.5 * 2 ** 23
            for scale in (2 ** 13, 1):
                setup(V.tensor_scalar(turns[:, :, :], ang[:, :, :], 1 / (2 * math.pi * scale), magic,
                                      ALU.mult, ALU.add))
                setup(V.tensor_scalar(turns[:, :, :], turns[:, :, :], -magic, None, ALU.add))
                for part in split_two_pi(scale):
                    setup(V.scalar_tensor_tensor(out=ang[:, :, :], in0=turns[:, :, :], scalar=-part,
                                                 in1=ang[:, :, :], op0=ALU.mult, op1=ALU.add))
            pi = 3.1415925
            setup(V.tensor_scalar(trig_in[:, 1, :, :], ang[:, :, :], pi, -pi, ALU.min, ALU.max))
            setup(V.scalar_tensor_tensor(out=turns[:, :, :], in0=trig_in[:, 1, :, :], scalar=-1.0,
                                         in1=trig_in[:, 1, :, :], op0=ALU.mult, op1=ALU.max))
            assert setup(V.tensor_scalar(trig_in[:, 0, :, :], turns[:, :, :], -1.0, math.pi / 2,
                                         ALU.mult, ALU.add)) == SD_TRIG
            dve.wait_ge(setup_act, 1)
            for half in range(2):
                sl = slice(half * ROPE_HALF, (half + 1) * ROPE_HALF)
                setup(V.tensor_copy(cos16[:, :, sl], trig[:, 0, :, :]))
                setup(V.tensor_scalar(sin16[:, :, sl], trig[:, 1, :, :], 1.0 if half else -1.0, None,
                                      ALU.mult))
                setup(V.tensor_copy(gswap[:, :, sl],
                                    gnat[:, :, (1 - half) * ROPE_HALF:(2 - half) * ROPE_HALF]))
            tall = [P, 4 * LAYERS, TT, ROPE]
            setup(V.tensor_tensor(ropeC[:, :, :, :], cos16[:, :, :].unsqueeze(1).to_broadcast(tall),
                                  gnat[:, :, :].unsqueeze(2).to_broadcast(tall), ALU.mult))
            setup(V.tensor_tensor(ropeS[:, :, :, :], sin16[:, :, :].unsqueeze(1).to_broadcast(tall),
                                  gswap[:, :, :].unsqueeze(2).to_broadcast(tall), ALU.mult))
            for i in range(2):
                setup(V.tensor_tensor(lamv[:, 2 * i, :, :], lamv[:, 2 * i, :, :],
                                      lamv[:, 2 * i + 1, :, :], ALU.mult))
                last = setup(V.tensor_reduce(lam_s[:, 0, 2 * i:2 * i + 2], lamv[:, 2 * i, :, :],
                                             AX.X, ALU.add))
            assert last == SD_LAM
            dve.wait_ge(setup_act, 2)
            for l in range(LAYERS):
                setup(V.tensor_tensor(neglam[:, l:l + 1], lam_s[:, 1, 2 + l:3 + l],
                                      lam_s[:, 1, l:l + 1], ALU.subtract))
                setup(V.tensor_scalar(neglam[:, l:l + 1], neglam[:, l:l + 1], -lam_init(l), None,
                                      ALU.add))
            dve.wait_ge(cond_ready, 1)
            for k in range(KD):
                dve.wait_ge(first_loaded[k % 2], 16 * (k // 2 + 1))
                if k == 0:
                    V.tensor_scalar(ada_acc[:, :], ada_first[0], cond[:, 0:1], None, ALU.mult)\
                        .then_inc(first_summed, 1)
                else:
                    dve.wait_ge(first_summed, k)
                    V.scalar_tensor_tensor(out=ada_acc[:, :], in0=ada_first[k % 2],
                                           scalar=cond[:, k:k + 1], in1=ada_acc[:, :],
                                           op0=ALU.mult, op1=ALU.add).then_inc(first_summed, 1)
            dve.wait_ge(pool_mask, 13)

            def take_mod(L, i, b):
                dve.wait_ge(ada_summed, L * 3 + i + 1)
                V.tensor_tensor(mod[:, 2 * i * KD:2 * (i + 1) * KD], b[:, 0:2 * KD],
                                par[:, L, C_ADA + 2 * i * KD:C_ADA + 2 * (i + 1) * KD], ALU.add)\
                    .then_inc(mod_ready, 1)

            def norm(L, which):
                N = L * 2 + which
                scale, gain = ((SC_A, C_GMIX), (SC_F, C_GFFN))[which]
                dve.wait_ge(mean_done, (N + 1) * KD)
                V.tensor_scalar(work[W_V], bank[0][:, :], EPS, None, ALU.add).then_inc(norm_dve, 1)
                take_mod(L, 2 * which, bank[7])
                dve.wait_ge(mod_ready, L * 3 + 1 + 2 * which)
                V.scalar_tensor_tensor(out=afac[:, :], in0=mod[:, scale * KD:(scale + 1) * KD],
                                       scalar=1.0, in1=par[:, L, gain:gain + KD],
                                       op0=ALU.add, op1=ALU.mult).then_inc(afac_done, 1)
                dve.wait_ge(afac_done, N * 2 + 1)
                V.tensor_scalar(afac[:, :], afac[:, :], -0.5, None, ALU.mult).then_inc(afac_done, 1)
                dve.wait_ge(norm_act, N * 3 + 3)
                V.tensor_tensor(work[W_YY], work[W_YY], work[W_V], ALU.mult).then_inc(norm_dve, 1)
                dve.wait_ge(norm_dve, N * 3 + 2)
                V.scalar_tensor_tensor(out=work[W_Y], in0=work[W_YY], scalar=-3.0,
                                       in1=work[W_Y], op0=ALU.add, op1=ALU.mult)\
                    .then_inc(norm_dve, 1)
                dve.wait_ge(norm_dve, N * 3 + 3)
                dve.wait_ge(afac_done, N * 2 + 2)
                shift = (SH_A, SH_F)[which] * KD

                def lo(m):
                    dve.wait_ge(h_hi_done, N * KD + m + 1)
                    V.scalar_tensor_tensor(out=h_lo[:, m, :], in0=work[W_TILE + m % 2],
                                           scalar=mod[:, shift + m:shift + m + 1],
                                           in1=h_hi[:, m, :], op0=ALU.add, op1=ALU.subtract)\
                        .then_inc(h_lo_done, 1)
                for m in range(KD):
                    if m >= 2:
                        dve.wait_ge(h_lo_done, N * KD + m - 1)
                    V.scalar_tensor_tensor(out=work[W_TILE + m % 2], in0=xT[:, m, :],
                                           scalar=afac[:, m:m + 1], in1=work[W_Y],
                                           op0=ALU.mult, op1=ALU.mult).then_inc(h_pre, 1)
                    if m:
                        lo(m - 1)
                lo(KD - 1)

            def newton(dst, y, v, tmp, done, base):
                V.tensor_tensor(tmp, y, y, ALU.mult).then_inc(done, 1)
                dve.wait_ge(done, base + 1)
                V.tensor_tensor(tmp, tmp, v, ALU.mult).then_inc(done, 1)
                dve.wait_ge(done, base + 2)
                V.scalar_tensor_tensor(out=dst, in0=tmp, scalar=-3.0, in1=y, op0=ALU.add,
                                       op1=ALU.mult).then_inc(done, 1)
                dve.wait_ge(done, base + 3)

            def nat(L, g, t):
                k = qk_index(g)
                Q = (L * 4 + k) * TT + t
                heads = [P, GH, HEAD]
                dve.wait_ge(nat_act, Q * 3 + 1)
                V.tensor_reduce(small[:, 3, :], work[W_SQ].rearrange("p (h d) -> p h d", d=HEAD),
                                AX.X, ALU.add).then_inc(nat_dve, 1)
                dve.wait_ge(nat_dve, Q * 5 + 1)
                V.tensor_scalar(small[:, 0, :], small[:, 3, :], 1.0 / HEAD, EPS, ALU.mult, ALU.add)\
                    .then_inc(nat_dve, 1)
                dve.wait_ge(nat_act, Q * 3 + 3)
                newton(small[:, 4, :], small[:, 2, :], small[:, 0, :], small[:, 5, :], nat_dve,
                       Q * 5 + 2)
                buf = work[W_NAT + t % 2]
                if k * TT + t >= 2:
                    dve.wait_ge(nat_turned, Q - 1)
                fac = -0.5 * (-HEAD ** -0.5 if g in (0, 3) else 1.0)
                V.scalar_tensor_tensor(out=buf.rearrange("p (h d) -> p h d", d=HEAD),
                                       in0=bank[t][:, :].rearrange("p (h d) -> p h d", d=HEAD),
                                       scalar=fac, in1=small[:, 4, :].unsqueeze(2).to_broadcast(heads),
                                       op0=ALU.mult, op1=ALU.mult).then_inc(nat_mul, 1)
                dve.wait_ge(nat_mul, Q + 1)
                head = buf.rearrange("p (h d) -> p h d", d=HEAD)[:, :, 0:ROPE]
                pair = head.rearrange("p h (a d) -> p h a d", a=2)
                own = work[W_ROPE][:, 0:GH * ROPE].rearrange("p (h d) -> p h d", d=ROPE)
                other = work[W_ROPE][:, GH * ROPE:2 * GH * ROPE].rearrange("p (h a d) -> p h a d", a=2,
                                                                      d=ROPE_HALF)
                table = bass.ds(L + LAYERS * k, 1)
                V.tensor_tensor(own, head, ropeC[:, table, t, :].to_broadcast([P, GH, ROPE]),
                                ALU.mult).then_inc(rope_dve, 1)
                V.tensor_tensor(other, pair[:, :, ::-1, :],
                                ropeS[:, table, t, :].rearrange("p o (a d) -> p o a d", a=2)
                                .to_broadcast([P, GH, 2, ROPE_HALF]), ALU.mult).then_inc(rope_dve, 1)
                dve.wait_ge(rope_dve, Q * 2 + 2)
                V.tensor_tensor(head, own, other.rearrange("p h a d -> p h (a d)"), ALU.add)\
                    .then_inc(nat_ready, 1)
                dve.wait_ge(nat_ready, Q + 1)

            def score_rows(L, task, n):
                W = (n + 1) * P
                mask = maskA if is_diff(task) else maskB
                for e in range(2):
                    r = row_of(task, n, e)
                    dve.wait_ge(scores_mm, L * ROWS + r + 1)
                    if task * TT + n >= 2:
                        last_unit = turn_units(*divmod(task * TT + n - 2, TT))[-1][0]
                        dve.wait_ge(p_turned, L * T_ALL + last_unit + 1)
                    dve.nop(nofuse=True)
                    V.tensor_tensor_reduce(prob(n, e)[:, 0:W], score_bank(task, n, e)[:, 0:W],
                                           mask[:, S - W:S],
                                           1.0, 3e38, ALU.add, ALU.min, mneg[:, r:r + 1])\
                        .then_inc(score_done, 1)

            def combine(L, task, n):
                W = (n + 1) * P
                i = task * TT + n
                B = (L * T_DIFF + i) * 3
                r = row_of(task, n, 0)
                c2 = comb[:, n % 2, :]
                dve.wait_ge(exp_done, L * ROWS + r + 2)
                V.reciprocal(c2[:, 0:1], lsum[:, r + 1:r + 2]).then_inc(comb_done, 1)
                dve.wait_ge(comb_done, B + 1)
                V.scalar_tensor_tensor(out=c2[:, 1:2], in0=lsum[:, r:r + 1], scalar=c2[:, 0:1],
                                       in1=neglam[:, bass.ds(L, 1)], op0=ALU.mult, op1=ALU.mult)\
                    .then_inc(comb_done, 1)
                dve.wait_ge(comb_done, B + 2)
                p1, p2 = (prob(n, e)[:, 0:W] for e in range(2))
                V.scalar_tensor_tensor(out=p1, in0=p2, scalar=c2[:, 1:2], in1=p1,
                                       op0=ALU.mult, op1=ALU.add).then_inc(comb_done, 1)

            def finish(L, task, stage):
                F = L * TASKS + task
                per = 1 if is_diff(task) else 2
                k = TT * per
                shape = [P, k, P // per]
                o = normed(task).rearrange("p (k d) -> p k d", k=k)
                if stage == 1:
                    dve.wait_ge(pv_done, L * T_ALL + turn_units(task, TT - 1)[-1][0] + 1)
                    r0 = row_of(task, 0, 0)
                    V.reciprocal(fsmall[:, 3, 0:k], lsum[:, r0:r0 + 8:2 // per]).then_inc(fin_dve, 1)
                    dve.wait_ge(fin_dve, F * 8 + 1)
                    if task >= DIFF_TASKS + 2:
                        dve.wait_ge(o_turned, F - 1)
                    V.tensor_tensor(o, out_bank(task)[:, :].rearrange("p (k d) -> p k d", k=k),
                                    fsmall[:, 3, 0:k].unsqueeze(2).to_broadcast(shape), ALU.mult)\
                        .then_inc(fin_dve, 1)
                if stage == 2:
                    dve.wait_ge(fin_act, F * 3 + 1)
                    V.tensor_reduce(fsmall[:, 5, 0:k], work[W_OSQ].rearrange("p (k d) -> p k d", k=k),
                                    AX.X, ALU.add).then_inc(fin_dve, 1)
                    dve.wait_ge(fin_dve, F * 8 + 3)
                    V.tensor_scalar(fsmall[:, 0, 0:k], fsmall[:, 5, 0:k], per / P, EPS, ALU.mult,
                                    ALU.add).then_inc(fin_dve, 1)
                if stage == 3:
                    dve.wait_ge(fin_act, F * 3 + 3)
                    newton(fsmall[:, 4, 0:k], fsmall[:, 2, 0:k], fsmall[:, 0, 0:k], fsmall[:, 5, 0:k],
                           fin_dve, F * 8 + 4)
                    V.scalar_tensor_tensor(out=o, in0=o, scalar=-0.5,
                                           in1=fsmall[:, 4, 0:k].unsqueeze(2).to_broadcast(shape),
                                           op0=ALU.mult, op1=ALU.mult).then_inc(fin_dve, 1)
                if stage == 4:
                    dve.wait_ge(o_hi_done, F + 1)
                    kind = G_SUB if is_diff(task) else G_OUT
                    V.scalar_tensor_tensor(out=h_lo[:, task, :], in0=f_bank(task)[:, :],
                                           scalar=gcol[:, bass.ds(L + LAYERS * kind, 1)],
                                           in1=h_hi[:, task, :], op0=ALU.mult, op1=ALU.subtract)\
                        .then_inc(o_lo_done, 1)

            def update_x(L, which, gate):
                for m in range(KD):
                    dve.wait_ge(acc_done, L * X_LAYER + which * KD + m + 2)
                    V.scalar_tensor_tensor(out=xT[:, m, :], in0=bank[m][:, :],
                                           scalar=mod[:, gate * KD + m:gate * KD + m + 1],
                                           in1=xT[:, m, :], op0=ALU.mult, op1=ALU.add)\
                        .then_inc(x_done, 1)

            with dve.Fori(0, LAYERS) as L:
                split_lo(L, 0, 0)
                norm(L, 0)
                for g in range(GROUPS):
                    for s in range(2):
                        split_lo(L, g + s, 1 - s)
                        for t in range(TT):
                            j = slot_of(g, s, t)
                            if j == ADA_SLOT + 1:
                                take_mod(L, 1, bank[6])
                            for stage, lag in ((1, 7), (2, 8), (3, 9)):
                                if has_end(j - lag):
                                    finish(L, (j - lag) // TT, stage)
                            if has(j - 2):
                                combine(L, *step(j - 2))
                            if has(j - 1):
                                score_rows(L, *step(j - 1))
                            if s == 1 and g in QK_GROUPS:
                                nat(L, g, t)
                split_lo(L, P_OUT, 1)

                score_rows(L, *step(T_DIFF))
                for k in range(T_DIFF, STEPS):
                    task, n = step(k)
                    if k + 1 < STEPS:
                        score_rows(L, *step(k + 1))
                    if task == DIFF_TASKS:
                        finish(L, n, 4)
                    elif n >= 1:
                        finish(L, task - 1, n)
                    elif task > DIFF_TASKS + 1:
                        finish(L, task - 2, 4)
                finish(L, TASKS - 1, 1)
                finish(L, TASKS - 2, 4)
                for stage in (2, 3, 4):
                    finish(L, TASKS - 1, stage)

                for q in range(OUT_PAIRS):
                    if q:
                        split_lo(L, P_OUT + q, 1)
                    split_lo(L, P_OUT + q + 1, 0)
                update_x(L, 0, GT_A)
                norm(L, 1)

                for half, tiles in enumerate(FFN_SETS):
                    pairs = tiles // 2
                    with dve.Fori(0, pairs) as i:
                        X = L * UP_LAYER + (i * 4 + UP_BASE[half])
                        Y = L * FT + (i * 2 + FF_BASE[half])
                        split_lo(L, i + P_UP[half], 1)
                        for part in range(2):
                            for q in range(2):
                                b = 2 * part + q
                                col = i * 2 + (part * FT + FF_BASE[half] + q)
                                dve.wait_ge(tap2_done, X + b + 1)
                                for tap, lag, done in ((C_W1, 1, tap1_done), (C_W0, 2, conv_done)):
                                    V.scalar_tensor_tensor(
                                        out=work[b][:, lag:S], in0=bank[b][:, 0:S - lag],
                                        scalar=par[:, L, bass.ds(col + tap, 1)],
                                        in1=work[b][:, lag:S], op0=ALU.mult, op1=ALU.add)\
                                        .then_inc(done, 1)
                                    if tap == C_W1:
                                        dve.wait_ge(tap1_done, X + b + 1)
                            if part == 0:
                                split_lo(L, i + (P_UP[half] + 1), 0)
                        for q in range(2):
                            dve.wait_ge(silu_done, Y + q + 1)
                            dve.wait_ge(conv_done, X + 6 + q + 1)
                            V.tensor_tensor(work[2 + q], work[2 + q], work[4 + q],
                                            ALU.mult).then_inc(prod_done, 1)
                        for q in range(2):
                            dve.wait_ge(act_hi_done, Y + q + 1)
                            V.tensor_tensor(act_lo[:, bass.ds(i * 2 + q, 1), :],
                                            work[2 + q].unsqueeze(1),
                                            act_hi[:, bass.ds(i * 2 + q, 1), :], ALU.subtract)\
                                .then_inc(act_lo_done, 1)
                    split_lo(L, P_DOWN[half], 1, D)
                    with dve.Fori(1, pairs) as i:
                        for s in range(2):
                            split_lo(L, i + P_DOWN[half], s, D)
                    if half == 0:
                        split_lo(L, P_UP[1], 0)
                    update_x(L, 1 + half, GT_F)

            for t in range(TT):
                dve.wait_ge(out_turned, 2 * t + 1)
                V.tensor_copy(xnat[:, t, 0:512], bank[2 * t][:, :]).then_inc(out_copied_dve, 1)


SD_STRIDED = 7
SD_PAR0 = SD_STRIDED + 1
SD_TRIG = SD_PAR0 + LAYERS - 1 + 1 + LAYERS + 1 + ROPE_HALF + 2 * 6 + 3
SD_LAM = SD_TRIG + 6 + 2 + 4
N_PARAM_LOADS = LAYERS * 8 + 4 * 3 + 8

_INS = ["x", "c", "positions", "g_mix", "g_ffn", "w_ada", "b_ada", "w_in", "w_out", "diff_q_g",
        "diff_k_g", "lam_q1", "lam_k1", "lam_q2", "lam_k2", "diff_subln_g", "dil_q_g", "dil_k_g",
        "dil_out_g", "w_up", "conv_w", "conv_b", "w_down"]


def kernel(**inputs):
    import concourse.bacc as bacc
    from concourse.bass_utils import run_bass_kernel_spmd

    nc = bacc.Bacc("TRN2", target_bir_lowering=False, num_devices=1)
    arrays, args = {}, []
    for name in _INS:
        a = np.ascontiguousarray(inputs[name])
        arrays[f"in_{name}"] = a
        args.append(nc.dram_tensor(f"in_{name}", a.shape, mybir.dt.from_np(a.dtype),
                                   kind="ExternalInput").ap())
    args.append(nc.dram_tensor("out_x", (1, S, D), F32, kind="ExternalOutput").ap())
    trunk_kernel(nc, *args)
    r = run_bass_kernel_spmd(nc, [arrays], core_ids=[0])
    return r.results[0]["out_x"]
```

```python
import math
from contextlib import ExitStack

import numpy as np

import concourse.bass as bass
from concourse import mybir

F32 = mybir.dt.float32
F32R = mybir.dt.float32r
I32 = mybir.dt.int32
ALU = mybir.AluOpType
ACT = mybir.ActivationFunctionType
AX = mybir.AxisListType

P = 128
LAYERS = 2
D = 1024
S = 512
HEAD = 64
D_FF = 2816
ROPE = HEAD // 4
ROPE_HALF = ROPE // 2
THETA = 500000.0
EPS = 1e-6
BIG = 1e30

KD = D // P
TT = S // P
GROUPS = 6
GW = 512
GH = GW // HEAD
FT = D_FF // P
FFN_SETS = (12, 10)
ACT_SLOTS = max(FFN_SETS)
TASKS = 8
DIFF_TASKS = 4
STEPS = TASKS * TT
ROWS = 2 * STEPS
T_DIFF = DIFF_TASKS * TT
T_ALL = T_DIFF + 2 * (TASKS - DIFF_TASKS) * TT
SLOT = 2048

P_IN = 0
P_OUT = P_IN + GROUPS
OUT_PAIRS = 2
P_UP, P_DOWN = [], []
_p = P_OUT + OUT_PAIRS
for _n in FFN_SETS:
    P_UP.append(_p)
    P_DOWN.append(_p + _n // 2)
    _p += _n
PAIRS = _p

USED0_LAYER = GROUPS + OUT_PAIRS + FT // 2
USED1_LAYER = (OUT_PAIRS - 1) + sum(n // 2 - 1 for n in FFN_SETS)
USED0_OUT = GROUPS
USED1_OUT = 0
USED0_DOWN = [GROUPS + OUT_PAIRS, GROUPS + OUT_PAIRS + FFN_SETS[0] // 2]
USED1_DOWN = [OUT_PAIRS - 1, OUT_PAIRS - 1 + FFN_SETS[0] // 2 - 1]

UP_LAYER = 2 * FT
UP_BASE = [0, 2 * FFN_SETS[0]]
FF_BASE = [0, FFN_SETS[0]]
X_LAYER = 3 * KD
X_INIT = KD

FIRST_SLOTS = 6
ADA_ADDS = 2 * (KD - 1)

SLABS = 15
W_SQ, W_NAT, W_ROPE, W_PROB, W_TURNED, W_OSQ, W_OUT = 0, 1, 3, 4, 8, 9, 10
W_NATS = (1, 2, 14)
W_PROB_B = ((4, 5), (6, 7), (0, 14))
W_TILE, W_V, W_Y, W_YY = 8, 10, 11, 12
SQUARES = 6
SPLIT_AFTER = 6

A_COUNTS = (1, 1, 1, 1, 0, 1, 0, 1, 1, 1, 1, 1, 0, 1, 0, 1, 1, 1, 1, 1, 2, 2, 1, 1)
A_TIMES, _a = [], 0
for _n in A_COUNTS:
    A_TIMES.append(range(_a, _a + _n))
    _a += _n
assert _a == T_DIFF + 6
_at = [_j for _j, _t in enumerate(A_TIMES) for _ in _t]
_early = [min(_j, _at[_i - 1] + 1) if _i else _j for _i, _j in enumerate(_at)]
EARLY_TIMES = [[_i for _i, _e in enumerate(_early) if _e == _j] for _j in range(len(A_TIMES))]
ADA_AT = {1: (1, ((0, 7), (1, 6))), 2: (1, ((2, 7), (3, 6))),
          21: (2, ((0, 4), (1, 5))), 22: (2, ((2, 6),)), 23: (2, ((3, 4),))}
ADA_BANKS = 4

C_W0, C_W1, C_W2, C_B = (i * 2 * FT for i in range(4))
C_ADA = 8 * FT
C_GMIX = C_ADA + 6 * KD
C_GFFN = C_GMIX + KD
C_COND = C_GFFN + KD
PARAMS = C_COND + KD
SH_A, SC_A, GT_A, SH_F, SC_F, GT_F = range(6)
G_DQ, G_DK, G_LQ, G_LK, G_SUB, G_OUT = range(6)


def lam_init(layer):
    return 0.8 - 0.6 * math.exp(-0.3 * layer)


def split_two_pi(scale):
    rest, parts = 2 * math.pi * scale, []
    for _ in range(3):
        ulp = 2.0 ** (math.floor(math.log2(rest)) - 7)
        part = math.floor(rest / ulp) * ulp
        parts.append(part)
        rest -= part
    return parts + [float(np.float32(rest))]


def trunk_kernel(nc, x, c, positions, g_mix, g_ffn, w_ada, b_ada, w_in, w_out, diff_q_g, diff_k_g,
                 lam_q1, lam_k1, lam_q2, lam_k2, diff_subln_g, dil_q_g, dil_k_g, dil_out_g,
                 w_up, conv_w, conv_b, w_down, out):
    ctx = ExitStack()
    with ctx:
        def sb(name, shape, dt=F32):
            return ctx.enter_context(nc.sbuf_tensor(name, shape, dt))

        def sem(name):
            return ctx.enter_context(nc.semaphore(name))

        xT = sb("xT", [P, KD, S])
        with ExitStack() as inner:
            ada_first = [inner.enter_context(nc.sbuf_tensor(f"ada_first{i}", [P, 2 * D], F32))
                         for i in range(4)]
        h_hi = sb("h_hi", [P, KD, S], F32R)
        h_lo = sb("h_lo", [P, KD, S], F32R)
        w_raw = [sb(f"w_raw{s}", [P, SLOT]) for s in range(2)]
        w_hi = [sb(f"w_hi{s}", [P, SLOT], F32R) for s in range(2)]
        w_lo = [sb(f"w_lo{s}", [P, SLOT], F32R) for s in range(2)]
        ada_raw = [sb(f"ada_raw{i}", [P, D]) for i in range(2)]
        ada_acc = sb("ada_acc", [P, 2 * D])
        scratch = sb("scratch", [P, SLABS, S])
        work = [scratch[:, i, :] for i in range(SLABS)]
        ada_first += [scratch[:, 4 * i:4 * i + 4, :].rearrange("p a n -> p (a n)") for i in range(2)]
        maskA = sb("maskA", [P, S])
        maskB = sb("maskB", [P, S])
        ident = sb("ident", [P, P])
        mean_w = sb("mean_w", [P, P])
        ones = sb("ones", [P, 1])
        par = sb("par", [P, LAYERS, PARAMS])
        gcol = sb("gcol", [P, 6 * LAYERS])
        mod = sb("mod", [P, 6 * KD])
        mod_sum = sb("mod_sum", [P, 2 * KD])
        cond = sb("cond", [P, KD])
        afac = sb("afac", [P, KD])
        neglam = sb("neglam", [P, LAYERS])
        ropeC = sb("ropeC", [P, 4 * LAYERS, TT, ROPE])
        ropeS = sb("ropeS", [P, 4 * LAYERS, TT, ROPE])
        small = sb("small", [P, 6, GH])
        fsmall = sb("fsmall", [P, 6, GH])
        mneg = sb("mneg", [P, ROWS])
        lsum = sb("lsum", [P, ROWS])
        comb = sb("comb", [P, 2, 2])
        with ExitStack() as inner:
            qkT = inner.enter_context(nc.sbuf_tensor("qkT", [P, 16, S], F32))
            vnat = inner.enter_context(nc.sbuf_tensor("vnat", [P, TT, 2 * GW], F32))
        with ExitStack() as inner:
            act_hi = inner.enter_context(nc.sbuf_tensor("act_hi", [P, ACT_SLOTS, S], F32R))
            act_lo = inner.enter_context(nc.sbuf_tensor("act_lo", [P, ACT_SLOTS, S], F32R))
        with ExitStack() as inner:
            xnat = inner.enter_context(nc.sbuf_tensor("xnat", [P, TT, D], F32))
            prow = inner.enter_context(nc.sbuf_tensor("prow", [P, 3 * LAYERS + 1, P], F32))
            lamv = inner.enter_context(nc.sbuf_tensor("lamv", [P, 4, LAYERS, HEAD], F32))
            gnat = inner.enter_context(nc.sbuf_tensor("gnat", [P, 4 * LAYERS, ROPE], F32))
            gswap = inner.enter_context(nc.sbuf_tensor("gswap", [P, 4 * LAYERS, ROPE], F32))
            pos_i = inner.enter_context(nc.sbuf_tensor("pos_i", [P, TT], I32))
            pos_f = inner.enter_context(nc.sbuf_tensor("pos_f", [P, TT], F32))
            ang = inner.enter_context(nc.sbuf_tensor("ang", [P, TT, ROPE_HALF], F32))
            turns = inner.enter_context(nc.sbuf_tensor("turns", [P, TT, ROPE_HALF], F32))
            trig_in = inner.enter_context(nc.sbuf_tensor("trig_in", [P, 2, TT, ROPE_HALF], F32))
            trig = inner.enter_context(nc.sbuf_tensor("trig", [P, 2, TT, ROPE_HALF], F32))
            cos16 = inner.enter_context(nc.sbuf_tensor("cos16", [P, TT, ROPE], F32))
            sin16 = inner.enter_context(nc.sbuf_tensor("sin16", [P, TT, ROPE], F32))
            delta = inner.enter_context(nc.sbuf_tensor("delta", [P, S], I32))
            rem = inner.enter_context(nc.sbuf_tensor("rem", [P, 2, S], I32))
            cnt = inner.enter_context(nc.sbuf_tensor("cnt", [P, 5, S], F32))
            lam_s = inner.enter_context(nc.sbuf_tensor("lam_s", [P, 3, 4], F32))

        bank = [ctx.enter_context(nc.psum_tensor(f"bank{i}", [P, 512], F32)) for i in range(8)]

        rows_loaded = [sem(f"rows_loaded{l}") for l in range(LAYERS)]
        gains_loaded = sem("gains_loaded")
        pos_loaded = sem("pos_loaded")
        angle_done = sem("angle_done")
        x_loaded = sem("x_loaded")
        rows_set = sem("rows_set")
        ident_ready = sem("ident_ready")
        pool_mask = sem("pool_mask")
        setup_dve = sem("setup_dve")
        setup_act = sem("setup_act")
        setup_pe = sem("setup_pe")
        cond_ready = sem("cond_ready")
        raw_loaded = [sem(f"raw_loaded{s}") for s in range(2)]
        hi_ready = [sem(f"hi_ready{s}") for s in range(2)]
        lo_ready = [sem(f"lo_ready{s}") for s in range(2)]
        weights_used = [sem(f"weights_used{s}") for s in range(2)]
        ada_loaded = [sem(f"ada_loaded{i}") for i in range(2)]
        first_loaded = [sem(f"first_loaded{k}") for k in range(FIRST_SLOTS)]
        first_summed = sem("first_summed")
        ada_scaled = sem("ada_scaled")
        ada_step = sem("ada_step")
        ada_turned = sem("ada_turned")
        ada_reduced = sem("ada_reduced")
        mod_ready = sem("mod_ready")
        x_done = sem("x_done")
        sq_done = sem("sq_done")
        pair_done = sem("pair_done")
        mean_done = sem("mean_done")
        norm_dve = sem("norm_dve")
        norm_act = sem("norm_act")
        afac_done = sem("afac_done")
        h_pre = sem("h_pre")
        h_hi_done = sem("h_hi_done")
        h_lo_done = sem("h_lo_done")
        proj_done = sem("proj_done")
        nat_act = sem("nat_act")
        nat_dve = sem("nat_dve")
        rope_dve = sem("rope_dve")
        nat_mul = sem("nat_mul")
        nat_ready = sem("nat_ready")
        nat_turned = sem("nat_turned")
        qk_ready = sem("qk_ready")
        v_ready = sem("v_ready")
        scores_mm = sem("scores_mm")
        score_done = sem("score_done")
        exp_done = sem("exp_done")
        comb_done = sem("comb_done")
        p_turned = sem("p_turned")
        pT_ready = sem("pT_ready")
        pv_done = sem("pv_done")
        fin_dve = sem("fin_dve")
        fin_act = sem("fin_act")
        o_turned = sem("o_turned")
        o_hi_done = sem("o_hi_done")
        o_lo_done = sem("o_lo_done")
        acc_done = sem("acc_done")
        up_done = sem("up_done")
        tap2_done = sem("tap2_done")
        tap1_done = sem("tap1_done")
        conv_done = sem("conv_done")
        silu_done = sem("silu_done")
        prod_done = sem("prod_done")
        act_hi_done = sem("act_hi_done")
        act_lo_done = sem("act_lo_done")
        out_turned = sem("out_turned")
        out_copied_dve = sem("out_copied_dve")
        out_copied_act = sem("out_copied_act")
        out_stored = sem("out_stored")

        def is_diff(task):
            return task < DIFF_TASKS

        def turn_units(task, n):
            if is_diff(task):
                return [(task * TT + n, 0)]
            base = T_DIFF + (task - DIFF_TASKS) * 2 * TT + 2 * n
            return [(base, 0), (base + 1, 1)]

        def score_bank(task, n, e):
            return bank[4 + e] if is_diff(task) or n % 2 else bank[e]

        def turn_bank(i):
            return bank[6] if i < T_DIFF or i % 2 else bank[2]

        def out_bank(task):
            return bank[7] if is_diff(task) or task % 2 else bank[3]

        def prob(k, e):
            return work[(W_PROB + k % 2 * 2 + e) if k < T_DIFF else W_PROB_B[k % 3][e]]

        def turned(i):
            return work[W_TURNED if i < T_DIFF or i % 2 == 0 else W_NAT]

        def normed(task):
            return work[W_OUT + task] if is_diff(task) else work[W_NAT + 1 + task % 2]

        def f_bank(task):
            return bank[7] if is_diff(task) else out_bank(task)

        def row_of(task, n, e):
            return task * 8 + 2 * n + e

        QK_GROUPS = [0, 1, 3, 4]

        def qk_index(g):
            return QK_GROUPS.index(g)

        def slot_of(g, s, t):
            return (g - 3) * 2 * TT + s * TT + t

        def a_times(g, s, t):
            return A_TIMES[slot_of(g, s, t)] if g >= 3 else ()

        def early_times(g, s, t):
            return EARLY_TIMES[slot_of(g, s, t)] if g >= 3 else ()

        def means_before(L, which):
            return L * (KD + KD // 2) + which * KD

        def mean_count(which, m):
            return m // 2 + 1 if which else m + 1

        def turned_tile(g, s, t):
            g, t = (g, 0) if s == 1 and t == 3 else (g - 1, t + 1) if s == 0 and t < 3 else (-1, 0)
            return (g, t) if g in QK_GROUPS else None

        def normed_tile(g, s, t):
            g, t = (g, t - 1) if s == 1 and t >= 1 else (g - 1, TT - 1) if s == 0 and t == 0 else (-1, 0)
            return (g, t) if g in QK_GROUPS else None

        def has(a):
            return 0 <= a < T_DIFF

        def has_end(a):
            return has(a) and a % TT == 0

        def step(a):
            return divmod(a, TT)

        def slot_free(eng, L, p, s):
            if p == 0:
                eng.wait_ge(weights_used[0], L * USED0_LAYER + 1)
                if s == 1:
                    eng.wait_ge(acc_done, L * X_LAYER + 1)
                return
            q = p - 1
            if q < P_OUT:
                if s == 0:
                    eng.wait_ge(weights_used[0], L * USED0_LAYER + q + 2)
                else:
                    eng.wait_ge(proj_done, (L * GROUPS + q + 1) * TT)
                return
            if q < P_OUT + OUT_PAIRS:
                if s == 0:
                    eng.wait_ge(weights_used[0], L * USED0_LAYER + USED0_OUT + q - P_OUT + 2)
                elif q == P_OUT + OUT_PAIRS - 1:
                    eng.wait_ge(acc_done, L * X_LAYER + KD + 1)
                else:
                    eng.wait_ge(weights_used[1], L * USED1_LAYER + USED1_OUT + q - P_OUT + 1)
                return
            raise AssertionError("pairs of the feed-forward loops have waits of their own")

        def split_hi(L, p, s, width=SLOT):
            nc.scalar.wait_ge(raw_loaded[s], (L * PAIRS + p + 1) * 16)
            for half in range(2):
                cols = slice(half * width // 2, (half + 1) * width // 2)
                nc.scalar.activation(w_hi[s][:, cols], w_raw[s][:, cols], ACT.Copy)\
                    .then_inc(hi_ready[s], 1)

        def split_lo(L, p, s, width=SLOT):
            for half in range(2):
                cols = slice(half * width // 2, (half + 1) * width // 2)
                nc.vector.wait_ge(hi_ready[s], (L * PAIRS + p) * 2 + (half + 1))
                last = nc.vector.tensor_tensor(w_lo[s][:, cols], w_raw[s][:, cols],
                                               w_hi[s][:, cols], ALU.subtract)
            last.then_inc(lo_ready[s], 1)

        block = ctx.enter_context(nc.Block())

        @block.sync
        def _(sp):
            with nc.allow_non_contiguous_dma(reason="512 positions, one a partition and tile"):
                sp.dma_start(pos_i[:, :], positions[0].rearrange("(t p) -> p t", p=P))\
                    .then_inc(pos_loaded, 16)
            for t in range(TT):
                sp.dma_start(xnat[:, t, :], x[0, t * P:(t + 1) * P, :]).then_inc(x_loaded, 16)
            def load_rows(l):
                rows = [(0, 0, conv_w[l, 0], 2 * FT), (0, 2 * FT, conv_w[l, 1], 2 * FT),
                        (1, 0, conv_w[l, 2], 2 * FT), (1, 2 * FT, conv_b[l], 2 * FT),
                        (2, 0, b_ada[l], 6 * KD), (2, 6 * KD, g_mix[l], KD),
                        (2, 7 * KD, g_ffn[l], KD), (2, 8 * KD, c[0], KD)]
                assert len(rows) == N_ROW_LOADS
                for blk, r0, src, k in rows:
                    sp.dma_start(prow[r0:r0 + k, 3 * l + blk, :],
                                 src.rearrange("(r q) -> r q", q=P)).then_inc(rows_loaded[l], 16)
            load_rows(0)
            def load_first(k):
                sp.dma_start(ada_first[k % FIRST_SLOTS][:, :], w_ada[0, k * P:(k + 1) * P, 0:2 * D])\
                    .then_inc(first_loaded[k % FIRST_SLOTS], 16)
            for k in range(4):
                load_first(k)
            for l in range(1, LAYERS):
                load_rows(l)
            n = 0
            sp.wait_ge(rows_set, 1)
            G = 3 * LAYERS
            for k, g in enumerate((diff_q_g, diff_k_g, dil_q_g, dil_k_g)):
                for half in range(2):
                    sp.dma_start(prow[2 * k:2 * k + 2, G, half * HEAD + ROPE:(half + 1) * HEAD],
                                 g[:, ROPE:HEAD]).then_inc(gains_loaded, 16)
                    n += 1
                sp.dma_start(gnat[:, 2 * k:2 * k + 2, :],
                             g[:, 0:ROPE].partition_broadcast(P)).then_inc(gains_loaded, 16)
                n += 1
            sp.dma_start(prow[2 * G_SUB:2 * G_SUB + 2, G, :], diff_subln_g).then_inc(gains_loaded, 16)
            for half in range(2):
                sp.dma_start(prow[2 * G_OUT:2 * G_OUT + 2, G, half * HEAD:(half + 1) * HEAD],
                             dil_out_g).then_inc(gains_loaded, 16)
            for i, v in enumerate((lam_q1, lam_k1, lam_q2, lam_k2)):
                sp.dma_start(lamv[:, i, :, :], v.partition_broadcast(P)).then_inc(gains_loaded, 16)
            assert n + 7 == N_GAIN_LOADS
            for k in range(4, KD):
                if k >= FIRST_SLOTS:
                    sp.wait_ge(first_summed, k - FIRST_SLOTS + 1)
                load_first(k)

            def load(L, p, s, dst, src):
                sp.wait_ge(lo_ready[s], L * PAIRS + p + 1)
                sp.dma_start(dst, src).then_inc(raw_loaded[s], 16)

            with sp.Fori(0, LAYERS) as L:
                for g in range(GROUPS):
                    for s in range(2):
                        load(L, P_IN + g, s, w_raw[s][:, :].rearrange("p (k n) -> p k n", n=GW),
                             w_in[L, s * 512:(s + 1) * 512, g * GW:(g + 1) * GW]
                             .rearrange("(k p) n -> p k n", p=P))
                for q in range(OUT_PAIRS):
                    for s in range(2):
                        r0 = (2 * q + s) * 2 * P
                        load(L, P_OUT + q, s, w_raw[s][:, :].rearrange("p (k n) -> p k n", n=D),
                             w_out[L, r0:r0 + 2 * P, :].rearrange("(k p) n -> p k n", p=P))
                for half, tiles in enumerate(FFN_SETS):
                    with sp.Fori(0, tiles // 2) as i:
                        for s in range(2):
                            col = i * (2 * P) + (s * D_FF + FF_BASE[half] * P)
                            load(L, P_UP[half] + i, s,
                                 w_raw[s][:, :].rearrange("p (k n) -> p k n", n=2 * P),
                                 w_up[L, :, bass.ds(col, 2 * P)].rearrange("(k p) n -> p k n", p=P))
                    with sp.Fori(0, tiles // 2) as i:
                        for s in range(2):
                            row = i * (2 * P) + (s * P + FF_BASE[half] * P)
                            load(L, P_DOWN[half] + i, s, w_raw[s][:, 0:D],
                                 w_down[L, bass.ds(row, P), :])
            for t in range(TT):
                sp.wait_ge(out_copied_dve, t + 1)
                sp.wait_ge(out_copied_act, t + 1)
                sp.dma_start(out[0, t * P:(t + 1) * P, :], xnat[:, t, :]).then_inc(out_stored, 16)
            sp.wait_ge(out_stored, 16 * TT)

        @block.gpsimd
        def _(pool):
            pool.memset(ident[:, :], 0.0).then_inc(pool_mask, 1)
            pool.memset(maskA[:, :], 0.0).then_inc(pool_mask, 1)
            pool.memset(cnt[:, 0, :], 1.0).then_inc(pool_mask, 1)
            pool.iota(delta[:, :], pattern=[[-1, S]], base=S - P, channel_multiplier=1)\
                .then_inc(pool_mask, 1)
            pool.wait_ge(pool_mask, 4)
            pool.affine_select(out=ident[:, :], in_=ident[:, :], compare_op=ALU.not_equal, fill=1.0,
                               base=0, pattern=[[-1, P]], channel_multiplier=1).then_inc(ident_ready, 1)
            diag = maskA[:, S - P:S]
            pool.affine_select(out=diag, in_=diag, compare_op=ALU.is_ge, fill=BIG,
                               base=0, pattern=[[-1, P]], channel_multiplier=1).then_inc(pool_mask, 1)
            pool.affine_select(out=cnt[:, 0, :], in_=cnt[:, 0, :], compare_op=ALU.is_ge, fill=0.0,
                               base=S - P, pattern=[[-1, S]], channel_multiplier=1)\
                .then_inc(pool_mask, 1)
            pool.wait_ge(pool_mask, 6)
            pool.affine_select(out=cnt[:, 0, :], in_=cnt[:, 0, :], compare_op=ALU.is_ge, fill=0.0,
                               base=P - (S - P), pattern=[[1, S]], channel_multiplier=-1)\
                .then_inc(pool_mask, 1)
            count = [0]

            def angle(ins):
                ins.then_inc(angle_done, 1)
                count[0] += 1
                pool.wait_ge(angle_done, count[0])
                return count[0]

            pool.wait_ge(pos_loaded, 16)
            angle(pool.tensor_copy(pos_f[:, :], pos_i[:, :]))
            inv_freq = np.float32(THETA) ** (-np.arange(0, ROPE, 2, dtype=np.float32) / np.float32(ROPE))
            for j in range(ROPE_HALF):
                angle(pool.tensor_scalar(ang[:, :, j], pos_f[:, :], float(inv_freq[j]), None, ALU.mult))
            magic = 1.5 * 2 ** 23
            for scale in (2 ** 13, 1):
                angle(pool.tensor_scalar(turns[:, :, :], ang[:, :, :], 1 / (2 * math.pi * scale), magic,
                                         ALU.mult, ALU.add))
                angle(pool.tensor_scalar(turns[:, :, :], turns[:, :, :], -magic, None, ALU.add))
                for part in split_two_pi(scale):
                    angle(pool.tensor_scalar(trig_in[:, 0, :, :], turns[:, :, :], -part, None, ALU.mult))
                    angle(pool.tensor_tensor(ang[:, :, :], ang[:, :, :], trig_in[:, 0, :, :], ALU.add))
            pi = 3.1415925
            angle(pool.tensor_scalar(trig_in[:, 1, :, :], ang[:, :, :], pi, -pi, ALU.min, ALU.max))
            angle(pool.tensor_scalar(turns[:, :, :], trig_in[:, 1, :, :], math.pi / 2, -2 * math.pi,
                                     ALU.is_gt, ALU.mult))
            angle(pool.tensor_scalar(trig_in[:, 0, :, :], trig_in[:, 1, :, :], math.pi / 2, None,
                                     ALU.add))
            angle(pool.tensor_tensor(trig_in[:, 0, :, :], trig_in[:, 0, :, :], turns[:, :, :], ALU.add))
            assert angle(pool.tensor_scalar(trig_in[:, 0, :, :], trig_in[:, 0, :, :], pi, -pi,
                                            ALU.min, ALU.max)) == ANGLES

            pool.wait_ge(setup_dve, SD_STRIDED)
            pool.affine_select(out=cnt[:, 1, :], in_=cnt[:, 1, :], compare_op=ALU.is_ge, fill=0.0,
                               base=S - P, pattern=[[-1, S]], channel_multiplier=1)\
                .then_inc(pool_mask, 1)
            pool.wait_ge(pool_mask, 8)
            pool.tensor_tensor(cnt[:, 0, :], cnt[:, 0, :], cnt[:, 1, :], ALU.add).then_inc(ada_step, 1)
            pool.wait_ge(ada_step, 1)
            pool.tensor_scalar(maskB[:, :], cnt[:, 0, :], 0.0, BIG, ALU.is_equal, ALU.mult)\
                .then_inc(pool_mask, 1)
            for m in (2, 3):
                pool.tensor_scalar(cnt[:, 1 + m, :], cnt[:, 0, :], float(m), -math.log(m),
                                   ALU.is_equal, ALU.mult).then_inc(pool_mask, 1)
            for m in (2, 3):
                pool.wait_ge(pool_mask, 9 + m)
                pool.tensor_tensor(maskB[:, :], maskB[:, :], cnt[:, 1 + m, :], ALU.add)\
                    .then_inc(pool_mask, 1)

            def ada_pair(l, i):
                f = i + (3 * l - 1)
                for b in range(2):
                    def load(k):
                        pool.dma_start(ada_raw[k % 2][:, :],
                                       w_ada[l, k * P:(k + 1) * P, bass.ds(i * (2 * D) + b * D, D)])\
                            .then_inc(ada_loaded[k % 2], 16)
                    scaled = f * (2 * KD) + b * KD
                    adds = f * ADA_ADDS + (b * (KD - 1) + 1)
                    pool.wait_ge(ada_step, adds)
                    for k in range(2):
                        load(k)
                    if b == 0:
                        pool.wait_ge(ada_turned, f * ADA_BANKS + ADA_BANKS)
                    acc = ada_acc[:, b * D:(b + 1) * D]
                    for k in range(KD):
                        raw = ada_raw[k % 2][:, :]
                        pool.wait_ge(ada_loaded[k % 2], (f * KD + (b * (KD // 2) + k // 2 + 1)) * 16)
                        pool.nop(nofuse=True)
                        pool.tensor_tensor(raw if k else acc, raw,
                                           cond[:, k:k + 1].to_broadcast([P, D]), ALU.mult)\
                            .then_inc(ada_scaled, 1)
                        pool.wait_ge(ada_scaled, scaled + (k + 1))
                        if k:
                            pool.tensor_tensor(acc, acc, raw, ALU.add).then_inc(ada_step, 1)
                        if k + 2 < KD:
                            if k:
                                pool.wait_ge(ada_step, adds + k)
                            load(k + 2)

            pool.wait_ge(setup_act, 1)
            pool.wait_ge(gains_loaded, 16 * N_GAIN_LOADS)
            for half in range(2):
                sl = slice(half * ROPE_HALF, (half + 1) * ROPE_HALF)
                angle(pool.tensor_copy(cos16[:, :, sl], trig[:, 0, :, :]))
                angle(pool.tensor_scalar(sin16[:, :, sl], trig[:, 1, :, :], 1.0 if half else -1.0, None,
                                      ALU.mult))
                angle(pool.tensor_copy(gswap[:, :, sl],
                                    gnat[:, :, (1 - half) * ROPE_HALF:(2 - half) * ROPE_HALF]))
            tall = [P, 4 * LAYERS, TT, ROPE]
            angle(pool.tensor_tensor(ropeC[:, :, :, :], cos16[:, :, :].unsqueeze(1).to_broadcast(tall),
                                  gnat[:, :, :].unsqueeze(2).to_broadcast(tall), ALU.mult))
            angle(pool.tensor_tensor(ropeS[:, :, :, :], sin16[:, :, :].unsqueeze(1).to_broadcast(tall),
                                  gswap[:, :, :].unsqueeze(2).to_broadcast(tall), ALU.mult))
            assert count[0] == ROPE_TABLES

            pool.wait_ge(first_summed, KD)
            with pool.Fori(1, 3) as i:
                ada_pair(0, i)
            with pool.Fori(0, 3) as i:
                ada_pair(1, i)

        @block.scalar
        def _(act):
            A = nc.scalar

            A.preload_act_table(ACT.Silu)
            act.wait_ge(setup_dve, SD_PAR0)
            A.activation(cond[:, :], par[:, 0, C_COND:C_COND + KD], ACT.Silu).then_inc(cond_ready, 1)
            act.wait_ge(angle_done, ANGLES)
            A.activation(trig[:, :, :, :], trig_in[:, :, :, :], ACT.Sin).then_inc(setup_act, 1)
            A.preload_act_table_set("natural_log_exp_and_others")
            act.wait_ge(setup_dve, SD_LAM)
            A.activation(lam_s[:, 1, :], lam_s[:, 0, :], ACT.Exp).then_inc(setup_act, 1)

            def norm(L, which):
                N = L * 2 + which
                base = X_INIT + L * X_LAYER + which * KD - KD
                for m in range(KD):
                    act.wait_ge(x_done, base + m + 1)
                    if m >= SQUARES:
                        act.wait_ge(mean_done, means_before(L, which) + mean_count(which, m - SQUARES))
                    A.activation(work[W_TILE + m % SQUARES], xT[:, m, :], ACT.Square).then_inc(sq_done, 1)
                if which == 0:
                    slot_free(act, L, 0, 0)
                    split_hi(L, 0, 0)
                act.wait_ge(norm_dve, N * 3 + 1)
                A.activation(work[W_Y], work[W_V], ACT.Ln).then_inc(norm_act, 1)
                act.wait_ge(norm_act, N * 3 + 1)
                A.activation(work[W_Y], work[W_Y], ACT.Exp, scale=-0.5).then_inc(norm_act, 1)
                act.wait_ge(norm_act, N * 3 + 2)
                A.activation(work[W_YY], work[W_Y], ACT.Square).then_inc(norm_act, 1)
                shift = (SH_A, SH_F)[which] * KD
                for m in range(KD):
                    act.wait_ge(h_pre, N * KD + m + 1)
                    A.activation(h_hi[:, m, :], work[W_TILE + m % 2], ACT.Identity,
                                 bias=mod[:, shift + m:shift + m + 1]).then_inc(h_hi_done, 1)
                    if m == SPLIT_AFTER:
                        slot_free(act, L, (P_IN, P_UP[0])[which], 1)
                        split_hi(L, (P_IN, P_UP[0])[which], 1)

            def nat_squares(L, g, t):
                Q = (L * 4 + qk_index(g)) * TT + t
                act.wait_ge(proj_done, (L * GROUPS + g) * TT + t + 1)
                if qk_index(g) * TT + t:
                    act.wait_ge(nat_dve, Q * 5)
                A.activation(work[W_SQ], bank[t][:, :], ACT.Square).then_inc(nat_act, 1)

            def nat_stats(L, g, t):
                Q = (L * 4 + qk_index(g)) * TT + t
                act.wait_ge(nat_dve, Q * 5 + 2)
                A.activation(small[:, 1, :], small[:, 0, :], ACT.Ln).then_inc(nat_act, 1)
                act.wait_ge(nat_act, Q * 3 + 2)
                A.activation(small[:, 2, :], small[:, 1, :], ACT.Exp, scale=-0.5).then_inc(nat_act, 1)

            def qk_evacuate(L, g, t):
                k = qk_index(g)
                act.wait_ge(nat_turned, (L * 4 + k) * TT + t + 1)
                act.nop(nofuse=True)
                A.activation(qkT[:, 4 * k:4 * k + 4, t * P:(t + 1) * P],
                             bank[6][:, :].rearrange("p (b n) -> p b n", n=P), ACT.Copy,
                             scale=gcol[:, bass.ds(L + LAYERS * k, 1)]).then_inc(qk_ready, 1)

            def v_copy(L, g, t):
                act.wait_ge(proj_done, (L * GROUPS + g) * TT + t + 1)
                A.activation(vnat[:, t, (g // 3) * GW:(g // 3 + 1) * GW], bank[t][:, :], ACT.Copy)\
                    .then_inc(v_ready, 1)

            def exps(L, task, n):
                W = (n + 1) * P
                for e in range(2):
                    r = row_of(task, n, e)
                    buf = prob(task * TT + n, e)[:, 0:W]
                    act.wait_ge(score_done, L * ROWS + r + 1)
                    A.activation(buf, buf, ACT.Exp, bias=mneg[:, r:r + 1], scale=-1.0,
                                 accum_out=lsum[:, r:r + 1]).then_inc(exp_done, 1)

            def pT_copy(L, task, n):
                W = (n + 1) * P
                for i, _ in turn_units(task, n):
                    act.wait_ge(p_turned, L * T_ALL + i + 1)
                    if 1 <= i <= T_DIFF:
                        act.wait_ge(pv_done, L * T_ALL + i)
                    elif i:
                        act.wait_ge(pv_done, L * T_ALL + i - 1)
                    A.activation(turned(i)[:, 0:W], turn_bank(i)[:, 0:W], ACT.Copy)\
                        .then_inc(pT_ready, 1)

            def finish(L, task, stage):
                F = L * TASKS + task
                k = TT if is_diff(task) else 2 * TT
                if stage == 1:
                    act.wait_ge(fin_dve, F * 8 + 2)
                    A.activation(work[W_OSQ], normed(task), ACT.Square).then_inc(fin_act, 1)
                if stage == 2:
                    act.wait_ge(fin_dve, F * 8 + 4)
                    A.activation(fsmall[:, 1, 0:k], fsmall[:, 0, 0:k], ACT.Ln).then_inc(fin_act, 1)
                    act.wait_ge(fin_act, F * 3 + 2)
                    A.activation(fsmall[:, 2, 0:k], fsmall[:, 1, 0:k], ACT.Exp, scale=-0.5)\
                        .then_inc(fin_act, 1)
                if stage == 4:
                    act.wait_ge(o_turned, F + 1)
                    kind = G_SUB if is_diff(task) else G_OUT
                    act.nop(nofuse=True)
                    A.activation(h_hi[:, task, :], f_bank(task)[:, :], ACT.Copy,
                                 scale=gcol[:, bass.ds(L + LAYERS * kind, 1)]).then_inc(o_hi_done, 1)

            with act.Fori(0, LAYERS) as L:
                A.preload_act_table_set("natural_log_exp_and_others")
                norm(L, 0)
                for g in range(GROUPS):
                    for s in range(2):
                        for t in range(TT):
                            if normed_tile(g, s, t):
                                nat_stats(L, *normed_tile(g, s, t))
                            evacuated = turned_tile(g, s, t) is None
                            steps = sorted([(a, 0) for a in early_times(g, s, t)] +
                                           [(a, 1) for a in a_times(g, s, t)])
                            for a, late in steps:
                                if not late:
                                    if has(a - 1):
                                        exps(L, *step(a - 1))
                                    for stage, lag in ((1, 7), (2, 8)):
                                        if has_end(a - lag):
                                            finish(L, (a - lag) // TT, stage)
                                    continue
                                if not evacuated:
                                    qk_evacuate(L, *turned_tile(g, s, t))
                                    evacuated = True
                                if has(a - 2):
                                    pT_copy(L, *step(a - 2))
                            if not evacuated:
                                qk_evacuate(L, *turned_tile(g, s, t))
                            if t == 0 and g + s:
                                slot_free(act, L, g + s, 1 - s)
                                split_hi(L, g + s, 1 - s)
                            if s == 1 and g in QK_GROUPS:
                                nat_squares(L, g, t)
                            if s == 1 and g not in QK_GROUPS:
                                v_copy(L, g, t)
                for k in range(T_DIFF, T_DIFF + 2):
                    exps(L, *step(k))
                for k in range(T_DIFF, STEPS):
                    task, n = step(k)
                    pT_copy(L, task, n)
                    if task > DIFF_TASKS and 1 <= n < 3:
                        finish(L, task - 1, n)
                    if k + 2 < STEPS:
                        exps(L, *step(k + 2))
                    if task == DIFF_TASKS:
                        finish(L, n, 4)
                    elif n == 3:
                        finish(L, task - 1, 4)
                for stage in (1, 2, 4):
                    finish(L, TASKS - 1, stage)

                for q in range(OUT_PAIRS):
                    slot_free(act, L, P_OUT + q, 1)
                    split_hi(L, P_OUT + q, 1)
                    slot_free(act, L, P_OUT + q + 1, 0)
                    split_hi(L, P_OUT + q + 1, 0)
                norm(L, 1)
                A.preload_act_table(ACT.Silu)

                for half, tiles in enumerate(FFN_SETS):
                    pairs = tiles // 2
                    with act.Fori(0, pairs) as i:
                        X = L * UP_LAYER + (i * 4 + UP_BASE[half])
                        Y = L * FT + (i * 2 + FF_BASE[half])
                        for part in range(2):
                            for q in range(2):
                                b = 2 * part + q
                                col = i * 2 + (part * FT + FF_BASE[half] + q)
                                act.wait_ge(act_lo_done, Y + 1)
                                act.wait_ge(up_done, X + b + 2)
                                act.nop(nofuse=True)
                                A.activation(work[b], bank[b][:, :], ACT.Identity,
                                             scale=par[:, L, bass.ds(col + C_W2, 1)],
                                             bias=par[:, L, bass.ds(col + C_B, 1)])\
                                    .then_inc(tap2_done, 1)
                            if part == 0:
                                for q in range(2):
                                    act.wait_ge(conv_done, X + 4 + q + 1)
                                    A.activation(work[4 + q], work[q], ACT.Silu)\
                                        .then_inc(silu_done, 1)
                                act.wait_ge(up_done, X + 3)
                                split_hi(L, i + (P_UP[half] + 1), 0)
                        act.wait_ge(up_done, X + 5)
                        split_hi(L, i + (P_UP[half] + 1), 1)
                        for q in range(2):
                            act.wait_ge(prod_done, Y + q + 1)
                            act.nop(nofuse=True)
                            A.activation(act_hi[:, bass.ds(i * 2 + q, 1), :],
                                         work[2 + q].unsqueeze(1), ACT.Copy)\
                                .then_inc(act_hi_done, 1)

                    def split_down(i):
                        act.wait_ge(weights_used[0], L * USED0_LAYER + (i + (USED0_DOWN[half] + 1)))
                        split_hi(L, i + P_DOWN[half], 0, D)
                        act.wait_ge(weights_used[1], L * USED1_LAYER + (i + USED1_DOWN[half]))
                        split_hi(L, i + P_DOWN[half], 1, D)
                    with act.Fori(1, pairs) as i:
                        split_down(i)
                    if half == 0:
                        act.wait_ge(weights_used[0], L * USED0_LAYER + USED0_DOWN[half] + pairs + 1)
                        split_hi(L, P_UP[1], 0)
                        act.wait_ge(acc_done, L * X_LAYER + 2 * KD + 1)
                        split_hi(L, P_UP[1], 1)

            for t in range(TT):
                act.wait_ge(out_turned, 2 * t + 2)
                A.activation(xnat[:, t, 512:D], bank[2 * t + 1][:, :], ACT.Copy)\
                    .then_inc(out_copied_act, 1)

        @block.tensor
        def _(pe):
            M = nc.tensor.matmul

            def three(dst, w, wsl, h, hsl, first, last):
                M(dst, w[0][wsl], h[0][hsl], start=first, stop=False)
                M(dst, w[1][wsl], h[0][hsl], start=False, stop=False)
                return M(dst, w[0][wsl], h[1][hsl], start=False, stop=last)

            def first_tile(count, products, dsts, operands):
                pe.wait_ge(h_hi_done, count)
                for lo in range(2):
                    if lo:
                        pe.wait_ge(h_lo_done, count)
                    for dst, (a, b) in zip(dsts, operands):
                        for i, j in products[lo]:
                            last = M(dst, a[i], b[j], start=(lo == 0 and i + j == 0), stop=False)
                return last

            pe.wait_ge(ident_ready, 1)
            pe.wait_ge(x_loaded, 16 * TT)
            for m in range(KD):
                b = bank[4 + m % 4]
                if m >= 4:
                    pe.wait_ge(x_done, m - 3)
                for t in range(TT):
                    last = nc.tensor.transpose(b[:, t * P:(t + 1) * P], xnat[:, t, m * P:(m + 1) * P],
                                               ident[:, :])
                last.then_inc(setup_pe, 1)
            for l in range(LAYERS):
                pe.wait_ge(rows_loaded[l], 16 * N_ROW_LOADS)
                at = 0
                for blk, k in ((0, 4 * FT), (1, 4 * FT), (2, 6 * KD + 3 * KD)):
                    last = nc.tensor.transpose(bank[l][:, at:at + k], prow[0:k, 3 * l + blk, :],
                                               ident[0:k, 0:k])
                    at += k
                last.then_inc(setup_pe, 1)
            pe.wait_ge(gains_loaded, 16 * N_GAIN_LOADS)
            nc.tensor.transpose(bank[2][:, 0:12], prow[0:12, 3 * LAYERS, :], ident[0:12, 0:12])\
                .then_inc(setup_pe, 1)
            pe.wait_ge(setup_dve, 2)
            for done in (weights_used[0], acc_done, up_done):
                M(bank[3][0:1, 0:1], ones[:, :], ones[:, :], start=True, stop=True).then_inc(done, 1)

            def norm_means(L, which):
                N = L * 2 + which
                for m in range(0, KD, 1 + which):
                    if which:
                        pe.wait_ge(pair_done, L * (KD // 2) + m // 2 + 1)
                    else:
                        pe.wait_ge(sq_done, N * KD + m + 1)
                    M(bank[0][:, :], mean_w[:, :], work[W_TILE + m % SQUARES], start=(m == 0),
                      stop=(m >= KD - 1 - which)).then_inc(mean_done, 1)

            def keep_warm(n):
                for _ in range(n):
                    M(bank[1][:, 0:P], mean_w[:, :], ident[:, :], start=True, stop=True)

            def await_norm(L, which):
                N = L * 2 + which
                for done, count in ((norm_dve, N * 3 + 1), (norm_act, N * 3 + 1), (norm_act, N * 3 + 2),
                                    (norm_act, N * 3 + 3), (norm_dve, N * 3 + 2), (norm_dve, N * 3 + 3)):
                    pe.wait_ge(done, count)
                    pe.nop(nofuse=True)
                    keep_warm(2)

            def turn_ada(L, i, q, b):
                if q == 0:
                    if i == 0:
                        pe.wait_ge(first_summed, KD)
                    pe.wait_ge(ada_step, (L * 3 + i) * ADA_ADDS + 1)
                for m in range(4):
                    last = nc.tensor.transpose(bank[b][:, m * P:(m + 1) * P],
                                               ada_acc[:, (4 * q + m) * P:(4 * q + m + 1) * P],
                                               ident[:, :])
                last.then_inc(ada_turned, 1)

            def turn_nat(L, g, t, p_tiles):
                k = qk_index(g)
                Q = (L * 4 + k) * TT + t
                pe.wait_ge(nat_ready, Q + 1)
                if k * TT + t:
                    pe.wait_ge(qk_ready, Q)
                if p_tiles:
                    pe.wait_ge(pT_ready, L * T_ALL + p_tiles)
                for b in range(4):
                    last = nc.tensor.transpose(bank[6][:, b * P:(b + 1) * P],
                                               work[W_NATS[(k * TT + t) % 3]][:, b * P:(b + 1) * P], ident[:, :])
                last.then_inc(nat_turned, 1)

            def scores(L, task, n):
                W = (n + 1) * P
                for e in range(2):
                    r = row_of(task, n, e)
                    if is_diff(task):
                        if r >= 2:
                            pe.wait_ge(score_done, L * ROWS + r - 1)
                    elif r >= 2 * T_DIFF + 2:
                        pe.wait_ge(score_done, L * ROWS + r - 3)
                    base = 0 if is_diff(task) else 8
                    f = task if is_diff(task) else task - DIFF_TASKS
                    M(score_bank(task, n, e)[:, 0:W],
                      qkT[e * HEAD:(e + 1) * HEAD, base + f, n * P:(n + 1) * P],
                      qkT[e * HEAD:(e + 1) * HEAD, base + 4 + f, 0:W],
                      start=True, stop=True).then_inc(scores_mm, 1)

            def turn_p(L, task, n):
                for i, e in turn_units(task, n):
                    if is_diff(task):
                        pe.wait_ge(comb_done, (L * T_DIFF + i + 1) * 3)
                    else:
                        pe.wait_ge(exp_done, L * ROWS + row_of(task, n, e) + 1)
                    if 1 <= i < T_DIFF:
                        pe.wait_ge(pT_ready, L * T_ALL + i)
                    elif i:
                        pe.wait_ge(pT_ready, L * T_ALL + i - 1)
                    for b in range(n + 1):
                        last = nc.tensor.transpose(turn_bank(i)[:, b * P:(b + 1) * P],
                                                   prob(task * TT + n, e)[:, b * P:(b + 1) * P], ident[:, :])
                    last.then_inc(p_turned, 1)

            def weigh_values(L, task, n):
                for i, e in turn_units(task, n):
                    pe.wait_ge(pT_ready, L * T_ALL + i + 1)
                    if n == 0 and e == 0 and task:
                        if is_diff(task):
                            pe.wait_ge(fin_dve, (L * TASKS + task - 1) * 8 + 2)
                        elif task > DIFF_TASKS:
                            pe.wait_ge(o_lo_done, L * TASKS + task - 1)
                    if is_diff(task):
                        dst, v0, w = n * P, task * P, P
                    else:
                        dst, v0, w = n * P + e * HEAD, GW + (task - DIFF_TASKS) * P + e * HEAD, HEAD
                    for b in range(n + 1):
                        last = M(out_bank(task)[:, dst:dst + w],
                                 turned(i)[:, b * P:(b + 1) * P], vnat[:, b, v0:v0 + w],
                                 start=(b == 0), stop=(b == n))
                    last.then_inc(pv_done, 1)

            def turn_o(L, task):
                pe.wait_ge(fin_dve, (L * TASKS + task + 1) * 8)
                if is_diff(task):
                    if task == 0:
                        pe.wait_ge(fin_dve, (L * TASKS + DIFF_TASKS) * 8)
                    else:
                        pe.wait_ge(o_lo_done, L * TASKS + task)
                for n in range(TT):
                    last = nc.tensor.transpose(f_bank(task)[:, n * P:(n + 1) * P],
                                               normed(task)[:, n * P:(n + 1) * P], ident[:, :])
                last.then_inc(o_turned, 1)

            with pe.Fori(0, LAYERS) as L:
                norm_means(L, 0)
                for q in range(ADA_BANKS):
                    turn_ada(L, 0, q, 4 + q)
                await_norm(L, 0)
                def project(t, s, k):
                    kt = 4 * s + k
                    return three(bank[t][:, :], (h_hi, h_lo),
                                 (slice(None), kt, slice(t * P, (t + 1) * P)),
                                 (w_hi[s], w_lo[s]), (slice(None), slice(k * GW, (k + 1) * GW)),
                                 kt == 0, kt == KD - 1)

                p_tiles = 0
                for g in range(GROUPS):
                    for s in range(2):
                        pe.wait_ge(lo_ready[s], L * PAIRS + P_IN + g + 2)
                        if g == 0 and s == 0:
                            for k in range(4):
                                if k == 0:
                                    last = first_tile(
                                        L * 2 * KD + 1, (((0, 0), (0, 1)), ((1, 0),)),
                                        [bank[t][:, :] for t in range(TT)],
                                        [([h[:, 0, t * P:(t + 1) * P] for h in (h_hi, h_lo)],
                                          [w[:, 0:GW] for w in (w_hi[0], w_lo[0])]) for t in range(TT)])
                                    continue
                                pe.wait_ge(h_lo_done, L * 2 * KD + k + 1)
                                for t in range(TT):
                                    last = project(t, s, k)
                            last.then_inc(weights_used[0], 1)
                            continue
                        for t in range(TT):
                            if s == 0:
                                if g - 1 in QK_GROUPS:
                                    pe.wait_ge(nat_mul, (L * 4 + qk_index(g - 1)) * TT + t + 1)
                                else:
                                    pe.wait_ge(v_ready, (L * 2 + (g - 1) // 3) * TT + t + 1)
                            for k in range(4 if g or t > 1 else 4 * (t == 0)):
                                if g == 0 and t == 0:
                                    pe.wait_ge(h_lo_done, L * 2 * KD + 4 + k + 1)
                                    last = project(0, s, k)
                                    if k == 3:
                                        last.then_inc(proj_done, 1)
                                    last = project(1, s, k)
                                else:
                                    last = project(t, s, k)
                            if s == 1 and (g or t != 1):
                                last.then_inc(proj_done, 1)
                            elif s == 0 and t == TT - 1:
                                last.then_inc(weights_used[0], 1)
                            tile = turned_tile(g, s, t)
                            if tile:
                                turn_nat(L, *tile, p_tiles)
                            j = slot_of(g, s, t)
                            if j in ADA_AT and ADA_AT[j][0] == 1:
                                for q, b in ADA_AT[j][1]:
                                    if q >= 2:
                                        pe.wait_ge(ada_reduced, (L * 3 + 1) * ADA_BANKS + q - 1)
                                    turn_ada(L, 1, q, b)
                            for a in a_times(g, s, t):
                                if a == 0:
                                    pe.wait_ge(qk_ready, (L * 4 + 2) * TT)
                                    pe.wait_ge(v_ready, (L * 2 + 1) * TT)
                                if has(a):
                                    scores(L, *step(a))
                                if has(a - 3):
                                    weigh_values(L, *step(a - 3))
                                if a == 2:
                                    pe.wait_ge(ada_reduced, (L * 3 + 2) * ADA_BANKS)
                                if has(a - 2):
                                    if tile:
                                        pe.wait_ge(qk_ready,
                                                   (L * 4 + qk_index(tile[0])) * TT + tile[1] + 1)
                                    turn_p(L, *step(a - 2))
                                    p_tiles += 1
                            for q, b in ADA_AT[j][1] if j in ADA_AT and ADA_AT[j][0] == 2 else ():
                                if q == 0:
                                    pe.wait_ge(score_done, L * ROWS + 2 * T_DIFF)
                                if q == 2:
                                    pe.wait_ge(pT_ready, L * T_ALL + T_DIFF)
                                if q == 3:
                                    pe.wait_ge(ada_reduced, (L * 3 + 2) * ADA_BANKS + 1)
                                turn_ada(L, 2, q, b)

                pe.wait_ge(qk_ready, (L + 1) * 4 * TT)
                pe.wait_ge(v_ready, (L * 2 + 1) * TT + 2)
                pe.wait_ge(ada_reduced, (L + 1) * 3 * ADA_BANKS)
                for k in range(T_DIFF, T_DIFF + 2):
                    scores(L, *step(k))
                for k in range(T_DIFF, STEPS):
                    task, n = step(k)
                    if k + 2 < STEPS:
                        scores(L, *step(k + 2))
                    if k == T_DIFF:
                        pe.wait_ge(v_ready, (L + 1) * 2 * TT)
                    turn_p(L, task, n)
                    if k > T_DIFF:
                        weigh_values(L, *step(k - 1))
                    if task == DIFF_TASKS:
                        turn_o(L, n)
                    elif n == 3:
                        turn_o(L, task - 1)
                weigh_values(L, TASKS - 1, TT - 1)

                for q in range(OUT_PAIRS):
                    for s in range(2):
                        pe.wait_ge(lo_ready[s], L * PAIRS + P_OUT + q + 2)
                        unit = 2 * q + s
                        for m in ((0, 1, 2, 4, 5, 6, 3, 7) if unit == 0 else range(KD)):
                            if unit == 0 and m == 0:
                                pe.wait_ge(o_lo_done, L * TASKS + 2)
                                pe.wait_ge(pT_ready, (L + 1) * T_ALL)
                            if unit == 0 and m == 3:
                                turn_o(L, TASKS - 1)
                                pe.wait_ge(o_lo_done, L * TASKS + TASKS - 1)
                            if unit == 0 and m == 7:
                                pe.wait_ge(o_lo_done, L * TASKS + TASKS)
                            for k in range(2):
                                kt = 2 * unit + k
                                last = three(bank[m][:, :], (w_hi[s], w_lo[s]),
                                             (slice(None), slice(k * D + m * P, k * D + (m + 1) * P)),
                                             (h_hi, h_lo), (slice(None), kt, slice(None)),
                                             kt == 0, kt == KD - 1)
                            if kt == KD - 1:
                                last.then_inc(acc_done, 1)
                        if unit < 2 * OUT_PAIRS - 1:
                            last.then_inc(weights_used[s], 1)
                norm_means(L, 1)
                await_norm(L, 1)

                for half, tiles in enumerate(FFN_SETS):
                    pairs = tiles // 2
                    pe.wait_ge(x_done, L * X_LAYER + (X_INIT + half * KD + 4))
                    pe.nop(nofuse=True)
                    with pe.Fori(0, pairs) as i:
                        X = L * UP_LAYER + (i * 4 + UP_BASE[half])

                        def up(s, q, kt):
                            at = kt * 2 * P + q * P
                            return three(bank[2 * s + q][:, :], (w_hi[s], w_lo[s]),
                                         (slice(None), slice(at, at + P)),
                                         (h_hi, h_lo), (slice(None), kt, slice(None)),
                                         kt == 0, kt == KD - 1)

                        pe.wait_ge(lo_ready[0], L * PAIRS + (i + (P_UP[half] + 2)))
                        pe.wait_ge(conv_done, X + 2)
                        for kt in range(KD):
                            if half == 0 and kt == 0:
                                first_tile((L * 2 + 1) * KD + 1, (((0, 0), (1, 0)), ((0, 1),)),
                                           [bank[q][:, :] for q in range(2)],
                                           [([w[:, q * P:(q + 1) * P] for w in (w_hi[0], w_lo[0])],
                                             [h[:, 0, :] for h in (h_hi, h_lo)]) for q in range(2)])
                                continue
                            if half == 0:
                                pe.wait_ge(h_lo_done, (L * 2 + 1) * KD + kt + 1)
                            for q in range(2):
                                last = up(0, q, kt)
                                if kt == KD - 1:
                                    last.then_inc(up_done, 1)
                        pe.wait_ge(lo_ready[1], L * PAIRS + (i + (P_UP[half] + 2)))
                        for q in range(2):
                            pe.wait_ge(conv_done, X + q + 3)
                            for kt in range(KD):
                                last = up(1, q, kt)
                            last.then_inc(up_done, 1)

                    def down_pair(i, first, final):
                        for s in range(2):
                            pe.wait_ge(lo_ready[s], L * PAIRS + (i + (P_DOWN[half] + 2)))
                            pe.wait_ge(act_lo_done, L * FT + (i * 2 + (FF_BASE[half] + s + 2)))
                            rhs = (slice(None), bass.ds(i * 2 + s, 1), slice(None))
                            start = first and s == 0
                            stop = final and s == 1
                            for m in ((4, 5, 6, 7, 0, 1, 2, 3) if start else range(KD)):
                                if start and m == 4 and half:
                                    pe.wait_ge(x_done, L * X_LAYER + (X_INIT + 2 * KD))
                                if start and m < 4:
                                    pe.wait_ge(conv_done, L * UP_LAYER + UP_BASE[half] + 2 * tiles + m + 1)
                                last = three(bank[m][:, :].unsqueeze(1), (w_hi[s], w_lo[s]),
                                             (slice(None), slice(m * P, (m + 1) * P)),
                                             (act_hi, act_lo), rhs, start, stop)
                                if stop:
                                    last.then_inc(acc_done, 1)
                            if not stop:
                                last.then_inc(weights_used[s], 1)

                    down_pair(0, True, False)
                    with pe.Fori(1, pairs - 1) as i:
                        down_pair(i, False, False)
                    down_pair(pairs - 1, False, True)

            pe.wait_ge(x_done, X_INIT + LAYERS * X_LAYER)
            for t in range(TT):
                for f in range(2):
                    for m in range(4):
                        last = nc.tensor.transpose(bank[2 * t + f][:, m * P:(m + 1) * P],
                                                   xT[:, 4 * f + m, t * P:(t + 1) * P], ident[:, :])
                    last.then_inc(out_turned, 1)

        @block.vector
        def _(dve):
            V = nc.vector
            count = [0]

            def setup(ins):
                ins.then_inc(setup_dve, 1)
                count[0] += 1
                dve.wait_ge(setup_dve, count[0])
                return count[0]

            V.memset(prow[0:12, 3 * LAYERS, :], 1.0).then_inc(rows_set, 1)
            setup(V.memset(mean_w[:, :], 1.0 / D))
            setup(V.memset(ones[:, :], 1.0))
            for i, done in enumerate((*lo_ready, act_lo_done)):
                V.memset(small[:, i, :], 1.0).then_inc(done, 1)
            V.memset(small[:, 3, :], 1.0).then_inc(conv_done, 4)
            dve.wait_ge(pool_mask, 4)
            setup(V.tensor_scalar(rem[:, 0, :], delta[:, :], 3, None, ALU.bitwise_and))
            setup(V.tensor_scalar(rem[:, 1, :], delta[:, :], 15, None, ALU.bitwise_and))
            setup(V.tensor_scalar(cnt[:, 1, :], rem[:, 0, :], 0.0, None, ALU.is_equal))
            setup(V.tensor_scalar(cnt[:, 2, :], rem[:, 1, :], 0.0, None, ALU.is_equal))
            assert setup(V.tensor_tensor(cnt[:, 1, :], cnt[:, 1, :], cnt[:, 2, :], ALU.add)) == SD_STRIDED
            for m in range(KD):
                dve.wait_ge(setup_pe, m + 1)
                V.tensor_copy(xT[:, m, :], bank[4 + m % 4][:, :]).then_inc(x_done, 1)
            dve.wait_ge(setup_pe, KD + 1)
            assert setup(V.tensor_copy(par[:, 0, :], bank[0][:, 0:PARAMS])) == SD_PAR0
            def first(k):
                dve.wait_ge(first_loaded[k % FIRST_SLOTS], 16 * (k // FIRST_SLOTS + 1))
                if k == 0:
                    dve.wait_ge(cond_ready, 1)
                    V.tensor_scalar(ada_acc[:, :], ada_first[0][:, :], cond[:, 0:1], None, ALU.mult)\
                        .then_inc(first_summed, 1)
                else:
                    dve.wait_ge(first_summed, k)
                    V.scalar_tensor_tensor(out=ada_acc[:, :], in0=ada_first[k % FIRST_SLOTS][:, :],
                                           scalar=cond[:, k:k + 1], in1=ada_acc[:, :],
                                           op0=ALU.mult, op1=ALU.add).then_inc(first_summed, 1)
            for k in range(3):
                first(k)
            for l in range(1, LAYERS):
                dve.wait_ge(setup_pe, KD + l + 1)
                setup(V.tensor_copy(par[:, l, :], bank[l][:, 0:PARAMS]))
            dve.wait_ge(setup_pe, KD + LAYERS + 1)
            setup(V.tensor_copy(gcol[:, :], bank[2][:, 0:12]))
            for l in range(LAYERS):
                k = G_SUB * LAYERS + l
                setup(V.tensor_scalar(gcol[:, k:k + 1], gcol[:, k:k + 1], 1.0 - lam_init(l), None,
                                      ALU.mult))
            for i in range(2):
                setup(V.tensor_tensor(lamv[:, 2 * i, :, :], lamv[:, 2 * i, :, :],
                                      lamv[:, 2 * i + 1, :, :], ALU.mult))
                last = setup(V.tensor_reduce(lam_s[:, 0, 2 * i:2 * i + 2], lamv[:, 2 * i, :, :],
                                             AX.X, ALU.add))
            assert last == SD_LAM
            first(3)
            first(4)
            dve.wait_ge(setup_act, 2)
            for l in range(LAYERS):
                setup(V.tensor_tensor(neglam[:, l:l + 1], lam_s[:, 1, 2 + l:3 + l],
                                      lam_s[:, 1, l:l + 1], ALU.subtract))
                setup(V.tensor_scalar(neglam[:, l:l + 1], neglam[:, l:l + 1], -lam_init(l), None,
                                      ALU.add))
            for k in range(5, KD):
                first(k)
            dve.wait_ge(pool_mask, 13)
            dve.wait_ge(angle_done, ROPE_TABLES)

            def reduce_ada(L, i, q, b):
                N = (L * 3 + i) * ADA_BANKS + q
                dve.wait_ge(ada_turned, N + 1)
                V.tensor_reduce(mod_sum[:, 4 * q:4 * q + 4],
                                bank[b][:, :].rearrange("p (k n) -> p k n", n=P), AX.X, ALU.add)\
                    .then_inc(ada_reduced, 1)
                if q == ADA_BANKS - 1:
                    dve.wait_ge(ada_reduced, N + 1)
                    V.tensor_tensor(mod[:, 2 * i * KD:2 * (i + 1) * KD], mod_sum[:, :],
                                    par[:, L, C_ADA + 2 * i * KD:C_ADA + 2 * (i + 1) * KD], ALU.add)\
                        .then_inc(mod_ready, 1)

            def norm(L, which):
                N = L * 2 + which
                scale, gain = ((SC_A, C_GMIX), (SC_F, C_GFFN))[which]
                if which == 0:
                    split_lo(L, 0, 0)
                dve.wait_ge(mean_done, means_before(L, which) + mean_count(which, KD - 1))
                V.tensor_scalar(work[W_V], bank[0][:, :], EPS, None, ALU.add).then_inc(norm_dve, 1)
                if which == 0:
                    for q in range(ADA_BANKS):
                        reduce_ada(L, 0, q, 4 + q)
                dve.wait_ge(mod_ready, L * 3 + 1 + 2 * which)
                V.scalar_tensor_tensor(out=afac[:, :], in0=mod[:, scale * KD:(scale + 1) * KD],
                                       scalar=1.0, in1=par[:, L, gain:gain + KD],
                                       op0=ALU.add, op1=ALU.mult).then_inc(afac_done, 1)
                dve.wait_ge(afac_done, N * 2 + 1)
                V.tensor_scalar(afac[:, :], afac[:, :], -0.5, None, ALU.mult).then_inc(afac_done, 1)
                dve.wait_ge(norm_act, N * 3 + 3)
                V.tensor_tensor(work[W_YY], work[W_YY], work[W_V], ALU.mult).then_inc(norm_dve, 1)
                dve.wait_ge(norm_dve, N * 3 + 2)
                V.scalar_tensor_tensor(out=work[W_Y], in0=work[W_YY], scalar=-3.0,
                                       in1=work[W_Y], op0=ALU.add, op1=ALU.mult)\
                    .then_inc(norm_dve, 1)
                dve.wait_ge(norm_dve, N * 3 + 3)
                dve.wait_ge(afac_done, N * 2 + 2)
                shift = (SH_A, SH_F)[which] * KD

                def lo(m):
                    dve.wait_ge(h_hi_done, N * KD + m + 1)
                    V.scalar_tensor_tensor(out=h_lo[:, m, :], in0=work[W_TILE + m % 2],
                                           scalar=mod[:, shift + m:shift + m + 1],
                                           in1=h_hi[:, m, :], op0=ALU.add, op1=ALU.subtract)\
                        .then_inc(h_lo_done, 1)
                for m in range(KD):
                    if m >= 2:
                        dve.wait_ge(h_lo_done, N * KD + m - 1)
                    V.scalar_tensor_tensor(out=work[W_TILE + m % 2], in0=xT[:, m, :],
                                           scalar=afac[:, m:m + 1], in1=work[W_Y],
                                           op0=ALU.mult, op1=ALU.mult).then_inc(h_pre, 1)
                    if m:
                        lo(m - 1)
                    if m == SPLIT_AFTER + 1:
                        split_lo(L, (P_IN, P_UP[0])[which], 1)
                lo(KD - 1)

            def newton(dst, y, v, tmp, done, base):
                V.tensor_tensor(tmp, y, y, ALU.mult).then_inc(done, 1)
                dve.wait_ge(done, base + 1)
                V.tensor_tensor(tmp, tmp, v, ALU.mult).then_inc(done, 1)
                dve.wait_ge(done, base + 2)
                V.scalar_tensor_tensor(out=dst, in0=tmp, scalar=-3.0, in1=y, op0=ALU.add,
                                       op1=ALU.mult).then_inc(done, 1)
                dve.wait_ge(done, base + 3)

            def nat_sums(L, g, t):
                Q = (L * 4 + qk_index(g)) * TT + t
                dve.wait_ge(nat_act, Q * 3 + 1)
                V.tensor_reduce(small[:, 3, :], work[W_SQ].rearrange("p (h d) -> p h d", d=HEAD),
                                AX.X, ALU.add).then_inc(nat_dve, 1)
                dve.wait_ge(nat_dve, Q * 5 + 1)
                V.tensor_scalar(small[:, 0, :], small[:, 3, :], 1.0 / HEAD, EPS, ALU.mult, ALU.add)\
                    .then_inc(nat_dve, 1)

            def nat(L, g, t):
                k = qk_index(g)
                Q = (L * 4 + k) * TT + t
                heads = [P, GH, HEAD]
                dve.wait_ge(nat_act, Q * 3 + 3)
                newton(small[:, 4, :], small[:, 2, :], small[:, 0, :], small[:, 5, :], nat_dve,
                       Q * 5 + 2)
                buf = work[W_NATS[(k * TT + t) % 3]]
                if k * TT + t >= 3:
                    dve.wait_ge(nat_turned, Q - 2)
                fac = -0.5 * (-HEAD ** -0.5 if g in (0, 3) else 1.0)
                V.scalar_tensor_tensor(out=buf.rearrange("p (h d) -> p h d", d=HEAD),
                                       in0=bank[t][:, :].rearrange("p (h d) -> p h d", d=HEAD),
                                       scalar=fac, in1=small[:, 4, :].unsqueeze(2).to_broadcast(heads),
                                       op0=ALU.mult, op1=ALU.mult).then_inc(nat_mul, 1)
                dve.wait_ge(nat_mul, Q + 1)
                head = buf.rearrange("p (h d) -> p h d", d=HEAD)[:, :, 0:ROPE]
                pair = head.rearrange("p h (a d) -> p h a d", a=2)
                own = work[W_ROPE][:, 0:GH * ROPE].rearrange("p (h d) -> p h d", d=ROPE)
                other = work[W_ROPE][:, GH * ROPE:2 * GH * ROPE].rearrange("p (h a d) -> p h a d", a=2,
                                                                      d=ROPE_HALF)
                table = bass.ds(L + LAYERS * k, 1)
                V.tensor_tensor(own, head, ropeC[:, table, t, :].to_broadcast([P, GH, ROPE]),
                                ALU.mult).then_inc(rope_dve, 1)
                V.tensor_tensor(other, pair[:, :, ::-1, :],
                                ropeS[:, table, t, :].rearrange("p o (a d) -> p o a d", a=2)
                                .to_broadcast([P, GH, 2, ROPE_HALF]), ALU.mult).then_inc(rope_dve, 1)
                dve.wait_ge(rope_dve, Q * 2 + 2)
                V.tensor_tensor(head, own, other.rearrange("p h a d -> p h (a d)"), ALU.add)\
                    .then_inc(nat_ready, 1)
                dve.wait_ge(nat_ready, Q + 1)

            def score_rows(L, task, n):
                W = (n + 1) * P
                mask = maskA if is_diff(task) else maskB
                for e in range(2):
                    r = row_of(task, n, e)
                    dve.wait_ge(scores_mm, L * ROWS + r + 1)
                    k = task * TT + n
                    if k >= 2:
                        before = k - 2 if k < T_DIFF else max(k - 3, T_DIFF - 1)
                        last_unit = turn_units(*step(before))[-1][0]
                        dve.wait_ge(p_turned, L * T_ALL + last_unit + 1)
                    dve.nop(nofuse=True)
                    V.tensor_tensor_reduce(prob(task * TT + n, e)[:, 0:W], score_bank(task, n, e)[:, 0:W],
                                           mask[:, S - W:S],
                                           1.0, 3e38, ALU.add, ALU.min, mneg[:, r:r + 1])\
                        .then_inc(score_done, 1)

            def combine(L, task, n):
                W = (n + 1) * P
                i = task * TT + n
                B = (L * T_DIFF + i) * 3
                r = row_of(task, n, 0)
                c2 = comb[:, n % 2, :]
                dve.wait_ge(exp_done, L * ROWS + r + 2)
                V.reciprocal(c2[:, 0:1], lsum[:, r + 1:r + 2]).then_inc(comb_done, 1)
                dve.wait_ge(comb_done, B + 1)
                V.scalar_tensor_tensor(out=c2[:, 1:2], in0=lsum[:, r:r + 1], scalar=c2[:, 0:1],
                                       in1=neglam[:, bass.ds(L, 1)], op0=ALU.mult, op1=ALU.mult)\
                    .then_inc(comb_done, 1)
                dve.wait_ge(comb_done, B + 2)
                p1, p2 = (prob(task * TT + n, e)[:, 0:W] for e in range(2))
                V.scalar_tensor_tensor(out=p1, in0=p2, scalar=c2[:, 1:2], in1=p1,
                                       op0=ALU.mult, op1=ALU.add).then_inc(comb_done, 1)

            def finish(L, task, stage):
                F = L * TASKS + task
                per = 1 if is_diff(task) else 2
                k = TT * per
                shape = [P, k, P // per]
                o = normed(task).rearrange("p (k d) -> p k d", k=k)
                if stage == 1:
                    dve.wait_ge(pv_done, L * T_ALL + turn_units(task, TT - 1)[-1][0] + 1)
                    r0 = row_of(task, 0, 0)
                    V.reciprocal(fsmall[:, 3, 0:k], lsum[:, r0:r0 + 8:2 // per]).then_inc(fin_dve, 1)
                    dve.wait_ge(fin_dve, F * 8 + 1)
                    if task >= DIFF_TASKS + 2:
                        dve.wait_ge(o_turned, F - 1)
                    V.tensor_tensor(o, out_bank(task)[:, :].rearrange("p (k d) -> p k d", k=k),
                                    fsmall[:, 3, 0:k].unsqueeze(2).to_broadcast(shape), ALU.mult)\
                        .then_inc(fin_dve, 1)
                if stage == 2:
                    dve.wait_ge(fin_act, F * 3 + 1)
                    V.tensor_reduce(fsmall[:, 5, 0:k], work[W_OSQ].rearrange("p (k d) -> p k d", k=k),
                                    AX.X, ALU.add).then_inc(fin_dve, 1)
                    dve.wait_ge(fin_dve, F * 8 + 3)
                    V.tensor_scalar(fsmall[:, 0, 0:k], fsmall[:, 5, 0:k], per / P, EPS, ALU.mult,
                                    ALU.add).then_inc(fin_dve, 1)
                if stage == 3:
                    dve.wait_ge(fin_act, F * 3 + 3)
                    newton(fsmall[:, 4, 0:k], fsmall[:, 2, 0:k], fsmall[:, 0, 0:k], fsmall[:, 5, 0:k],
                           fin_dve, F * 8 + 4)
                    V.scalar_tensor_tensor(out=o, in0=o, scalar=-0.5,
                                           in1=fsmall[:, 4, 0:k].unsqueeze(2).to_broadcast(shape),
                                           op0=ALU.mult, op1=ALU.mult).then_inc(fin_dve, 1)
                if stage == 4:
                    dve.wait_ge(o_hi_done, F + 1)
                    kind = G_SUB if is_diff(task) else G_OUT
                    V.scalar_tensor_tensor(out=h_lo[:, task, :], in0=f_bank(task)[:, :],
                                           scalar=gcol[:, bass.ds(L + LAYERS * kind, 1)],
                                           in1=h_hi[:, task, :], op0=ALU.mult, op1=ALU.subtract)\
                        .then_inc(o_lo_done, 1)

            def update_x(L, which, gate, tiles=range(KD)):
                for m in tiles:
                    dve.wait_ge(acc_done, L * X_LAYER + which * KD + m + 2)
                    V.scalar_tensor_tensor(out=xT[:, m, :], in0=bank[m][:, :],
                                           scalar=mod[:, gate * KD + m:gate * KD + m + 1],
                                           in1=xT[:, m, :], op0=ALU.mult, op1=ALU.add)\
                        .then_inc(x_done, 1)
                    if which == 0 and m >= 2 and m % 2 == 0:
                        add_squares(L, m - 2)
                if which == 0:
                    add_squares(L, KD - 2)

            def add_squares(L, m):
                dve.wait_ge(sq_done, (L * 2 + 1) * KD + m + 2)
                pair = [work[W_TILE + (m + i) % SQUARES] for i in range(2)]
                V.tensor_tensor(pair[0], pair[0], pair[1], ALU.add).then_inc(pair_done, 1)

            with dve.Fori(0, LAYERS) as L:
                norm(L, 0)
                for g in range(GROUPS):
                    for s in range(2):
                        for t in range(TT):
                            j = slot_of(g, s, t)
                            if normed_tile(g, s, t):
                                nat_sums(L, *normed_tile(g, s, t))
                            for a in early_times(g, s, t):
                                for stage, lag in ((1, 7), (2, 8), (3, 9)):
                                    if has_end(a - lag):
                                        finish(L, (a - lag) // TT, stage)
                                if has(a - 2):
                                    combine(L, *step(a - 2))
                                if has(a - 1):
                                    score_rows(L, *step(a - 1))
                            if normed_tile(g, s, t):
                                nat(L, *normed_tile(g, s, t))
                            if t == 1 - s and g + s:
                                split_lo(L, g + s, 1 - s)
                            if j in ADA_AT:
                                for q, b in ADA_AT[j][1]:
                                    reduce_ada(L, ADA_AT[j][0], q, b)
                for k in range(T_DIFF, T_DIFF + 2):
                    score_rows(L, *step(k))
                for k in range(T_DIFF, STEPS):
                    task, n = step(k)
                    if n == 0 and task > DIFF_TASKS + 1:
                        finish(L, task - 2, 4)
                    if k + 2 < STEPS:
                        score_rows(L, *step(k + 2))
                    if task == DIFF_TASKS:
                        finish(L, n, 4)
                    elif n >= 1:
                        finish(L, task - 1, n)
                finish(L, TASKS - 2, 4)
                for stage in (1, 2, 3, 4):
                    finish(L, TASKS - 1, stage)

                for q in range(OUT_PAIRS):
                    split_lo(L, P_OUT + q, 1)
                    split_lo(L, P_OUT + q + 1, 0)
                update_x(L, 0, GT_A)
                norm(L, 1)

                for half, tiles in enumerate(FFN_SETS):
                    pairs = tiles // 2
                    with dve.Fori(0, pairs) as i:
                        X = L * UP_LAYER + (i * 4 + UP_BASE[half])
                        Y = L * FT + (i * 2 + FF_BASE[half])
                        for part in range(2):
                            for q in range(2):
                                b = 2 * part + q
                                col = i * 2 + (part * FT + FF_BASE[half] + q)
                                dve.wait_ge(tap2_done, X + b + 1)
                                for tap, lag, done in ((C_W1, 1, tap1_done), (C_W0, 2, conv_done)):
                                    V.scalar_tensor_tensor(
                                        out=work[b][:, lag:S], in0=bank[b][:, 0:S - lag],
                                        scalar=par[:, L, bass.ds(col + tap, 1)],
                                        in1=work[b][:, lag:S], op0=ALU.mult, op1=ALU.add)\
                                        .then_inc(done, 1)
                                    if tap == C_W1:
                                        dve.wait_ge(tap1_done, X + b + 1)
                            if part == 0:
                                split_lo(L, i + (P_UP[half] + 1), 0)
                        for q in range(2):
                            dve.wait_ge(silu_done, Y + q + 1)
                            dve.wait_ge(conv_done, X + 6 + q + 1)
                            V.tensor_tensor(work[2 + q], work[2 + q], work[4 + q],
                                            ALU.mult).then_inc(prod_done, 1)
                        split_lo(L, i + (P_UP[half] + 1), 1)
                        for q in range(2):
                            dve.wait_ge(act_hi_done, Y + q + 1)
                            V.tensor_tensor(act_lo[:, bass.ds(i * 2 + q, 1), :],
                                            work[2 + q].unsqueeze(1),
                                            act_hi[:, bass.ds(i * 2 + q, 1), :], ALU.subtract)\
                                .then_inc(act_lo_done, 1)
                    with dve.Fori(1, pairs) as i:
                        for s in range(2):
                            split_lo(L, i + P_DOWN[half], s, D)
                    update_x(L, 1 + half, GT_F, range(4))
                    if half == 0:
                        split_lo(L, P_UP[1], 0)
                    update_x(L, 1 + half, GT_F, range(4, KD))
                    if half == 0:
                        split_lo(L, P_UP[1], 1)

            for t in range(TT):
                dve.wait_ge(out_turned, 2 * t + 1)
                V.tensor_copy(xnat[:, t, 0:512], bank[2 * t][:, :]).then_inc(out_copied_dve, 1)


SD_STRIDED = 2 + 5
SD_PAR0 = SD_STRIDED + 1
SD_LAM = SD_PAR0 + LAYERS - 1 + 1 + LAYERS + 4
ROPE_TABLES = 1 + ROPE_HALF + 2 * (2 + 2 * 4) + 5 + 2 * 3 + 2
ANGLES = 1 + ROPE_HALF + 2 * (2 + 2 * 4) + 5
N_ROW_LOADS = 8
N_GAIN_LOADS = 4 * 3 + 7

_INS = ["x", "c", "positions", "g_mix", "g_ffn", "w_ada", "b_ada", "w_in", "w_out", "diff_q_g",
        "diff_k_g", "lam_q1", "lam_k1", "lam_q2", "lam_k2", "diff_subln_g", "dil_q_g", "dil_k_g",
        "dil_out_g", "w_up", "conv_w", "conv_b", "w_down"]


def kernel(**inputs):
    import concourse.bacc as bacc
    from concourse.bass_utils import run_bass_kernel_spmd

    nc = bacc.Bacc("TRN2", target_bir_lowering=False, num_devices=1)
    arrays, args = {}, []
    for name in _INS:
        a = np.ascontiguousarray(inputs[name])
        arrays[f"in_{name}"] = a
        args.append(nc.dram_tensor(f"in_{name}", a.shape, mybir.dt.from_np(a.dtype),
                                   kind="ExternalInput").ap())
    args.append(nc.dram_tensor("out_x", (1, S, D), F32, kind="ExternalOutput").ap())
    trunk_kernel(nc, *args)
    r = run_bass_kernel_spmd(nc, [arrays], core_ids=[0])
    return r.results[0]["out_x"]
```
